# Optimizing a Trainium2 kernel written in Bass

```python
import math
import jax, jax.numpy as jnp
from jax import lax
import numpy as np

D_MODEL = 1024
BATCH = 1
SEQ = 512
DEPTH = 2

HEAD_DIM = 64
ROPE_DIMS = HEAD_DIM // 4
ROPE_THETA = 500000.0
Q_BLOCK = 128
CONV_W = 3
CONV_WIDTH = 512
DIFF_HEADS = 4
DIFF_V_DIM = 2 * HEAD_DIM
NSA_HEADS = 8
NSA_GROUPS = 2
NSA_HPG = NSA_HEADS // NSA_GROUPS
CMP_BLOCK = 32
CMP_STRIDE = 16
SEL_BLOCK = 64
SEL_TOPK = 16
N_LOCAL_SEL = 2
WINDOW = 512
PHI_HIDDEN = 128
BRANCH_WIDTH = 512
N_BRANCHES = 3
D_FF = 2816
ALPHA = (2 * DEPTH) ** 0.25
BETA = (8 * DEPTH) ** -0.25
LN_EPS = 1e-5
NEG = -1e30
BIG = 1e30

COL_SIZES = (CONV_WIDTH, CONV_WIDTH, CONV_WIDTH,
             DIFF_HEADS * 2 * HEAD_DIM, DIFF_HEADS * 2 * HEAD_DIM, DIFF_HEADS * DIFF_V_DIM,
             NSA_HEADS * HEAD_DIM, 6 * NSA_GROUPS * HEAD_DIM, N_BRANCHES * NSA_HEADS,
             N_BRANCHES * D_MODEL)
D_IN = sum(COL_SIZES)
SPLIT_POINTS = tuple(int(c) for c in np.cumsum(COL_SIZES)[:-1])


def rope_tables(seq):
    pos = jnp.arange(seq, dtype=jnp.float32)
    inv_freq = ROPE_THETA ** (-jnp.arange(0, ROPE_DIMS, 2, dtype=jnp.float32) / ROPE_DIMS)
    ang = pos[:, None] * inv_freq[None, :]
    return jnp.cos(ang), jnp.sin(ang)

def partial_rope(t, cos, sin):
    half = ROPE_DIMS // 2
    c = cos[None, :, None, :].astype(t.dtype)
    s = sin[None, :, None, :].astype(t.dtype)
    t1, t2, rest = t[..., :half], t[..., half:ROPE_DIMS], t[..., ROPE_DIMS:]
    return jnp.concatenate([t1 * c - t2 * s, t1 * s + t2 * c, rest], axis=-1)

def causal_dwconv(x, w):
    c = x.shape[-1]
    return lax.conv_general_dilated(
        x, w[:, None, :].astype(x.dtype), window_strides=(1,),
        padding=[(w.shape[0] - 1, 0)], dimension_numbers=('NWC', 'WIO', 'NWC'),
        feature_group_count=c)

def layer_norm(x, g, b):
    xf = x.astype(jnp.float32)
    mu = jnp.mean(xf, axis=-1, keepdims=True)
    var = jnp.mean(jnp.square(xf - mu), axis=-1, keepdims=True)
    return ((xf - mu) * lax.rsqrt(var + LN_EPS) * g.astype(jnp.float32) + b.astype(jnp.float32)).astype(x.dtype)

def rms_norm(x, g):
    xf = x.astype(jnp.float32)
    ms = jnp.mean(jnp.square(xf), axis=-1, keepdims=True)
    return (xf * lax.rsqrt(ms + LN_EPS) * g.astype(jnp.float32)).astype(x.dtype)

def diff_attention(q, k, v, lam, lam_init, subln_g):
    b, s = q.shape[0], q.shape[1]
    nb = s // Q_BLOCK
    scale = HEAD_DIM ** -0.5
    qb = q.reshape(b, nb, Q_BLOCK, DIFF_HEADS, 2, HEAD_DIM).transpose(1, 0, 2, 3, 4, 5)
    kpos = jnp.arange(s)

    def one_block(args):
        i, q_i = args
        qpos = i * Q_BLOCK + jnp.arange(Q_BLOCK)
        sc = jnp.einsum('bqhmd,bkhmd->bhmqk', q_i, k).astype(jnp.float32) * scale
        sc = jnp.where(kpos[None, :] <= qpos[:, None], sc, -jnp.inf)
        p = jax.nn.softmax(sc, axis=-1)
        a = p[:, :, 0] - lam * p[:, :, 1]
        return jnp.einsum('bhqk,bkhd->bqhd', a.astype(v.dtype), v)

    o = lax.map(one_block, (jnp.arange(nb), qb))
    o = o.transpose(1, 0, 2, 3, 4).reshape(b, s, DIFF_HEADS, DIFF_V_DIM)
    o = rms_norm(o, subln_g) * (1.0 - lam_init)
    return o.reshape(b, s, DIFF_HEADS * DIFF_V_DIM)

def compress_kv(kv, pos_emb, w1, w2):
    b, s = kv.shape[0], kv.shape[1]
    n_cmp = (s - CMP_BLOCK) // CMP_STRIDE + 1
    idx = jnp.arange(n_cmp)[:, None] * CMP_STRIDE + jnp.arange(CMP_BLOCK)[None, :]
    blocks = kv[:, idx] + pos_emb[None, None, :, None, :]
    flat = blocks.transpose(0, 1, 3, 2, 4).reshape(b, n_cmp, NSA_GROUPS, CMP_BLOCK * HEAD_DIM)
    return jax.nn.gelu(flat @ w1, approximate=False) @ w2

def nsa_attention(q, kc, vc, ks, vs, kw, vw, gate_logits, cmp_pos, phi_w1, phi_w2):
    b, s = q.shape[0], q.shape[1]
    scale = HEAD_DIM ** -0.5
    qg = q.reshape(b, s, NSA_GROUPS, NSA_HPG, HEAD_DIM)
    tpos = jnp.arange(s)

    kc_c = compress_kv(kc, cmp_pos[0], phi_w1[0], phi_w2[0])
    vc_c = compress_kv(vc, cmp_pos[1], phi_w1[1], phi_w2[1])
    n_cmp = kc_c.shape[1]
    cstart = jnp.arange(n_cmp) * CMP_STRIDE
    cvalid = (cstart + CMP_BLOCK - 1)[None, :] <= tpos[:, None]
    sc = jnp.einsum('bsghd,bngd->bghsn', qg, kc_c).astype(jnp.float32) * scale
    p_cmp = jax.nn.softmax(jnp.where(cvalid, sc, NEG), axis=-1) * cvalid
    o_cmp = jnp.einsum('bghsn,bngd->bsghd', p_cmp.astype(vc_c.dtype), vc_c)

    n_sel = s // SEL_BLOCK
    sstart = jnp.arange(n_sel) * SEL_BLOCK
    overlap = jnp.maximum(
        jnp.minimum((cstart + CMP_BLOCK)[:, None], (sstart + SEL_BLOCK)[None, :])
        - jnp.maximum(cstart[:, None], sstart[None, :]), 0).astype(jnp.float32) / CMP_BLOCK
    imp = jnp.einsum('bghsn,nj->bgsj', p_cmp, overlap)
    cur = tpos // SEL_BLOCK
    j = jnp.arange(n_sel)
    forced = (j[None, :] == 0) | ((j[None, :] <= cur[:, None]) & (j[None, :] > cur[:, None] - N_LOCAL_SEL))
    future = j[None, :] > cur[:, None]
    imp = jnp.where(forced, BIG, jnp.where(future, NEG, imp))
    top_k = min(SEL_TOPK, n_sel)
    _, sel_idx = lax.top_k(imp, top_k)

    nb = s // Q_BLOCK
    qb = qg.reshape(b, nb, Q_BLOCK, NSA_GROUPS, NSA_HPG, HEAD_DIM).transpose(1, 0, 2, 3, 4, 5)
    idxb = sel_idx.reshape(b, NSA_GROUPS, nb, Q_BLOCK, top_k).transpose(2, 0, 1, 3, 4)
    ks_blk = ks.reshape(b, n_sel, SEL_BLOCK, NSA_GROUPS, HEAD_DIM).transpose(0, 3, 1, 2, 4)
    vs_blk = vs.reshape(b, n_sel, SEL_BLOCK, NSA_GROUPS, HEAD_DIM).transpose(0, 3, 1, 2, 4)
    gather = jax.vmap(jax.vmap(lambda blocks, ix: blocks[ix]))
    kw_p = jnp.pad(kw, ((0, 0), (WINDOW, 0), (0, 0), (0, 0)))
    vw_p = jnp.pad(vw, ((0, 0), (WINDOW, 0), (0, 0), (0, 0)))
    offs = jnp.arange(SEL_BLOCK)
    n_keys = top_k * SEL_BLOCK

    def one_block(args):
        i, q_i, ix = args
        qpos = i * Q_BLOCK + jnp.arange(Q_BLOCK)
        kg = gather(ks_blk, ix).reshape(b, NSA_GROUPS, Q_BLOCK, n_keys, HEAD_DIM)
        vg = gather(vs_blk, ix).reshape(b, NSA_GROUPS, Q_BLOCK, n_keys, HEAD_DIM)
        kpos = (ix[..., None] * SEL_BLOCK + offs).reshape(b, NSA_GROUPS, Q_BLOCK, n_keys)
        sc = jnp.einsum('bqghd,bgqnd->bghqn', q_i, kg).astype(jnp.float32) * scale
        sc = jnp.where((kpos <= qpos[None, None, :, None])[:, :, None], sc, -jnp.inf)
        o_sel = jnp.einsum('bghqn,bgqnd->bqghd', jax.nn.softmax(sc, axis=-1).astype(vg.dtype), vg)
        kwin = lax.dynamic_slice_in_dim(kw_p, i * Q_BLOCK, Q_BLOCK + WINDOW, axis=1)
        vwin = lax.dynamic_slice_in_dim(vw_p, i * Q_BLOCK, Q_BLOCK + WINDOW, axis=1)
        wpos = i * Q_BLOCK - WINDOW + jnp.arange(Q_BLOCK + WINDOW)
        wmask = ((wpos[None, :] <= qpos[:, None]) & (wpos[None, :] > qpos[:, None] - WINDOW)
                 & (wpos[None, :] >= 0))
        sc = jnp.einsum('bqghd,bkgd->bghqk', q_i, kwin).astype(jnp.float32) * scale
        sc = jnp.where(wmask, sc, -jnp.inf)
        o_win = jnp.einsum('bghqk,bkgd->bqghd', jax.nn.softmax(sc, axis=-1).astype(vwin.dtype), vwin)
        return o_sel, o_win

    o_sel, o_win = lax.map(one_block, (jnp.arange(nb), qb, idxb))
    o_sel = o_sel.transpose(1, 0, 2, 3, 4, 5).reshape(b, s, NSA_GROUPS, NSA_HPG, HEAD_DIM)
    o_win = o_win.transpose(1, 0, 2, 3, 4, 5).reshape(b, s, NSA_GROUPS, NSA_HPG, HEAD_DIM)
    g = jax.nn.sigmoid(gate_logits).reshape(b, s, NSA_GROUPS, NSA_HPG, N_BRANCHES)
    o = g[..., 0:1] * o_cmp + g[..., 1:2] * o_sel + g[..., 2:3] * o_win
    return o.reshape(b, s, NSA_HEADS * HEAD_DIM)

def token_mixing(x, w_in, conv_a_w, lam_vec, subln_g, cmp_pos, phi_w1, phi_w2, w_branch, w_o,
                 lam_init, cos, sin):
    b, s = x.shape[0], x.shape[1]
    z = x @ w_in
    a_b, a_c, a_v, d_q, d_k, d_v, n_q, n_kv, n_g, m_g = jnp.split(z, SPLIT_POINTS, axis=-1)
    y_a = a_b * causal_dwconv(a_c * a_v, conv_a_w)
    dq = partial_rope(d_q.reshape(b, s, DIFF_HEADS * 2, HEAD_DIM), cos, sin).reshape(b, s, DIFF_HEADS, 2, HEAD_DIM)
    dk = partial_rope(d_k.reshape(b, s, DIFF_HEADS * 2, HEAD_DIM), cos, sin).reshape(b, s, DIFF_HEADS, 2, HEAD_DIM)
    dv = d_v.reshape(b, s, DIFF_HEADS, DIFF_V_DIM)
    lf = lam_vec.astype(jnp.float32)
    lam = jnp.exp(jnp.dot(lf[0], lf[1])) - jnp.exp(jnp.dot(lf[2], lf[3])) + lam_init
    y_b = diff_attention(dq, dk, dv, lam, lam_init, subln_g)
    nq = partial_rope(n_q.reshape(b, s, NSA_HEADS, HEAD_DIM), cos, sin)
    kv6 = n_kv.reshape(b, s, 6, NSA_GROUPS, HEAD_DIM)
    kc = partial_rope(kv6[:, :, 0], cos, sin)
    ks = partial_rope(kv6[:, :, 2], cos, sin)
    kw = partial_rope(kv6[:, :, 4], cos, sin)
    y_c = nsa_attention(nq, kc, kv6[:, :, 1], ks, kv6[:, :, 3], kw, kv6[:, :, 5], n_g,
                        cmp_pos, phi_w1, phi_w2)
    gates = jax.nn.sigmoid(m_g).reshape(b, s, N_BRANCHES, D_MODEL)
    merged = (gates[:, :, 0] * (y_a @ w_branch[0])
              + gates[:, :, 1] * (y_b @ w_branch[1])
              + gates[:, :, 2] * (y_c @ w_branch[2]))
    return merged @ w_o

def conv_ffn(x, w_up, conv_w, conv_b, w_down):
    h = causal_dwconv(x @ w_up, conv_w) + conv_b
    a, u = jnp.split(h, 2, axis=-1)
    return (jax.nn.gelu(a, approximate=False) * u) @ w_down

def first_inputs(seed: int = 0) -> dict:
    key = jax.random.key(seed)
    k = jax.random.split(key, 20)

    def nrm(kk, shape, scale):
        return jax.random.normal(kk, shape, jnp.float32) * scale

    return {
        'x': nrm(k[0], (BATCH, SEQ, D_MODEL), 1.0),
        'w_in': nrm(k[1], (DEPTH, D_MODEL, D_IN), D_MODEL ** -0.5),
        'conv_a_w': nrm(k[2], (DEPTH, CONV_W, CONV_WIDTH), CONV_W ** -0.5),
        'diff_lambda': nrm(k[3], (DEPTH, 4, HEAD_DIM), 0.1),
        'diff_subln': 1.0 + nrm(k[4], (DEPTH, DIFF_V_DIM), 0.02),
        'nsa_cmp_pos': nrm(k[5], (DEPTH, 2, CMP_BLOCK, HEAD_DIM), 0.1),
        'nsa_phi_w1': nrm(k[6], (DEPTH, 2, CMP_BLOCK * HEAD_DIM, PHI_HIDDEN), (CMP_BLOCK * HEAD_DIM) ** -0.5),
        'nsa_phi_w2': nrm(k[7], (DEPTH, 2, PHI_HIDDEN, HEAD_DIM), PHI_HIDDEN ** -0.5),
        'w_branch': nrm(k[8], (DEPTH, N_BRANCHES, BRANCH_WIDTH, D_MODEL), BRANCH_WIDTH ** -0.5),
        'w_o': nrm(k[9], (DEPTH, D_MODEL, D_MODEL), BETA * D_MODEL ** -0.5),
        'ln1_g': 1.0 + nrm(k[10], (DEPTH, D_MODEL), 0.02),
        'ln1_b': nrm(k[11], (DEPTH, D_MODEL), 0.02),
        'ffn_w_up': nrm(k[12], (DEPTH, D_MODEL, 2 * D_FF), D_MODEL ** -0.5),
        'ffn_conv_w': nrm(k[13], (DEPTH, CONV_W, 2 * D_FF), CONV_W ** -0.5),
        'ffn_conv_b': nrm(k[14], (DEPTH, 2 * D_FF), 0.02),
        'ffn_w_down': nrm(k[15], (DEPTH, D_FF, D_MODEL), BETA * D_FF ** -0.5),
        'ln2_g': 1.0 + nrm(k[16], (DEPTH, D_MODEL), 0.02),
        'ln2_b': nrm(k[17], (DEPTH, D_MODEL), 0.02),
    }

def first_block(x, w_in, conv_a_w, diff_lambda, diff_subln, nsa_cmp_pos, nsa_phi_w1, nsa_phi_w2,
              w_branch, w_o, ln1_g, ln1_b, ffn_w_up, ffn_conv_w, ffn_conv_b, ffn_w_down,
              ln2_g, ln2_b):
    cos, sin = rope_tables(x.shape[1])
    for l in range(DEPTH):
        lam_init = 0.8 - 0.6 * math.exp(-0.3 * l)
        mix = token_mixing(x, w_in[l], conv_a_w[l], diff_lambda[l], diff_subln[l], nsa_cmp_pos[l],
                           nsa_phi_w1[l], nsa_phi_w2[l], w_branch[l], w_o[l], lam_init, cos, sin)
        x = layer_norm(ALPHA * x + mix, ln1_g[l], ln1_b[l])
        ffn = conv_ffn(x, ffn_w_up[l], ffn_conv_w[l], ffn_conv_b[l], ffn_w_down[l])
        x = layer_norm(ALPHA * x + ffn, ln2_g[l], ln2_b[l])
    return x


N_MIXERS = 2
N_A_LAYERS = (DEPTH + 1) // 2
N_B_LAYERS = DEPTH // 2
RMS_EPS = 1e-6
LRU_WIDTH = D_MODEL
LRU_HEADS = 4
LRU_BLOCK = LRU_WIDTH // LRU_HEADS
CONV_WIDTH_2 = 4
LRU_C = 8.0
RWKV_HEAD = 64
RWKV_HEADS = D_MODEL // RWKV_HEAD
DECAY_LORA = 64
AAA_LORA = 64
GATE_LORA = 128
RWKV_GN_EPS = 64e-5
MEM_LEN = 256
MEM_HEADS = 4
MEM_HEAD_DIM = D_MODEL // MEM_HEADS
D_FF_2 = 4 * D_MODEL


def rms_norm_2(x, g):
    xf = x.astype(jnp.float32)
    y = xf * lax.rsqrt(jnp.mean(xf * xf, axis=-1, keepdims=True) + RMS_EPS)
    return (y * g.astype(jnp.float32)).astype(x.dtype)

def _lru_combine(c1, c2):
    a1, b1 = c1
    a2, b2 = c2
    return a1 * a2, a2 * b1 + b2

def rglru_mixer(x, conv_w, conv_b, w_in, b_in, gate_w, gate_b, lam, w_out, b_out):
    B, S, _ = x.shape
    proj = x @ w_in + b_in
    y_branch, u = jnp.split(proj, 2, axis=-1)
    y_branch = jax.nn.gelu(y_branch, approximate=True)
    u_pad = jnp.pad(u, ((0, 0), (CONV_WIDTH_2 - 1, 0), (0, 0)))
    conv = conv_b + u_pad[:, 0:S] * conv_w[0]
    for tap in range(1, CONV_WIDTH_2):
        conv = conv + u_pad[:, tap:tap + S] * conv_w[tap]
    ub = conv.reshape(B, S, LRU_HEADS, LRU_BLOCK)
    gates = jax.nn.sigmoid(jnp.einsum('bshi,ghij->gbshj', ub, gate_w) + gate_b[:, None, None])
    r_gate = gates[0].reshape(B, S, LRU_WIDTH).astype(jnp.float32)
    i_gate = gates[1].reshape(B, S, LRU_WIDTH).astype(jnp.float32)
    log_a = -LRU_C * r_gate * jax.nn.softplus(-lam.astype(jnp.float32))
    a = jnp.exp(log_a)
    mult = jnp.sqrt(-jnp.expm1(2.0 * log_a))
    b = mult * i_gate * conv.astype(jnp.float32)
    _, h = lax.associative_scan(_lru_combine, (a, b), axis=1)
    return (h.astype(x.dtype) * y_branch) @ w_out + b_out

def rwkv7_mixer(x, mu, w_rkv, w0, w1, w2, a0, a1, a2, g1, g2, k_k, k_a, r_k, gn_g, gn_b, w_o):
    B, S, D = x.shape
    H, N = RWKV_HEADS, RWKV_HEAD
    x_prev = jnp.pad(x, ((0, 0), (1, 0), (0, 0)))[:, :S]
    xx = x_prev - x
    r = (x + xx * mu[0]) @ w_rkv[0]
    xw = x + xx * mu[1]
    k = (x + xx * mu[2]) @ w_rkv[1]
    v = (x + xx * mu[3]) @ w_rkv[2]
    xa = x + xx * mu[4]
    xg = x + xx * mu[5]
    w_log = -jax.nn.softplus(-(w0 + jnp.tanh(xw @ w1) @ w2).astype(jnp.float32)) - 0.5
    decay = jnp.exp(-jnp.exp(w_log))
    a = jax.nn.sigmoid(a0 + (xa @ a1) @ a2)
    g = jax.nn.sigmoid(xg @ g1) @ g2
    kk = (k * k_k).reshape(B, S, H, N).astype(jnp.float32)
    kk = kk / jnp.maximum(jnp.linalg.norm(kk, axis=-1, keepdims=True), 1e-12)
    k = k * (1.0 + (a - 1.0) * k_a)

    rh = r.reshape(B, S, H, N).astype(jnp.float32)
    kh = k.reshape(B, S, H, N).astype(jnp.float32)
    vh = v.reshape(B, S, H, N).astype(jnp.float32)
    wh = decay.reshape(B, S, H, N)
    ah = a.reshape(B, S, H, N).astype(jnp.float32)
    rem_a = -kk
    rem_b = kk * ah

    def step(state, inp):
        r_t, w_t, k_t, v_t, a_t, b_t = inp
        sa = jnp.einsum('bhij,bhj->bhi', state, a_t)
        state = (state * w_t[:, :, None, :] + sa[..., None] * b_t[:, :, None, :]
                 + v_t[..., None] * k_t[:, :, None, :])
        y_t = jnp.einsum('bhij,bhj->bhi', state, r_t)
        return state, y_t

    seq_inputs = tuple(jnp.moveaxis(t, 1, 0) for t in (rh, wh, kh, vh, rem_a, rem_b))
    state0 = jnp.zeros((B, H, N, N), jnp.float32)
    _, ys = lax.scan(step, state0, seq_inputs)
    y = jnp.moveaxis(ys, 0, 1)
    mean = jnp.mean(y, axis=-1, keepdims=True)
    var = jnp.mean(jnp.square(y - mean), axis=-1, keepdims=True)
    yn = ((y - mean) * lax.rsqrt(var + RWKV_GN_EPS)).reshape(B, S, D)
    yn = yn * gn_g.astype(jnp.float32) + gn_b.astype(jnp.float32)
    bonus = jnp.sum(rh * kh * r_k.astype(jnp.float32), axis=-1, keepdims=True) * vh
    out = (yn + bonus.reshape(B, S, D)).astype(x.dtype)
    return (out * g) @ w_o

def mem_cross_attention(h, mem_n, w_q, w_kv, w_o):
    B, S, D = h.shape
    M = mem_n.shape[1]
    q = (h @ w_q).reshape(B, S, MEM_HEADS, MEM_HEAD_DIM)
    kv = (mem_n @ w_kv).reshape(B, M, 2, MEM_HEADS, MEM_HEAD_DIM)
    k, v = kv[:, :, 0], kv[:, :, 1]
    s = jnp.einsum('bqhd,bkhd->bhqk', q, k).astype(jnp.float32) * (MEM_HEAD_DIM ** -0.5)
    p = jax.nn.softmax(s, axis=-1).astype(h.dtype)
    o = jnp.einsum('bhqk,bkhd->bqhd', p, v).reshape(B, S, D)
    return o @ w_o

def sqrelu_mlp(h, w_up, w_down):
    return jnp.square(jax.nn.relu(h @ w_up)) @ w_down

def second_inputs(seed: int = 0) -> dict:
    key = jax.random.key(seed)
    ks = iter(jax.random.split(key, 48))
    f32 = jnp.float32

    def nrm(shape, scale):
        return jax.random.normal(next(ks), shape, f32) * scale

    def unif(shape, lo, hi):
        return jax.random.uniform(next(ks), shape, f32, lo, hi)

    D, NA, NB = D_MODEL, N_A_LAYERS, N_B_LAYERS
    x = nrm((BATCH, SEQ, D), 1.0)
    mem = nrm((BATCH, MEM_LEN, D), 1.0)
    ln_gains = 1.0 + nrm((DEPTH, 6, D), 0.05)
    mem_norm = 1.0 + nrm((D,), 0.05)
    a_conv_w = nrm((NA, CONV_WIDTH_2, LRU_WIDTH), CONV_WIDTH_2 ** -0.5)
    a_conv_b = nrm((NA, LRU_WIDTH), 0.01)
    a_w_in = nrm((NA, D, 2 * LRU_WIDTH), D ** -0.5)
    a_b_in = nrm((NA, 2 * LRU_WIDTH), 0.01)
    a_gate_w = nrm((NA, 2, LRU_HEADS, LRU_BLOCK, LRU_BLOCK), LRU_BLOCK ** -0.5)
    a_gate_b = nrm((NA, 2, LRU_HEADS, LRU_BLOCK), 0.01)
    u = unif((NA, LRU_WIDTH), 0.81, 0.998)
    sp = -0.5 * jnp.log(u)
    a_lambda = -jnp.log(jnp.expm1(sp))
    a_w_out = nrm((NA, LRU_WIDTH, D), LRU_WIDTH ** -0.5)
    a_b_out = nrm((NA, D), 0.01)
    b_mu = unif((NB, 6, D), 0.0, 1.0)
    b_w_rkv = nrm((NB, 3, D, D), D ** -0.5)
    b_w0 = unif((NB, D), -6.0, -1.0)
    b_w1 = nrm((NB, D, DECAY_LORA), D ** -0.5)
    b_w2 = nrm((NB, DECAY_LORA, D), 0.1 * DECAY_LORA ** -0.5)
    b_a0 = nrm((NB, D), 0.1)
    b_a1 = nrm((NB, D, AAA_LORA), D ** -0.5)
    b_a2 = nrm((NB, AAA_LORA, D), 0.1 * AAA_LORA ** -0.5)
    b_g1 = nrm((NB, D, GATE_LORA), D ** -0.5)
    b_g2 = nrm((NB, GATE_LORA, D), GATE_LORA ** -0.5)
    b_k_k = 0.85 + nrm((NB, D), 0.05)
    b_k_a = 1.0 + nrm((NB, D), 0.05)
    b_r_k = nrm((NB, RWKV_HEADS, RWKV_HEAD), 0.1)
    b_gn_g = 1.0 + nrm((NB, D), 0.05)
    b_gn_b = nrm((NB, D), 0.01)
    b_w_o = nrm((NB, D, D), D ** -0.5)
    c_w_q = nrm((DEPTH, D, D), D ** -0.5)
    c_w_kv = nrm((DEPTH, D, 2 * D), D ** -0.5)
    c_w_o = nrm((DEPTH, D, D), D ** -0.5)
    m_w_up = nrm((DEPTH, D, D_FF_2), D ** -0.5)
    m_w_down = nrm((DEPTH, D_FF_2, D), D_FF_2 ** -0.5)
    return {"x": x, "mem": mem, "ln_gains": ln_gains, "mem_norm": mem_norm,
            "a_conv_w": a_conv_w, "a_conv_b": a_conv_b, "a_w_in": a_w_in, "a_b_in": a_b_in,
            "a_gate_w": a_gate_w, "a_gate_b": a_gate_b, "a_lambda": a_lambda,
            "a_w_out": a_w_out, "a_b_out": a_b_out,
            "b_mu": b_mu, "b_w_rkv": b_w_rkv, "b_w0": b_w0, "b_w1": b_w1, "b_w2": b_w2,
            "b_a0": b_a0, "b_a1": b_a1, "b_a2": b_a2, "b_g1": b_g1, "b_g2": b_g2,
            "b_k_k": b_k_k, "b_k_a": b_k_a, "b_r_k": b_r_k, "b_gn_g": b_gn_g, "b_gn_b": b_gn_b,
            "b_w_o": b_w_o,
            "c_w_q": c_w_q, "c_w_kv": c_w_kv, "c_w_o": c_w_o,
            "m_w_up": m_w_up, "m_w_down": m_w_down}

def second_block(x, mem, ln_gains, mem_norm,
              a_conv_w, a_conv_b, a_w_in, a_b_in, a_gate_w, a_gate_b, a_lambda, a_w_out, a_b_out,
              b_mu, b_w_rkv, b_w0, b_w1, b_w2, b_a0, b_a1, b_a2, b_g1, b_g2,
              b_k_k, b_k_a, b_r_k, b_gn_g, b_gn_b, b_w_o,
              c_w_q, c_w_kv, c_w_o, m_w_up, m_w_down):
    mem_n = rms_norm_2(mem, mem_norm)
    for i in range(DEPTH):
        g = ln_gains[i]
        j = i // N_MIXERS
        hn = rms_norm_2(x, g[0])
        if i % N_MIXERS == 0:
            t = rglru_mixer(hn, a_conv_w[j], a_conv_b[j], a_w_in[j], a_b_in[j], a_gate_w[j],
                            a_gate_b[j], a_lambda[j], a_w_out[j], a_b_out[j])
        else:
            t = rwkv7_mixer(hn, b_mu[j], b_w_rkv[j], b_w0[j], b_w1[j], b_w2[j], b_a0[j],
                            b_a1[j], b_a2[j], b_g1[j], b_g2[j], b_k_k[j], b_k_a[j], b_r_k[j],
                            b_gn_g[j], b_gn_b[j], b_w_o[j])
        x = x + rms_norm_2(t, g[1])
        c = mem_cross_attention(rms_norm_2(x, g[2]), mem_n, c_w_q[i], c_w_kv[i], c_w_o[i])
        x = x + rms_norm_2(c, g[3])
        m = sqrelu_mlp(rms_norm_2(x, g[4]), m_w_up[i], m_w_down[i])
        x = x + rms_norm_2(m, g[5])
    return x


def setup_inputs(seed=0):
    out = dict(first_inputs(seed))
    for name, value in second_inputs(seed + 1).items():
        if name != "x":
            out[name + "_2"] = value
    return out


def reference(
    x, w_in, conv_a_w, diff_lambda, diff_subln, nsa_cmp_pos, nsa_phi_w1, nsa_phi_w2, w_branch,
    w_o, ln1_g, ln1_b, ffn_w_up, ffn_conv_w, ffn_conv_b, ffn_w_down, ln2_g, ln2_b, mem_2,
    ln_gains_2, mem_norm_2, a_conv_w_2, a_conv_b_2, a_w_in_2, a_b_in_2, a_gate_w_2, a_gate_b_2,
    a_lambda_2, a_w_out_2, a_b_out_2, b_mu_2, b_w_rkv_2, b_w0_2, b_w1_2, b_w2_2, b_a0_2, b_a1_2,
    b_a2_2, b_g1_2, b_g2_2, b_k_k_2, b_k_a_2, b_r_k_2, b_gn_g_2, b_gn_b_2, b_w_o_2, c_w_q_2,
    c_w_kv_2, c_w_o_2, m_w_up_2, m_w_down_2,
):
    x = first_block(
        x, w_in, conv_a_w, diff_lambda, diff_subln, nsa_cmp_pos, nsa_phi_w1, nsa_phi_w2,
        w_branch, w_o, ln1_g, ln1_b, ffn_w_up, ffn_conv_w, ffn_conv_b, ffn_w_down, ln2_g, ln2_b,
    )
    return second_block(
        x, mem_2, ln_gains_2, mem_norm_2, a_conv_w_2, a_conv_b_2, a_w_in_2, a_b_in_2,
        a_gate_w_2, a_gate_b_2, a_lambda_2, a_w_out_2, a_b_out_2, b_mu_2, b_w_rkv_2, b_w0_2,
        b_w1_2, b_w2_2, b_a0_2, b_a1_2, b_a2_2, b_g1_2, b_g2_2, b_k_k_2, b_k_a_2, b_r_k_2,
        b_gn_g_2, b_gn_b_2, b_w_o_2, c_w_q_2, c_w_kv_2, c_w_o_2, m_w_up_2, m_w_down_2,
    )


_drawn_inputs = setup_inputs


def setup_inputs(seed=0):
    import zlib

    import numpy as np

    out = dict(_drawn_inputs(seed))
    spreads = {}
    factors = {'diff_lambda': 2.957,
     'diff_subln': 6.569,
     'ffn_conv_b': 3.234,
     'a_gate_b_2': 8.0,
     'b_w1_2': 8.0,
     'b_w2_2': 8.0,
     'b_a0_2': 3.055,
     'b_a1_2': 3.023,
     'b_a2_2': 3.154,
     'b_gn_b_2': 8.0,
     'nsa_cmp_pos': 4.416,
     'a_conv_b_2': 3.256,
     'a_b_out_2': 3.48}
    for name, (base, spread) in spreads.items():
        noise = np.random.default_rng([zlib.crc32(name.encode()), seed]).standard_normal(out[name].shape)
        drawn = base * np.exp(spread * noise) if base else spread * noise
        out[name] = __import__('jax').numpy.asarray(drawn.astype(out[name].dtype))
    for name, factor in factors.items():
        out[name] = (out[name] * factor).astype(out[name].dtype)
    return out
```

```python
import concourse.bass as bass
from concourse import mybir
from concourse.alu_op_type import AluOpType as ALU
from contextlib import ExitStack
import math
import numpy as np

F32 = mybir.dt.float32
ACT = mybir.ActivationFunctionType
AXX = mybir.AxisListType.X

P = 128
S = 512
D = 1024
KT = D // P
ST = S // P
DEPTH = 2
HD = 64
DH = 4
NH = 8
NG = 2
HPG = NH // NG
CMP_BLOCK, CMP_STRIDE = 32, 16
NCMP = (S - CMP_BLOCK) // CMP_STRIDE + 1
DFF = 2816
FT = DFF // P
ALPHA = (2 * DEPTH) ** 0.25
LN_EPS = 1e-5
NEG = -1e30
SCALE = HD ** -0.5

RING = 4
CHUNK = 8 * P
C_Z, C_DV, C_VSG, C_PHI, C_MERGE, C_WO, C_UP, C_DOWN = 28, 4, 4, 8, 36, 8, 2 * FT, 24
B_Z = 0
B_DV = B_Z + C_Z
B_VSG = B_DV + C_DV
B_PHI = B_VSG + C_VSG
B_MERGE = B_PHI + C_PHI
B_WO = B_MERGE + C_MERGE
B_UP = B_WO + C_WO
B_DOWN = B_UP + C_UP
CPL = B_DOWN + C_DOWN

Z_AB, Z_AC, Z_AV, Z_DQ, Z_DK, Z_NQ, Z_KC, Z_VC, Z_KS, Z_KW = 0, 4, 8, 12, 16, 20, 24, 25, 26, 27
ROPE_TILES = list(range(Z_DQ, Z_KC + 1)) + [Z_KS, Z_KW]
NR = len(ROPE_TILES)
VSG_N = 2 * P + 3 * NH

PCOL = {}
_at = 0
for _name, _n in (("conv_a", 12), ("subln", 1), ("ln1_g", 8), ("ln1_b", 8), ("ln2_g", 8), ("ln2_b", 8),
                  ("up_w", 2 * FT * 3), ("up_b", 2 * FT), ("pos", 2 * CMP_BLOCK), ("phi_w2k", P), ("phi_w2v", HD),
                  ("lam", 4 * HD), ("lam_init", 1), ("lam_keep", 1)):
    PCOL[_name] = (_at, _n)
    _at += _n
NPAR = _at

CCOL = {}
_at = 0
for _name, _n in (("ident", P), ("rot", P), ("maskneg", P), ("mean", P), ("cmask", ST * NCMP),
                  ("cvalid", ST * NCMP), ("cos", S), ("sin", S), ("eps", 1)):
    CCOL[_name] = (_at, _n)
    _at += _n
NCST = _at

S2 = 256
MH, MT = 4, 2
F2T = 4 * KT
RMS_EPS, GN_EPS = 1e-6, 64e-5
LRU_C = 8.0
K0 = math.exp(-0.5)
RC = S // P
LEVELS = 6
C_LRU_IN, C_LRU_GATE, C_LRU_OUT = 16, 4, 8
C_RKV, C_LORA, C_G2, C_RWO = 24, 4, 4, 8
C_MQ, C_MK, C_MV, C_MO = 8, 8, 8, 8
C_MUP, C_MDN = F2T, 4 * KT
C_TAIL = C_MQ + C_MK + C_MV + C_MO + C_MUP + C_MDN
B_LRU = DEPTH * CPL
B_TAIL0 = B_LRU + C_LRU_IN + C_LRU_GATE + C_LRU_OUT
B_RWKV = B_TAIL0 + C_TAIL
B_TAIL1 = B_RWKV + C_RKV + C_LORA + C_G2 + C_RWO
N_CHUNKS = B_TAIL1 + C_TAIL

P2COL = {}
_at = 0
for _name, _n in (("ln", 2 * 6 * KT), ("mem_norm", KT), ("conv_w", 4 * KT), ("conv_b", KT), ("b_in", 2 * KT),
                  ("gate_b", 2 * KT), ("lam", KT), ("b_out", KT), ("mu", 6 * KT), ("w0", KT), ("a0", KT), ("k_k", KT),
                  ("k_a", KT), ("r_k", KT), ("gn_g", KT), ("gn_b", KT), ("rms_eps", 1), ("gn_eps", 1)):
    P2COL[_name] = (_at, _n)
    _at += _n
NPAR2 = _at

C2COL = {}
_at = 0
for _name, _n in (("pair", 2 * P), ("levels", (LEVELS + 1) * P), ("reset", S), ("ones", P)):
    C2COL[_name] = (_at, _n)
    _at += _n
NCST2 = _at

UNITS = [("diff", qi, hp) for qi in range(ST) for hp in range(DH // 2)] + \
        [(b, qi, g) for b in (0, 1) for qi in range(ST) for g in range(NG)]
NU = len(UNITS)
HEADS_OF = [2 if kind == "diff" else 4 for kind, _, _ in UNITS]
HEADS_BEFORE = [sum(HEADS_OF[:u]) for u in range(NU + 1)]
NHEADS = HEADS_BEFORE[NU]


def build(nc, a, out, stop=None):
    ctx = ExitStack()
    with ctx:
        def sb(name, shape, dt=F32):
            return ctx.enter_context(nc.sbuf_tensor(name, shape, dt))

        def sem(name):
            return ctx.enter_context(nc.semaphore(name))

        ps = ctx.enter_context(nc.psum_tensor("ps", [P, 8, 512], F32))
        X = sb("X", [P, KT, S])
        N = sb("N", [P, KT, S])
        Z = sb("Z", [P, 28, S])
        Y = sb("Y", [P, 12, S])
        T = sb("T", [P, 8, S])
        ring = sb("ring", [P, RING, CHUNK])
        PT = sb("PT", [P, 4, S])
        YB = sb("YB", [P, ST, DH, P])
        YC = sb("YC", [P, ST, NH, HD])
        DV = sb("DV", [P, ST, DH * P])
        VSG = sb("VSG", [P, ST, VSG_N])
        GSIG = sb("GSIG", [P, ST, 3, NH])
        RS = sb("RS", [P, S])
        CST = sb("CST", [P, NCST])
        PAR = sb("PAR", [P, NPAR])
        H = sb("H", [P, 2, NG, 32])
        KCC = sb("KCC", [P, 32])
        VCC = sb("VCC", [32, NG, HD])
        CS = sb("CS", [P, ST, NH, NCMP])
        CM = sb("CM", [P, 4, ST * NH])
        AM = sb("AM", [P, 2, 4, 4])
        LAM = sb("LAM", [P, 2 * HD + 8])
        MS = sb("MS", [P, 2, ST * DH])
        LE = sb("LE", [P, 2, 2, 2, P + 2])

        def cst(name):
            c, n = CCOL[name]
            return CST[:, c:c + n]

        def par(name, i=0, n=None):
            c, m = PCOL[name]
            return PAR[:, c + i:c + (m if n is None else i + n)]

        landed = [sem(f"landed{j}") for j in range(RING)]
        used = sem("used")
        x_in = sem("x_in")
        cst_in = sem("cst_in")
        par_in = sem("par_in")
        x_ready = sem("x_ready")
        out_done = sem("out_done")
        zc = sem("zc")
        tokc = sem("tokc")
        gsig = sem("gsig")
        rot = sem("rot")
        rope = sem("rope")
        cmpin = sem("cmpin")
        phih = sem("phih")
        phio = sem("phio")
        cmpkv = sem("cmpkv")
        cs_mm = sem("cs_mm")
        cs_sub = sem("cs_sub")
        cs_exp = sem("cs_exp")
        cs_p = sem("cs_p")
        cs_tr = sem("cs_tr")
        cs_pt = sem("cs_pt")
        cs_av = sem("cs_av")
        cs_out = sem("cs_out")
        conv_p = sem("conv_p")
        conv_out = sem("conv_out")
        lam_d = sem("lam_d")
        lam_e = sem("lam_e")
        at_sc = sem("at_sc")
        at_max = sem("at_max")
        at_exp = sem("at_exp")
        at_comb = sem("at_comb")
        at_tr = sem("at_tr")
        at_pt = sem("at_pt")
        at_av = sem("at_av")
        at_out = sem("at_out")
        yb_sq = sem("yb_sq")
        yb_ms = sem("yb_ms")
        yb_rt = sem("yb_rt")
        yb_fin = sem("yb_fin")
        ytr = sem("ytr")
        yfin = sem("yfin")
        nfree = sem("nfree")
        nzero = sem("nzero")
        sg = sem("sg")
        mg = sem("mg")
        x1pre = sem("x1pre")
        x2pre = sem("x2pre")
        x1 = sem("x1")
        up_a = sem("up_a")
        up_c = sem("up_c")
        up_g = sem("up_g")
        up_h = sem("up_h")
        ln = {k: sem(f"ln_{k}") for k in ("mean", "xc", "sq", "var", "std", "y")}

        PAR2 = sb("PAR2", [P, NPAR2])
        LRU = sb("LRU", [P, 4, KT])
        MID = sb("MID", [P, 3, KT, RC])
        MN = YB[:].rearrange("p t h d -> p (t h d)").rearrange("p (k s) -> p k s", k=KT)
        CST2 = DV[:].rearrange("p t n -> p (t n)")
        MK = Z[:, 8:12, :].rearrange("p k s -> p (k s)").rearrange("p (k s) -> p k s", k=KT)
        MV = Z[:, 12:16, :].rearrange("p k s -> p (k s)").rearrange("p (k n) -> p k n", k=2)
        MP = T[:, 0:4, :].rearrange("p k s -> p (k s)").rearrange("p (u h s) -> p u h s", u=2, h=MH)
        HID = [Z[:, f, :] for f in range(28)] + [Y[:, f, :] for f in range(F2T - 28)]
        YCF = YC[:].rearrange("p t h d -> p t (h d)")
        VSGF = VSG[:].rearrange("p t n -> p (t n)")
        CSF = CS[:].rearrange("p t h n -> p (t h n)")
        cos0 = CCOL["cos"][0]
        MIX = [[T[:, n, :] for n in range(KT)], [PT[:, n, :] for n in range(4)] + [YCF[:, n, :] for n in range(4)]]
        TW, TA_, TG = Y[0:HD, 8, :], Y[0:HD, 9, :], Y[:, 10, :]
        LANES = []
        for L in range(2):
            wide = Z[:, 24:28, :].rearrange("p k s -> p (k s)") if L == 0 else PT[:].rearrange("p k s -> p (k s)")
            single = [Y[:, 8, :], Y[:, 9, :], YCF[:, 0, :], YCF[:, 1, :], VSGF[:, 0:S], CST[:, cos0:cos0 + S]] if L == 0 else \
                     [YCF[:, 2, :], YCF[:, 3, :], VSGF[:, S:2 * S], Y[:, 11, :], CST[:, cos0 + S:cos0 + 2 * S], RS[:]]
            LANES.append(dict(
                ar=single[0].rearrange("p (n a t) -> p n a t", n=2, a=2),
                bk=single[1].rearrange("p (a n t) -> p a n t", a=2, n=2),
                pu=single[1].rearrange("p (a q i) -> p a q i", a=2, q=4),
                e=LE[:, L], z=single[2].rearrange("p (q t) -> p q t", q=4),
                g1=wide[:, 0:1024].rearrange("p (q a t) -> p q a t", q=4, a=2),
                g2=wide[:, 1024:2048].rearrange("p (q a t) -> p q a t", q=4, a=2),
                x=single[3].rearrange("p (q t) -> p q t", q=4), xt=single[4].rearrange("p (q t) -> p q t", q=4),
                bktok=single[5].rearrange("p (a n c) -> p a n c", a=2, n=2),
                vtok=CSF[:, L * 256:L * 256 + 256].rearrange("p (n c) -> p n c", n=2),
                sh=CSF[:, 512 + L * P:512 + L * P + P].rearrange("p (n i) -> p n i", n=2)))
        STATE = PAR[:, 0:KT * HD].rearrange("p (n i) -> p n i", n=KT)

        def par2(name, i=0, n=None):
            c, m = P2COL[name]
            return PAR2[:, c + i:c + (m if n is None else i + n)]

        def cst2(name, i=0, n=None):
            c, m = C2COL[name]
            return CST2[:, c + i:c + (m if n is None else i + n)]

        par2_in = sem("par2_in")
        cst2_in = sem("cst2_in")
        mem_in = sem("mem_in")
        xr2 = sem("xr2")
        t_ready = sem("t_ready")
        rms_sq, rms_var, rms_std, rms_y = [sem(f"rms_{k}") for k in ("sq", "var", "std", "y")]
        NORMED = {i: KT * (at + 1) for at, i in enumerate((0, 1, 3, 5, 7, 9, 11))}
        lru_in = sem("lru_in")
        lru_conv = sem("lru_conv")
        lru_gate = sem("lru_gate")
        lru_rate = [sem(f"lru_rate{i}") for i in range(5)]
        lru_ea = sem("lru_ea")
        lru_q = sem("lru_q")
        lru_m = sem("lru_m")
        lru_y = sem("lru_y")
        mq = sem("mq")
        mv = sem("mv")
        m_sc, m_max, m_exp, m_p, m_tr, m_pt, m_o, m_y = [sem(f"m_{k}") for k in
                                                       ("sc", "max", "exp", "p", "tr", "pt", "o", "y")]
        mup_r = sem("mup_r")
        mup = sem("mup")
        mix = sem("mix")
        rkv = sem("rkv")
        lora = sem("lora")
        lw = sem("lw")
        la = sem("la")
        kk_s = [sem(f"kk_{k}") for k in ("raw", "sq", "sum", "rt", "done")]
        cum = sem("cum")
        mid_e = sem("mid_e")
        ch = [{k: sem(f"ch{L}_{k}") for k in ("exp", "hat", "tr", "tok", "g1", "g2", "g2m", "x0t", "x0", "z", "zm", "x", "xc",
                                              "p", "pc", "u", "uc", "s", "yc", "sc")} for L in range(2)]
        gn = [sem(f"gn_{k}") for k in ("mean", "yc", "sq", "var", "std", "bp", "bonus", "sum", "g", "out")]

        block = ctx.enter_context(nc.Block())

        @block.sync
        def _(sp):
            sp.dma_start(X[:], a["x"]).then_inc(x_in, 16)
            for j in range(RING):
                sp.dma_start(ring[:, j, :], a["weights"][j]).then_inc(landed[j], 16)
            sp.dma_start(CST[:], a["cst"]).then_inc(cst_in, 16)
            sp.dma_start(PAR2[:], a["par2"]).then_inc(par2_in, 16)
            with sp.Fori(1, N_CHUNKS // RING) as q:
                for j in range(RING):
                    sp.wait_ge(used, q * RING + (j + 1 - RING))
                    sp.dma_start(ring[:, j, :], a["weights"][bass.ds(q * RING + j, 1)]
                                 .rearrange("a p c -> (a p) c")).then_inc(landed[j], 16)
            sp.wait_ge(xr2, 6 * KT)
            sp.dma_start(out, X[:]).then_inc(out_done, 16)
            sp.wait_ge(out_done, 16)

        @block.tensor
        def _(pe):
            mm = nc.tensor.matmul

            def arrived(quad, j):
                pe.wait_ge(landed[j], quad * 16 + 16)

            def w(j, k, n=P):
                return ring[:, j, k * n:k * n + n]

            def product(j, bank, src, nk=KT):
                for k in range(nk):
                    ins = mm(ps[:, bank, :], w(j, k), src[:, k, :], start=(k == 0), stop=(k == nk - 1))
                ins.then_inc(used, 1)

            def tokens(quad, banks, n):
                for j in range(RING):
                    arrived(quad, j)
                    for t in range(ST):
                        for e in range(2):
                            k = 2 * j + e
                            ins = mm(ps[:, banks + t, 0:n], X[:, k, t * P:t * P + P],
                                     ring[:, j, e * 512:e * 512 + n], start=(k == 0), stop=(k == KT - 1))
                    ins.then_inc(used, 1)

            def layer_norm(l, i, pre, pre_base):
                s, at = ln, l * 2 + i
                for n in range(KT):
                    pe.wait_ge(pre, l * KT + pre_base + n + 1)
                    ins = mm(ps[:, 4, :], cst("mean"), X[:, n, :], start=(n == 0), stop=(n == KT - 1))
                ins.then_inc(s["mean"], 1)
                for n in range(KT):
                    pe.wait_ge(s["sq"], at * KT + n + 1)
                    ins = mm(ps[:, 5, :], cst("mean"), T[:, n, :], start=(n == 0), stop=(n == KT - 1))
                ins.then_inc(s["var"], 1)

            def scores(l, u):
                kind, qi, which = UNITS[u]
                W = (qi + 1) * P
                if u > 0:
                    pe.wait_ge(at_exp, l * NU + u)
                for m in range(4):
                    if kind == "diff":
                        h, o = 2 * which + m // 2, (m % 2) * HD
                        q, k = Z[o:o + HD, Z_DQ + h, qi * P:W], Z[o:o + HD, Z_DK + h, 0:W]
                    else:
                        o = which * HD
                        q, k = Z[o:o + HD, Z_NQ + m, qi * P:W], Z[o:o + HD, Z_KS + kind, 0:W]
                    mm(ps[:, m, 0:W], q, k, start=True, stop=False)
                    ins = mm(ps[:, m, qi * P:W], cst("ident"), cst("maskneg"), start=False, stop=True)
                ins.then_inc(at_sc, 1)

            def turn(l, u, i):
                kind, qi, which = UNITS[u]
                t = HEADS_BEFORE[u] + i
                if i == 0:
                    if kind == "diff":
                        pe.wait_ge(at_comb, l * (NU // 3) + u + 1)
                    else:
                        pe.wait_ge(at_exp, l * NU + u + 1)
                if t >= 2:
                    pe.wait_ge(at_pt, l * NHEADS + t - 1)
                m = 2 * i if kind == "diff" else i
                for kb in range(qi + 1):
                    ins = nc.tensor.transpose(ps[:, 4 + t % 2, kb * P:kb * P + P],
                                              N[:, (u % 2) * 4 + m, kb * P:kb * P + P], cst("ident"))
                ins.then_inc(at_tr, 1)

            def values(l, u, i):
                kind, qi, which = UNITS[u]
                t = HEADS_BEFORE[u] + i
                if i == 0 and u >= 2:
                    pe.wait_ge(at_out, l * NU + u - 1)
                pe.wait_ge(at_pt, l * NHEADS + t + 1)
                for kb in range(qi + 1):
                    if kind == "diff":
                        h = 2 * which + i
                        o, v = ps[:, 6 + u % 2, i * P:i * P + P], DV[:, kb, h * P:h * P + P]
                    else:
                        c = kind * P + which * HD
                        o, v = ps[:, 6 + u % 2, i * HD:i * HD + HD], VSG[:, kb, c:c + HD]
                    ins = mm(o, PT[:, t % 4, kb * P:kb * P + P], v, start=(kb == 0), stop=(kb == qi))
                ins.then_inc(at_av, 1)

            pe.wait_ge(x_in, 16)
            pe.wait_ge(cst_in, 16)
            with pe.Fori(0, DEPTH) as l:
                Q = l * (CPL // RING)
                with pe.Fori(0, C_Z // RING) as i:
                    pe.wait_ge(x_ready, l * 16 + 16)
                    for j in range(RING):
                        pe.wait_ge(zc, l * C_Z + i * RING + (j + 1))
                        arrived(Q + i, j)
                        product(j, j, X)
                tokens(Q + B_DV // RING, 4, DH * P)
                pe.wait_ge(zc, l * C_Z + C_Z + 4)
                for r, t in enumerate(ROPE_TILES):
                    if r >= 4:
                        pe.wait_ge(rope, l * NR + r - 3)
                    mm(ps[:, r % 4, :], cst("rot"), Z[:, t, :], start=True, stop=True).then_inc(rot, 1)
                pe.wait_ge(tokc, l * 8 + 4)
                tokens(Q + B_VSG // RING, 4, VSG_N)
                pe.wait_ge(rope, l * NR + NR)
                pe.wait_ge(cmpin, l * 4 + 4)
                for c in range(C_PHI):
                    kv = c // 4
                    arrived(Q + (B_PHI + c) // RING, c % RING)
                    for e in range(8):
                        p = (c % 4) * 8 + e
                        for g in range(NG):
                            src = T[g * HD:g * HD + HD, 2 * kv + p // 16, p:p + CMP_STRIDE * (NCMP - 1) + 1:CMP_STRIDE]
                            ins = mm(ps[:, 2 * kv + g, 0:NCMP], ring[g * HD:g * HD + HD, c % RING, e * P:e * P + P], src,
                                     start=(p == 0), stop=(p == CMP_BLOCK - 1))
                    ins.then_inc(used, 1)
                pe.wait_ge(phih, l * 4 + 4)
                pe.wait_ge(tokc, l * 8 + 8)
                for g in range(NG):
                    mm(ps[:, 4, g * 32:g * 32 + NCMP], par("phi_w2k"), H[:, 0, g, 0:NCMP], start=True, stop=True)
                    ins = mm(ps[0:NCMP, 5, g * HD:g * HD + HD], H[:, 1, g, 0:NCMP], par("phi_w2v"), start=True, stop=True)
                ins.then_inc(phio, 1)
                pe.wait_ge(cmpkv, l + 1)
                for qi in range(ST):
                    for g in range(NG):
                        for r in range(HPG):
                            c = qi * P + r * 32
                            ins = mm(ps[:, g, c:c + NCMP], Z[g * HD:g * HD + HD, Z_NQ + r, qi * P:qi * P + P],
                                     KCC[g * HD:g * HD + HD, 0:NCMP], start=True, stop=True)
                ins.then_inc(cs_mm, 1)
                pe.wait_ge(cs_p, l + 1)
                for qi in range(ST):
                    b = 2 + 2 * (qi % 3)
                    if qi == 3:
                        pe.wait_ge(cs_pt, l * ST + 1)
                    for h in range(NH):
                        ins = nc.tensor.transpose(ps[0:NCMP, b + h // 4, (h % 4) * P:(h % 4) * P + P], CS[:, qi, h, :], cst("ident"))
                    ins.then_inc(cs_tr, 1)
                for qi in range(ST):
                    pe.wait_ge(cs_pt, l * ST + qi + 1)
                    if qi >= 2:
                        pe.wait_ge(cs_out, l * ST + qi - 1)
                    for h in range(NH):
                        e = T[0:NCMP, qi * 2 + h // 4, (h % 4) * P:(h % 4) * P + P]
                        ins = mm(ps[:, qi % 2, h * HD:h * HD + HD], e, VCC[0:NCMP, h // HPG, :], start=True, stop=True)
                    ins.then_inc(cs_av, 1)
                pe.wait_ge(cs_out, l * ST + ST)
                scores(l, 0)
                for u in range(NU):
                    if u + 1 < NU:
                        scores(l, u + 1)
                    n = HEADS_OF[u]
                    turn(l, u, 0)
                    for i in range(n):
                        if i + 1 < n:
                            turn(l, u, i + 1)
                        values(l, u, i)
                pe.wait_ge(at_out, l * NU + NU)
                for c in range(4):
                    for t in range(ST):
                        ins = nc.tensor.transpose(ps[:, c, t * P:t * P + P],
                                                  YC[:, t, 2 * c:2 * c + 2, :].rearrange("p h d -> p (h d)"), cst("ident"))
                    ins.then_inc(ytr, 1)
                pe.wait_ge(yb_fin, l + 1)
                for c in range(4):
                    for t in range(ST):
                        ins = nc.tensor.transpose(ps[:, 4 + c, t * P:t * P + P], YB[:, t, c, :], cst("ident"))
                    ins.then_inc(ytr, 1)
                with pe.Fori(0, 3) as b:
                    pe.wait_ge(yfin, l * 8 + 8)
                    pe.wait_ge(conv_out, l * 4 + 4)
                    for p in range(4):
                        for e in range(2):
                            c = 3 * p + e
                            pe.wait_ge(sg, l * 24 + b * 8 + (2 * p + e + 1))
                            arrived(Q + (B_MERGE // RING) + b * 3 + c // RING, c % RING)
                            product(c % RING, (2 * p + e) % 4, X)
                        c = 3 * p + 2
                        arrived(Q + (B_MERGE // RING) + b * 3 + c // RING, c % RING)
                        for e in range(2):
                            pe.wait_ge(mg, l * 24 + b * 8 + (2 * p + e + 1))
                            for k in range(4):
                                ins = mm(ps[:, 4 + (2 * p + e) % 4, :], w(c % RING, e * 4 + k),
                                         Y[:, bass.ds(b * 4 + k, 1), :].rearrange("p a t -> p (a t)"), start=(k == 0), stop=(k == 3))
                        ins.then_inc(used, 1)
                with pe.Fori(0, 2) as i:
                    pe.wait_ge(mg, l * 24 + 28)
                    for j in range(RING):
                        pe.wait_ge(x1pre, l * KT + i * RING + (j + 1))
                        arrived(Q + B_WO // RING + i, j)
                        product(j, j, N)
                layer_norm(l, 0, x1pre, 4)
                with pe.Fori(0, C_UP // RING) as i:
                    pe.wait_ge(x1, l * KT + KT)
                    for j in range(RING):
                        pe.wait_ge(up_c, l * C_UP + i * RING + (j + 1))
                        arrived(Q + B_UP // RING + i, j)
                        product(j, j, X)
                with pe.Fori(0, 2) as i:
                    pe.wait_ge(up_h, l * FT + FT + 2)
                    for n in range(4):
                        pe.wait_ge(x2pre, l * KT + i * 4 + (n + 1))
                        for c in range(3):
                            f = 3 * n + c
                            arrived(Q + B_DOWN // RING + i * 3 + f // RING, f % RING)
                            for k in range(8 * c, min(8 * c + 8, FT)):
                                ins = mm(ps[:, n, :], w(f % RING, k - 8 * c), Z[:, k, :], start=(k == 0), stop=(k == FT - 1))
                            ins.then_inc(used, 1)
                layer_norm(l, 1, x2pre, 4)

            def rms(i, bank_cols=S, sq=None):
                for n in range(KT):
                    pe.wait_ge(rms_sq, i * KT + n + 1)
                    src = T[:, n, 0:bank_cols]
                    ins = mm(ps[:, 5, 0:bank_cols], cst("mean"), src, start=(n == 0), stop=(n == KT - 1))
                ins.then_inc(rms_var, 1)

            def gemm(first, tiles, src, free, base, start=()):
                with pe.Fori(0, tiles // RING) as i:
                    for sm, val in start:
                        pe.wait_ge(sm, val)
                    for j in range(RING):
                        pe.wait_ge(free, i * RING + (base + j + 1))
                        arrived(i + first // RING, j)
                        product(j, j, src)

            def tail(l):
                B = B_TAIL0 if l == 0 else B_TAIL1
                rms(3 + 6 * l)
                gemm(B, C_MQ, N, mq, l * 16, [(rms_y, NORMED[3 + 6 * l])])
                with pe.Fori(0, C_MK // RING) as i:
                    for j in range(RING):
                        pe.wait_ge(mq, i * RING + (l * 16 + 8 + j + 1))
                        arrived(i + (B + C_MQ) // RING, j)
                        for k in range(KT):
                            ins = mm(ps[:, j, 0:S2], w(j, k), MN[:, k, :], start=(k == 0), stop=(k == KT - 1))
                        ins.then_inc(used, 1)
                for c in range(C_MV):
                    half, j = c // 4, c % 4
                    arrived((B + C_MQ + C_MK + c) // RING, j)
                    for t in range(2):
                        for e in range(2):
                            k = 2 * j + e
                            ins = mm(ps[:, 4 + 2 * half + t, :], MN[:, k, t * P:t * P + P], ring[:, j, e * 512:e * 512 + 512],
                                     start=(k == 0), stop=(k == KT - 1))
                    ins.then_inc(used, 1)
                pe.wait_ge(mq, l * 16 + 20)

                def scores2(qi):
                    if qi >= 2:
                        pe.wait_ge(m_exp, l * ST + qi - 1)
                    for h in range(MH):
                        for k in range(MT):
                            ins = mm(ps[:, 2 * (qi % 2) + h // 2, (h % 2) * S2:(h % 2) * S2 + S2],
                                     Z[:, h * MT + k, qi * P:qi * P + P], MK[:, h * MT + k, :], start=(k == 0), stop=(k == MT - 1))
                    ins.then_inc(m_sc, 1)

                scores2(0)
                for qi in range(ST):
                    if qi + 1 < ST:
                        scores2(qi + 1)
                    if qi == 0:
                        pe.wait_ge(mv, l * 4 + 4)
                    pe.wait_ge(m_p, l * ST + qi + 1)
                    for kb in range(2):
                        if qi >= 2:
                            pe.wait_ge(m_pt, l * 2 * ST + 2 * (qi - 2) + kb + 1)
                        for h in range(MH):
                            ins = nc.tensor.transpose(ps[:, 4 + 2 * (qi % 2) + kb, h * P:h * P + P],
                                                      MP[:, qi % 2, h, kb * P:kb * P + P], cst("ident"))
                        ins.then_inc(m_tr, 1)
                pe.wait_ge(m_pt, l * 2 * ST + 2 * ST)
                for c in range(KT):
                    h = c // MT
                    if c >= 4:
                        pe.wait_ge(m_y, l * KT + c - 3)
                    for kb in range(2):
                        ins = mm(ps[:, c % 4, :], MV[:, kb, c * P:c * P + P], Z[:, 16 + 2 * h + kb, :], start=(kb == 0), stop=(kb == 1))
                    ins.then_inc(m_o, 1)
                gemm(B + C_MQ + C_MK + C_MV, C_MO, Y, t_ready, l * 24 + 8, [(m_y, l * KT + KT)])
                rms(4 + 6 * l)
                rms(5 + 6 * l)
                gemm(B + C_MQ + C_MK + C_MV + C_MO, C_MUP, N, mup, l * F2T, [(rms_y, NORMED[5 + 6 * l])])
                with pe.Fori(0, 2) as i:
                    pe.wait_ge(mup, l * F2T + F2T + 4)
                    for n in range(4):
                        pe.wait_ge(t_ready, i * 4 + (l * 24 + 16 + n + 1))
                        for c in range(4):
                            arrived(i * 4 + ((B + C_TAIL - C_MDN) // RING + n), c)
                            for k in range(8):
                                ins = mm(ps[:, n, :], w(c, k), HID[8 * c + k], start=(c == 0 and k == 0), stop=(c == 3 and k == 7))
                            ins.then_inc(used, 1)
                rms(6 + 6 * l)

            rms(0, S2)
            rms(1)
            gemm(B_LRU, C_LRU_IN, N, lru_in, 0, [(rms_y, NORMED[1])])
            pe.wait_ge(lru_conv, KT)
            pe.wait_ge(lru_in, 20)
            for c in range(C_LRU_GATE):
                arrived((B_LRU + C_LRU_IN + c) // RING, c)
                if c >= 2:
                    pe.wait_ge(lru_gate, 4 * (c - 1))
                for b in range(4):
                    k0 = (c % 2) * 4 + (b // 2) * 2
                    for k in range(2):
                        ins = mm(ps[:, 4 * (c % 2) + b, :], w(c, b * 2 + k), Z[:, 16 + k0 + k, :], start=(k == 0), stop=(k == 1))
                ins.then_inc(used, 1)
            gemm(B_LRU + C_LRU_IN + C_LRU_GATE, C_LRU_OUT, Z[:, 16:24, :], t_ready, 0, [(lru_y, KT)])
            rms(2)
            tail(0)

            rms(7)
            for m in range(3):
                pe.wait_ge(mix, KT * (m + 1))
                for n in range(KT):
                    c = m * KT + n
                    pe.wait_ge(rkv, c + 1)
                    arrived((B_RWKV + c) // RING, c % RING)
                    for k in range(KT):
                        ins = mm(ps[:, c % 4, :], w(c % RING, k), MIX[m % 2][k], start=(k == 0), stop=(k == KT - 1))
                    ins.then_inc(used, 1)
            QL = (B_RWKV + C_RKV) // RING
            pe.wait_ge(mix, 4 * KT)
            arrived(QL, 0)
            for k in range(KT):
                ins = mm(ps[0:HD, 4, :], ring[:, 0, k * HD:k * HD + HD], MIX[1][k], start=(k == 0), stop=(k == KT - 1))
            ins.then_inc(lora, 1)
            pe.wait_ge(mix, 5 * KT)
            for k in range(KT):
                ins = mm(ps[0:HD, 5, :], ring[:, 0, 512 + k * HD:512 + k * HD + HD], MIX[0][k], start=(k == 0), stop=(k == KT - 1))
            ins.then_inc(used, 1)
            pe.wait_ge(mix, 6 * KT)
            arrived(QL, 1)
            for k in range(KT):
                ins = mm(ps[:, 6, :], w(1, k), MIX[1][k], start=(k == 0), stop=(k == KT - 1))
            ins.then_inc(used, 1)
            arrived(QL, 2)
            pe.wait_ge(rkv, 3 * KT + 4)
            pe.wait_ge(la, 1)
            for n in range(KT):
                if n >= 4:
                    pe.wait_ge(lw, n - 3)
                ins = mm(ps[:, n % 4, :], ring[0:HD, 2, n * P:n * P + P], TW, start=True, stop=True)
                ins.then_inc(lora, 1)
            arrived(QL, 3)
            pe.wait_ge(la, 3)
            for n in range(KT):
                if n >= 4:
                    pe.wait_ge(la, 3 + n - 3)
                ins = mm(ps[:, 4 + n % 4, :], ring[0:HD, 3, n * P:n * P + P], TA_, start=True, stop=True)
                ins.then_inc(lora, 1)
            pe.wait_ge(lw, KT)
            pe.wait_ge(la, 3 + KT)
            pe.sem_inc(used, 2)
            pe.wait_ge(cst2_in, 16)
            for n in range(KT):
                pe.wait_ge(kk_s[1], n + 1)
                if n >= 4:
                    pe.wait_ge(kk_s[3], n - 3)
                mm(ps[:, n % 4, :], cst2("ones"), Z[:, 24 + n % 2, :], start=True, stop=True).then_inc(kk_s[2], 1)

            def chain(c, half, L):
                s, B, o = ch[L], LANES[L], 4 * L
                return s, B, o, c * 2 + half

            with pe.Fori(0, RC) as c:
                for half in range(2):
                    for L in range(2):
                        s, B, o, it = chain(c, half, L)
                        pe.wait_ge(s["hat"], it + 1)
                        for e in range(2):
                            for n in range(2):
                                ins = nc.tensor.transpose(ps[:, o, (2 * e + n) * P:(2 * e + n) * P + P], B["bk"][:, e, n, :], cst("ident"))
                        for n in range(2):
                            ins = nc.tensor.transpose(ps[:, o + 1, n * P:n * P + P], B["x"][:, n, :], cst("ident"))
                        ins.then_inc(s["tr"], 1)
                        for q in range(4):
                            r, n = (q % 2) * HD, q // 2
                            ins = mm(ps[:, o + 2 + q % 2, n * 2 * P:n * 2 * P + 2 * P], B["bk"][r:r + HD, 0, n, :],
                                     B["ar"][r:r + HD, n, :, :].rearrange("p a t -> p (a t)"), start=True, stop=True)
                        ins.then_inc(s["g1"], 1)
                    for L in range(2):
                        s, B, o, it = chain(c, half, L)
                        pe.wait_ge(s["tok"], it + 1)
                        for q in range(4):
                            r, n = (q % 2) * HD, q // 2
                            ins = mm(ps[:, o + q % 2, n * 2 * P:n * 2 * P + 2 * P], B["bk"][r:r + HD, 1, n, :],
                                     B["ar"][r:r + HD, n, :, :].rearrange("p a t -> p (a t)"), start=True, stop=True)
                        ins.then_inc(s["g2"], 1)
                    for L in range(2):
                        s, B, o, it = chain(c, half, L)
                        pe.wait_ge(s["x0t"], it + 1)
                        for q in range(4):
                            ins = nc.tensor.transpose(ps[:, o + 2, q * P:q * P + P], B["xt"][:, q, :], cst("ident"))
                        ins.then_inc(s["x0"], 1)
                    for v in range(LEVELS):
                        for L in range(2):
                            s, B, o, it = chain(c, half, L)
                            if v == 0:
                                pe.wait_ge(s["g2m"], it + 1)
                            pe.wait_ge(s["xc"], it * (2 * LEVELS + 1) + 2 * v + 1)
                            for q in range(4):
                                ins = mm(ps[:, o, q * P:q * P + P], B["g1"][:, q, 0, :], B["x"][:, q, :], start=True, stop=True)
                            ins.then_inc(s["z"], 1)
                        for L in range(2):
                            s, B, o, it = chain(c, half, L)
                            pe.wait_ge(s["zm"], it * LEVELS + v + 1)
                            for q in range(4):
                                ins = mm(ps[:, o + 1, q * P:q * P + P], B["xt"][:, q, :], B["z"][:, q, :], start=True, stop=True)
                            ins.then_inc(s["x"], 1)
                            for q in range(4):
                                ins = mm(ps[:, o + 2, q * P:q * P + P], B["z"][:, q, :], B["xt"][:, q, :], start=True, stop=True)
                            ins.then_inc(s["x"], 1)
                    for L in range(2):
                        s, B, o, it = chain(c, half, L)
                        pe.wait_ge(s["xc"], it * (2 * LEVELS + 1) + 2 * LEVELS + 1)
                        for q in range(4):
                            r, n = (q % 2) * HD, q // 2
                            mm(ps[:, o + q % 2, n * HD:n * HD + HD], B["ar"][r:r + HD, n, 0, :], B["sh"][r:r + HD, n, :], start=True, stop=False)
                            ins = mm(ps[:, o + q % 2, n * HD:n * HD + HD], B["g2"][:, q, 0, :], B["vtok"][:, n, r:r + HD], start=False, stop=True)
                        ins.then_inc(s["p"], 1)
                    for L in range(2):
                        s, B, o, it = chain(c, half, L)
                        pe.wait_ge(s["pc"], it + 1)
                        for q in range(4):
                            ins = mm(ps[:, o + 2, q * HD:q * HD + HD], B["xt"][:, q, :], B["pu"][:, 0, q, :], start=True, stop=True)
                        ins.then_inc(s["u"], 1)
                    for L in range(2):
                        s, B, o, it = chain(c, half, L)
                        pe.wait_ge(s["uc"], it + 1)
                        for n in range(2):
                            y = ps[:, o, n * P:n * P + P]
                            mm(y, B["bktok"][:, 0, n, :], B["pu"][:, 1, 2 * n:2 * n + 2, :].rearrange("p q i -> p (q i)"), start=True, stop=False)
                            mm(y, B["bktok"][:, 1, n, :], B["vtok"][:, n, :], start=False, stop=True)
                        for q in range(4):
                            r, n = (q % 2) * HD, q // 2
                            y = ps[r:r + HD, o + 3, n * P:n * P + P]
                            mm(y, B["sh"][r:r + HD, n, :], B["ar"][r:r + HD, n, 1, :], start=True, stop=False)
                            mm(y, B["pu"][:, 1, q, :], B["g1"][:, q, 1, :], start=False, stop=False)
                            ins = mm(y, B["vtok"][:, n, r:r + HD], B["g2"][:, q, 1, :], start=False, stop=True)
                        ins.then_inc(s["s"], 1)

            for L in range(2):
                pe.wait_ge(ch[L]["yc"], 2 * RC)
                pe.wait_ge(ch[L]["sc"], 2 * RC)
            arrived((B_RWKV + C_RKV + C_LORA) // RING, 0)
            for n in range(KT):
                if n >= 2:
                    pe.wait_ge(gn[9], n - 1)
                o = 4 * (n % 2)
                mm(ps[:, o, :], cst2("ones"), T[:, n, :], start=True, stop=True).then_inc(gn[0], 1)
                pe.wait_ge(gn[5], n + 1)
                mm(ps[:, o + 2, :], cst2("ones"), Z[:, 24 + n % 2, :], start=True, stop=True).then_inc(gn[7], 1)
                ins = mm(ps[:, o + 3, :], w(0, n), TG, start=True, stop=True)
                ins.then_inc(gn[8], 1)
                pe.wait_ge(gn[2], n + 1)
                mm(ps[:, o + 1, :], cst2("ones"), Z[:, 26 + n % 2, :], start=True, stop=True).then_inc(gn[3], 1)
            pe.wait_ge(gn[9], KT)
            for j in range(1, RING):
                arrived((B_RWKV + C_RKV + C_LORA) // RING, j)
            pe.sem_inc(used, 4)
            gemm(B_RWKV + C_RKV + C_LORA + C_G2, C_RWO, Y, t_ready, 24, [(gn[9], KT)])
            rms(8)
            tail(1)

        @block.scalar
        def _(act):
            av = nc.scalar.activation

            def layer_norm(l, i, gain, bias, done, each):
                s, at = ln, l * 2 + i
                for n in range(KT):
                    act.wait_ge(s["xc"], at * KT + n + 1)
                    av(T[:, n, :], X[:, n, :], ACT.Square).then_inc(s["sq"], 1)
                act.wait_ge(s["var"], at + 1)
                av(RS[:], ps[:, 5, :], ACT.Sqrt, bias=cst("eps")).then_inc(s["std"], 1)
                for n in range(KT):
                    act.wait_ge(s["y"], at * KT + n + 1)
                    av(X[:, n, :], X[:, n, :], ACT.Identity, bias=par(bias, n, 1)).then_inc(done, each)

            act.sem_inc(zc, 4)
            act.sem_inc(sg, 4)
            act.sem_inc(mg, 4)
            act.sem_inc(x1pre, 4)
            act.sem_inc(x2pre, 4)
            act.sem_inc(up_c, 4)
            act.sem_inc(up_h, 2)
            for free in (lru_in, t_ready, mq, mup, rkv):
                act.sem_inc(free, 4)
            for L in range(2):
                act.sem_inc(ch[L]["s"], 1)
            act.wait_ge(x_in, 16)
            act.sem_inc(x_ready, 16)
            act.wait_ge(cst_in, 16)
            with act.Fori(0, DEPTH) as l:
                C = l * CPL
                act.wait_ge(x_ready, l * 16 + 16)
                act.dma_start(PAR[:], a["par"][bass.ds(l, 1)].rearrange("a p c -> (a p) c")).then_inc(par_in, 16)
                with act.Fori(0, C_Z // RING) as i:
                    for j in range(RING):
                        act.wait_ge(used, C + i * RING + (j + 1))
                        av(Z[:, bass.ds(i * RING + j, 1), :], ps[:, j:j + 1, :], ACT.Copy).then_inc(zc, 1)
                act.wait_ge(used, C + B_DV + C_DV)
                for t in range(ST):
                    av(DV[:, t, :], ps[:, 4 + t, :], ACT.Copy).then_inc(tokc, 1)
                act.wait_ge(used, C + B_VSG + C_VSG)
                for t in range(ST):
                    av(VSG[:, t, :], ps[:, 4 + t, 0:VSG_N], ACT.Copy).then_inc(tokc, 1)
                act.wait_ge(tokc, l * 8 + 8)
                av(GSIG[:].rearrange("p t b h -> p t (b h)"), VSG[:, :, 2 * P:VSG_N], ACT.Sigmoid).then_inc(gsig, 1)
                act.wait_ge(used, C + B_PHI + C_PHI)
                for kv in range(2):
                    for g in range(NG):
                        av(H[:, kv, g, 0:NCMP], ps[:, 2 * kv + g, 0:NCMP], ACT.Gelu).then_inc(phih, 1)
                act.wait_ge(lam_d, l + 1)
                av(LAM[:, 2 * HD + 2:2 * HD + 4], LAM[:, 2 * HD:2 * HD + 2], ACT.Exp).then_inc(lam_e, 1)
                act.wait_ge(cs_sub, l + 1)
                av(CS[:], CS[:], ACT.Exp, scale=SCALE).then_inc(cs_exp, 1)
                for qi in range(ST):
                    act.wait_ge(cs_tr, l * ST + qi + 1)
                    b = 2 + 2 * (qi % 3)
                    av(T[0:NCMP, 2 * qi:2 * qi + 2, :], ps[0:NCMP, b:b + 2, :], ACT.Copy).then_inc(cs_pt, 1)
                for u in range(NU):
                    W = (UNITS[u][1] + 1) * P
                    act.wait_ge(at_max, l * NU + u + 1)
                    if u >= 2:
                        act.wait_ge(at_av, l * NHEADS + HEADS_BEFORE[u - 1])
                    for m in range(4):
                        ins = av(N[:, (u % 2) * 4 + m, 0:W], ps[:, m, 0:W], ACT.Exp, bias=AM[:, u % 2, 1, m:m + 1],
                                 scale=SCALE, accum_out=AM[:, u % 2, 2, m:m + 1])
                    ins.then_inc(at_exp, 1)
                act.wait_ge(at_out, l * NU + NU)
                av(T[:, 0:4, :], YB[:].rearrange("p t h d -> p t (h d)"), ACT.Square).then_inc(yb_sq, 1)
                act.wait_ge(yb_ms, l + 1)
                av(MS[:, 1, :], MS[:, 0, :], ACT.Sqrt, bias=cst("eps"), scale=1.0 / P).then_inc(yb_rt, 1)
                for c in range(8):
                    act.wait_ge(ytr, l * 8 + c + 1)
                    if c < 4:
                        av(Y[:, 8 + c, :], ps[:, c, :], ACT.Copy).then_inc(yfin, 1)
                    else:
                        av(Y[:, c, :], ps[:, c, :], ACT.Copy, scale=LAM[:, 2 * HD + 6:2 * HD + 7]).then_inc(yfin, 1)
                with act.Fori(0, 3) as b:
                    for n in range(KT):
                        c = 3 * (n // 2) + n % 2
                        act.wait_ge(used, C + B_MERGE + b * 12 + (c + 1))
                        act.wait_ge(mg, l * 24 + b * 8 + (n + 1))
                        av(T[:, n % 4, :], ps[:, n % 4, :], ACT.Sigmoid).then_inc(sg, 1)
                layer_norm(l, 0, "ln1_g", "ln1_b", x1, 1)
                with act.Fori(0, C_UP // RING) as i:
                    for e in range(2):
                        act.wait_ge(up_h, l * FT + i * 2 + (e + 1))
                        for v in range(2):
                            j = 2 * e + v
                            act.wait_ge(used, C + B_UP + i * RING + (j + 1))
                            f = i * 2 + (e + v * FT)
                            av(T[:, j, :], ps[:, j, :], ACT.Identity, bias=PAR[:, bass.ds(f + PCOL["up_b"][0], 1)],
                               scale=PAR[:, bass.ds(f + (PCOL["up_w"][0] + 2 * 2 * FT), 1)]).then_inc(up_a, 1)
                        act.wait_ge(up_c, l * C_UP + i * RING + (2 * e + 5))
                        av(T[:, 4 + e, :], T[:, 2 * e, :], ACT.Gelu).then_inc(up_g, 1)
                layer_norm(l, 1, "ln2_g", "ln2_b", x_ready, 2)

            def rms(i, src, ready, base, cols=S):
                for n in range(KT):
                    if ready is not None:
                        act.wait_ge(ready, base + n + 1)
                    av(T[:, n, 0:cols], src[:, n, :], ACT.Square).then_inc(rms_sq, 1)
                act.wait_ge(rms_var, i + 1)
                if i == 1:
                    act.wait_ge(rms_y, NORMED[0])
                av(RS[:, 0:cols], ps[:, 5, 0:cols], ACT.Sqrt, bias=par2("rms_eps")).then_inc(rms_std, 1)

            def copies(first, tiles, dst, at, done, func=ACT.Copy, cols=S, bias=None):
                with act.Fori(0, tiles // RING) as i:
                    for j in range(RING):
                        act.wait_ge(used, i * RING + (first + j + 1))
                        kw = {} if bias is None else {"bias": PAR2[:, bass.ds(i * RING + (bias + j), 1)]}
                        av(dst[:, bass.ds(i * RING + (at + j), 1), :], ps[:, j:j + 1, 0:cols], func, **kw).then_inc(done, 1)

            def tail(l):
                B = B_TAIL0 if l == 0 else B_TAIL1
                rms(3 + 6 * l, X, xr2, 3 * KT * l)
                copies(B, C_MQ, Z, 0, mq)
                copies(B + C_MQ, C_MK, MK, 0, mq, cols=S2)
                for half in range(2):
                    act.wait_ge(used, B + C_MQ + C_MK + 4 * half + 4)
                    for t in range(2):
                        av(MV[:, t, half * 512:half * 512 + 512], ps[:, 4 + 2 * half + t, :], ACT.Copy).then_inc(mv, 1)

                def exps(qi):
                    act.wait_ge(m_max, l * ST + qi + 1)
                    if qi >= 2:
                        act.wait_ge(m_tr, l * 2 * ST + 2 * (qi - 1))
                    for h in range(MH):
                        ins = av(MP[:, qi % 2, h, :], ps[:, 2 * (qi % 2) + h // 2, (h % 2) * S2:(h % 2) * S2 + S2], ACT.Exp,
                                 bias=AM[:, qi % 2, 1, h:h + 1], scale=(MT * P) ** -0.5, accum_out=AM[:, qi % 2, 2, h:h + 1])
                    ins.then_inc(m_exp, 1)

                exps(0)
                for qi in range(ST):
                    if qi + 1 < ST:
                        exps(qi + 1)
                    for kb in range(2):
                        act.wait_ge(m_tr, l * 2 * ST + 2 * qi + kb + 1)
                        av(Z[:, 16 + kb:24:2, qi * P:qi * P + P],
                           ps[:, 4 + 2 * (qi % 2) + kb, :].rearrange("p (h q) -> p h q", h=MH), ACT.Copy).then_inc(m_pt, 1)
                for c in range(KT):
                    act.wait_ge(m_o, l * KT + c + 1)
                    av(Y[:, c, :], ps[:, c % 4, :], ACT.Copy).then_inc(m_y, 1)
                copies(B + C_MQ + C_MK + C_MV, C_MO, N, 0, t_ready)
                rms(4 + 6 * l, N, t_ready, 4 + l * 24 + 8)
                rms(5 + 6 * l, X, xr2, 3 * KT * l + KT)
                U = B + C_MQ + C_MK + C_MV + C_MO
                with act.Fori(0, C_MUP // RING) as i:
                    for j in range(RING):
                        act.wait_ge(used, i * RING + (U + j + 1))
                        act.wait_ge(mup, i * RING + (l * F2T + j + 1))
                        av(T[:, j, :], ps[:, j, :], ACT.Relu).then_inc(mup_r, 1)
                with act.Fori(0, 2) as i:
                    for n in range(4):
                        act.wait_ge(used, i * 16 + (U + C_MUP + 4 * n + 4))
                        av(N[:, bass.ds(i * 4 + n, 1), :], ps[:, n:n + 1, :], ACT.Copy).then_inc(t_ready, 1)
                rms(6 + 6 * l, N, t_ready, 4 + l * 24 + 16)

            act.wait_ge(x_ready, 16 * (DEPTH + 1))
            act.dma_start(MN, a["mem"]).then_inc(mem_in, 16)
            act.dma_start(CST2[:, 0:NCST2], a["cst2"]).then_inc(cst2_in, 16)
            act.wait_ge(par2_in, 16)
            act.wait_ge(mem_in, 16)
            rms(0, MN, None, 0, S2)
            rms(1, X, None, 0)
            copies(B_LRU, KT, Z, 0, lru_in, ACT.Gelu_apprx_tanh, bias=P2COL["b_in"][0])
            copies(B_LRU + KT, KT, Z, 8, lru_in, ACT.Identity, bias=P2COL["b_in"][0] + KT)
            act.wait_ge(lru_rate[0], 1)
            av(LRU[:, 1, :], LRU[:, 0, :], ACT.Exp, scale=-1.0).then_inc(lru_rate[1], 1)
            act.wait_ge(lru_rate[2], 1)
            av(LRU[:, 3, :], LRU[:, 2, :], ACT.Ln).then_inc(lru_rate[3], 1)
            for c in range(C_LRU_GATE):
                act.wait_ge(used, B_LRU + C_LRU_IN + c + 1)
                for b in range(4):
                    n = (c % 2) * 4 + b
                    av((Y if c < 2 else T)[:, n, :], ps[:, 4 * (c % 2) + b, :], ACT.Sigmoid,
                       bias=par2("gate_b", (c // 2) * KT + n, 1)).then_inc(lru_gate, 1)
            act.wait_ge(lru_gate, 16)
            act.wait_ge(lru_rate[4], 1)
            for n in range(KT):
                av(Z[:, 8 + n, :], Y[:, n, :], ACT.Tanh, scale=LRU[:, 2, n:n + 1]).then_inc(lru_ea, 1)
                av(Y[:, n, :], Y[:, n, :], ACT.Exp, scale=LRU[:, 3, n:n + 1]).then_inc(lru_ea, 1)
            for n in range(KT):
                act.wait_ge(lru_q, n + 1)
                av(Z[:, 8 + n, :], Z[:, 8 + n, :], ACT.Sqrt, scale=2.0).then_inc(lru_m, 1)
            copies(B_LRU + C_LRU_IN + C_LRU_GATE, C_LRU_OUT, N, 0, t_ready, ACT.Identity, bias=P2COL["b_out"][0])
            rms(2, N, t_ready, 4)
            tail(0)

            rms(7, X, xr2, 2 * KT)
            copies(B_RWKV, C_RKV, Z, 0, rkv)
            LB = B_RWKV + C_RKV
            act.wait_ge(lora, 1)
            av(TW, ps[0:HD, 4, :], ACT.Tanh).then_inc(la, 1)
            act.wait_ge(used, LB + 1)
            av(TA_, ps[0:HD, 5, :], ACT.Copy).then_inc(la, 1)
            act.wait_ge(used, LB + 2)
            av(TG, ps[:, 6, :], ACT.Sigmoid).then_inc(la, 1)
            for n in range(KT):
                act.wait_ge(lora, 2 + n)
                av(N[:, n, :], ps[:, n % 4, :], ACT.Sigmoid, bias=par2("w0", n, 1)).then_inc(lw, 1)
            for n in range(KT):
                act.wait_ge(lora, 2 + KT + n)
                av(T[:, n, :], ps[:, 4 + n % 4, :], ACT.Sigmoid, bias=par2("a0", n, 1)).then_inc(la, 1)

            def root(n):
                act.wait_ge(kk_s[2], n + 1)
                if n >= 2:
                    act.wait_ge(kk_s[4], n - 1)
                av(Z[:, 26 + n % 2, :], ps[:, n % 4, :], ACT.Sqrt).then_inc(kk_s[3], 1)

            for n in range(KT):
                av(Y[:, n, :], Z[:, 8 + n, :], ACT.Copy, scale=par2("k_k", n, 1)).then_inc(kk_s[0], 1)
                if n >= 2:
                    act.wait_ge(kk_s[2], n - 1)
                av(Z[:, 24 + n % 2, :], Z[:, 8 + n, :], ACT.Square, scale=par2("k_k", n, 1)).then_inc(kk_s[1], 1)
                if n >= 1:
                    root(n - 1)
            root(KT - 1)
            act.wait_ge(cum, KT)
            av(MID[:, 1:3], MID[:, 1:3], ACT.Exp, scale=-K0).then_inc(mid_e, 1)
            act.wait_ge(kk_s[4], KT)
            with act.Fori(0, RC) as c:
                for half in range(2):
                    def lane(L):
                        return ch[L], LANES[L], 4 * L, 2 * (2 * half + L), c * 2 + half

                    for L in range(2):
                        s, B, o, n0, it = lane(L)
                        act.wait_ge(s["s"], it + 1)
                        lws = N[:, n0:n0 + 2, bass.ds(c * P, P)]
                        av(B["e"][:, :, 0, 1:P + 1], lws, ACT.Exp, scale=-K0)
                        av(B["e"][:, :, 1, 0:P], lws, ACT.Exp, scale=K0)
                        av(B["e"][:, :, 0, 0:1], MID[:, 0, n0:n0 + 2, bass.ds(c, 1)], ACT.Exp, scale=K0)
                        av(B["x"][:, 0:2, :], Z[:, 16 + n0:18 + n0, bass.ds(c * P, P)], ACT.Copy).then_inc(s["exp"], 1)
                    for L in range(2):
                        s, B, o, n0, it = lane(L)
                        act.wait_ge(s["tr"], it + 1)
                        av(B["bktok"].rearrange("p a n c -> p (a n c)"), ps[:, o, :], ACT.Copy)
                        av(B["vtok"].rearrange("p n c -> p (n c)"), ps[:, o + 1, 0:2 * P], ACT.Copy).then_inc(s["tok"], 1)
                    for L in range(2):
                        s, B, o, n0, it = lane(L)
                        act.wait_ge(s["x0"], it + 1)
                        av(B["x"].rearrange("p q t -> p (q t)"), ps[:, o + 2, :], ACT.Copy).then_inc(s["xc"], 1)
                    for v in range(LEVELS):
                        for L in range(2):
                            s, B, o, n0, it = lane(L)
                            for e, t in enumerate(("x", "xt")):
                                act.wait_ge(s["x"], it * (2 * LEVELS) + 2 * v + e + 1)
                                av(B[t].rearrange("p q t -> p (q t)"), ps[:, o + 1 + e, :], ACT.Copy).then_inc(s["xc"], 1)
                    for L in range(2):
                        s, B, o, n0, it = lane(L)
                        act.wait_ge(s["p"], it + 1)
                        for r in range(2):
                            ins = av(B["pu"][:, 0, r:4:2, :], ps[:, o + r, 0:2 * HD].rearrange("p (n i) -> p n i", n=2), ACT.Copy)
                        ins.then_inc(s["pc"], 1)
                    for L in range(2):
                        s, B, o, n0, it = lane(L)
                        act.wait_ge(s["u"], it + 1)
                        av(B["pu"][:, 1].rearrange("p q i -> p (q i)"), ps[:, o + 2, 0:4 * HD], ACT.Copy).then_inc(s["uc"], 1)
                    for L in range(2):
                        s, B, o, n0, it = lane(L)
                        act.wait_ge(s["s"], it + 2)
                        av(T[:, n0:n0 + 2, bass.ds(c * P, P)], ps[:, o + 3, 0:2 * P].rearrange("p (n t) -> p n t", n=2),
                           ACT.Copy).then_inc(s["yc"], 1)
            for n in range(KT):
                act.wait_ge(gn[1], n + 1)
                av(Z[:, 26 + n % 2, :], T[:, n, :], ACT.Square).then_inc(gn[2], 1)
                act.wait_ge(gn[3], n + 1)
                av(PT[:, n % 2, :], ps[:, 4 * (n % 2) + 1, :], ACT.Sqrt, bias=par2("gn_eps"), scale=1.0 / HD).then_inc(gn[4], 1)
            copies(B_RWKV + C_RKV + C_LORA + C_G2, C_RWO, N, 0, t_ready)
            rms(8, N, t_ready, 4 + 24)
            tail(1)

        @block.vector
        def _(dve):
            v = nc.vector
            tt, ts, stt = v.tensor_tensor, v.tensor_scalar, v.scalar_tensor_tensor

            def layer_norm(l, i, gain):
                s, at = ln, l * 2 + i
                dve.wait_ge(s["mean"], at + 1)
                for n in range(KT):
                    tt(X[:, n, :], X[:, n, :], ps[:, 4, :], ALU.subtract).then_inc(s["xc"], 1)
                dve.wait_ge(s["std"], at + 1)
                v.reciprocal(RS[:], RS[:])
                dve.drain()
                for n in range(KT):
                    stt(X[:, n, :], X[:, n, :], par(gain, n, 1), RS[:], ALU.mult, ALU.mult).then_inc(s["y"], 1)

            def maxima(l, u):
                W = (UNITS[u][1] + 1) * P
                dve.wait_ge(at_sc, l * NU + u + 1)
                v.tensor_reduce(AM[:, u % 2, 0, :], ps[:, 0:4, 0:W], AXX, ALU.max)
                dve.drain()
                ts(AM[:, u % 2, 1, :], AM[:, u % 2, 0, :], -SCALE, None, ALU.mult).then_inc(at_max, 1)

            def factors(l, u):
                kind, qi, which = UNITS[u]
                W = (qi + 1) * P
                dve.wait_ge(at_exp, l * NU + u + 1)
                v.reciprocal(AM[:, u % 2, 3, :], AM[:, u % 2, 2, :])
                dve.drain()
                if kind == "diff":
                    ts(AM[:, u % 2, 3, 1:4:2], AM[:, u % 2, 3, 1:4:2], LAM[:, 2 * HD + 5:2 * HD + 6], None, ALU.mult)
                    dve.drain()
                    for i in range(2):
                        b = (u % 2) * 4 + 2 * i
                        ts(N[:, b + 1, 0:W], N[:, b + 1, 0:W], AM[:, u % 2, 3, 2 * i + 1:2 * i + 2], None, ALU.mult)
                    dve.drain()
                    for i in range(2):
                        b = (u % 2) * 4 + 2 * i
                        ins = stt(N[:, b, 0:W], N[:, b, 0:W], AM[:, u % 2, 3, 2 * i:2 * i + 1], N[:, b + 1, 0:W], ALU.mult, ALU.add)
                    ins.then_inc(at_comb, 1)
                else:
                    tt(AM[:, u % 2, 3, :], AM[:, u % 2, 3, :], GSIG[:, qi, 1 + kind, which * HPG:which * HPG + HPG], ALU.mult)

            def turned(l, u):
                W = (UNITS[u][1] + 1) * P
                for i in range(HEADS_OF[u]):
                    t = HEADS_BEFORE[u] + i
                    dve.wait_ge(at_tr, l * NHEADS + t + 1)
                    if t >= 4:
                        dve.wait_ge(at_av, l * NHEADS + t - 3)
                    v.tensor_copy(PT[:, t % 4, 0:W], ps[:, 4 + t % 2, 0:W]).then_inc(at_pt, 1)

            def outputs(l, u):
                kind, qi, which = UNITS[u]
                dve.wait_ge(at_av, l * NHEADS + HEADS_BEFORE[u + 1])
                if kind == "diff":
                    v.tensor_copy(YB[:, qi, 2 * which:2 * which + 2, :],
                                  ps[:, 6 + u % 2, 0:2 * P].rearrange("p (h d) -> p h d", h=2)).then_inc(at_out, 1)
                else:
                    o = RS[:, 0:HPG * HD].rearrange("p (h d) -> p h d", h=HPG)
                    tt(o, ps[:, 6 + u % 2, 0:HPG * HD].rearrange("p (h d) -> p h d", h=HPG),
                       AM[:, u % 2, 3, :].unsqueeze(2).to_broadcast([P, HPG, HD]), ALU.mult)
                    dve.drain()
                    y = YC[:, qi, which * HPG:which * HPG + HPG, :]
                    tt(y, y, o, ALU.add).then_inc(at_out, 1)

            dve.wait_ge(cst_in, 16)
            with dve.Fori(0, DEPTH) as l:
                C = l * CPL
                dve.wait_ge(par_in, l * 16 + 16)
                lam4 = par("lam").rearrange("p (a b d) -> p a b d", a=2, b=2)
                tt(LAM[:, 0:2 * HD].rearrange("p (a d) -> p a d", a=2), lam4[:, :, 0, :], lam4[:, :, 1, :], ALU.mult)
                dve.drain()
                v.tensor_reduce(LAM[:, 2 * HD:2 * HD + 2], LAM[:, 0:2 * HD].rearrange("p (a d) -> p a d", a=2), AXX, ALU.add).then_inc(lam_d, 1)
                ts(LAM[:, 2 * HD + 6:2 * HD + 7], par("subln"), par("lam_keep"), None, ALU.mult)
                for r, t in enumerate(ROPE_TILES):
                    dve.wait_ge(rot, l * NR + r + 1)
                    tt(T[:, 4 + r % 2, :], ps[:, r % 4, :], cst("sin"), ALU.mult)
                    tt(Z[:, t, :], Z[:, t, :], cst("cos"), ALU.mult)
                    dve.drain()
                    tt(Z[:, t, :], Z[:, t, :], T[:, 4 + r % 2, :], ALU.add).then_inc(rope, 1)
                    if t == Z_KC:
                        dve.drain()
                        for kv in range(2):
                            for half in range(2):
                                p0 = PCOL["pos"][0] + kv * CMP_BLOCK + half * CMP_STRIDE
                                tt(T[:, 2 * kv + half, :].rearrange("p (n s) -> p n s", s=CMP_STRIDE),
                                   Z[:, Z_KC + kv, :].rearrange("p (n s) -> p n s", s=CMP_STRIDE),
                                   PAR[:, p0:p0 + CMP_STRIDE].unsqueeze(1).to_broadcast([P, S // CMP_STRIDE, CMP_STRIDE]),
                                   ALU.add).then_inc(cmpin, 1)
                dve.drain()
                for c in range(4):
                    tt(T[:, 4 + c, :], Z[:, Z_AC + c, :], Z[:, Z_AV + c, :], ALU.mult)
                dve.drain()
                for c in range(4):
                    ts(Y[:, c, :], T[:, 4 + c, :], par("conv_a", 8 + c, 1), None, ALU.mult)
                for k in (1, 0):
                    dve.drain()
                    for c in range(4):
                        y = Y[:, c, 2 - k:S]
                        stt(y, T[:, 4 + c, 0:S - 2 + k], par("conv_a", 4 * k + c, 1), y, ALU.mult, ALU.add)
                dve.drain()
                for c in range(4):
                    tt(Y[:, c, :], Y[:, c, :], Z[:, Z_AB + c, :], ALU.mult).then_inc(conv_out, 1)
                dve.wait_ge(phio, l + 1)
                for g in range(NG):
                    o = g * HD
                    v.tensor_copy(KCC[o:o + HD, 0:NCMP], ps[o:o + HD, 4, g * 32:g * 32 + NCMP])
                v.tensor_copy(VCC[0:NCMP, :, :], ps[0:NCMP, 5, 0:NG * HD].rearrange("p (g d) -> p g d", g=NG)).then_inc(cmpkv, 1)
                dve.wait_ge(lam_e, l + 1)
                tt(LAM[:, 2 * HD + 4:2 * HD + 5], LAM[:, 2 * HD + 3:2 * HD + 4], LAM[:, 2 * HD + 2:2 * HD + 3], ALU.subtract)
                dve.drain()
                tt(LAM[:, 2 * HD + 5:2 * HD + 6], LAM[:, 2 * HD + 4:2 * HD + 5], par("lam_init"), ALU.subtract)
                dve.wait_ge(cs_mm, l + 1)
                cm = cst("cmask").rearrange("p (t n) -> p t n", t=ST)
                cv = cst("cvalid").rearrange("p (t n) -> p t n", t=ST)
                for qi in range(ST):
                    for g in range(NG):
                        tt(CS[:, qi, g * HPG:g * HPG + HPG, :],
                           ps[:, g, qi * P:qi * P + P].rearrange("p (h n) -> p h n", h=HPG)[:, :, 0:NCMP],
                           cm[:, qi].unsqueeze(1).to_broadcast([P, HPG, NCMP]), ALU.add)
                dve.drain()
                csf = CS[:].rearrange("p t h n -> p (t h) n")
                v.tensor_reduce(CM[:, 0, :], csf, AXX, ALU.max)
                dve.drain()
                tt(csf, csf, CM[:, 0, :].unsqueeze(2).to_broadcast([P, ST * NH, NCMP]), ALU.subtract).then_inc(cs_sub, 1)
                dve.wait_ge(cs_exp, l + 1)
                v.tensor_reduce(CM[:, 1, :], csf, AXX, ALU.add)
                dve.drain()
                for qi in range(ST):
                    ins = tt(CS[:, qi], CS[:, qi], cv[:, qi].unsqueeze(1).to_broadcast([P, NH, NCMP]), ALU.mult)
                ins.then_inc(cs_p, 1)
                v.reciprocal(CM[:, 2, :], CM[:, 1, :])
                dve.drain()
                dve.wait_ge(gsig, l + 1)
                tt(CM[:, 3, :].rearrange("p (t h) -> p t h", t=ST), CM[:, 2, :].rearrange("p (t h) -> p t h", t=ST), GSIG[:, :, 0, :], ALU.mult)
                dve.drain()
                for qi in range(ST):
                    dve.wait_ge(cs_av, l * ST + qi + 1)
                    tt(YC[:, qi], ps[:, qi % 2, :].rearrange("p (h d) -> p h d", h=NH),
                       CM[:, 3, qi * NH:qi * NH + NH].unsqueeze(2).to_broadcast([P, NH, HD]), ALU.mult).then_inc(cs_out, 1)
                dve.drain()
                maxima(l, 0)
                for u in range(NU):
                    factors(l, u)
                    if u + 1 < NU:
                        maxima(l, u + 1)
                    turned(l, u)
                    outputs(l, u)
                dve.wait_ge(yb_sq, l + 1)
                v.tensor_reduce(MS[:, 0, :], T[:, 0:4, :].rearrange("p t (h d) -> p (t h) d", h=DH), AXX, ALU.add).then_inc(yb_ms, 1)
                dve.wait_ge(yb_rt, l + 1)
                v.reciprocal(MS[:, 1, :], MS[:, 1, :])
                dve.drain()
                ybf = YB[:].rearrange("p t h d -> p (t h) d")
                tt(ybf, ybf, MS[:, 1, :].unsqueeze(2).to_broadcast([P, ST * DH, P]), ALU.mult).then_inc(yb_fin, 1)
                with dve.Fori(0, 3) as b:
                    dve.wait_ge(nzero, l + 1)
                    for n in range(KT):
                        dve.wait_ge(sg, l * 24 + b * 8 + (n + 5))
                        dve.wait_ge(used, C + B_MERGE + b * 12 + 3 * (n // 2) + 3)
                        tt(T[:, 4 + n % 4, :], T[:, n % 4, :], ps[:, 4 + n % 4, :], ALU.mult)
                        dve.drain()
                        tt(N[:, n, :], N[:, n, :], T[:, 4 + n % 4, :], ALU.add).then_inc(mg, 1)
                with dve.Fori(0, 2) as i:
                    for j in range(RING):
                        dve.wait_ge(used, C + B_WO + i * RING + (j + 1))
                        x = X[:, bass.ds(i * RING + j, 1), :]
                        stt(x, x, ALPHA, ps[:, j:j + 1, :], ALU.mult, ALU.add).then_inc(x1pre, 1)
                dve.drain()
                layer_norm(l, 0, "ln1_g")
                with dve.Fori(0, C_UP // RING) as i:
                    for e in range(2):
                        for b in range(2):
                            j = 2 * e + b
                            dve.wait_ge(up_a, l * C_UP + i * RING + (j + 1))
                            f = i * 2 + (e + b * FT)
                            for k in (1, 0):
                                y = T[:, j, 2 - k:S]
                                ins = stt(y, ps[:, j, 0:S - 2 + k], PAR[:, bass.ds(f + (PCOL["up_w"][0] + k * 2 * FT), 1)], y, ALU.mult, ALU.add)
                                if k:
                                    dve.drain()
                            ins.then_inc(up_c, 1)
                        dve.drain()
                        dve.wait_ge(up_g, l * FT + i * 2 + (e + 1))
                        tt(Z[:, bass.ds(i * 2 + e, 1), :], T[:, 4 + e:5 + e, :], T[:, 2 * e + 1:2 * e + 2, :], ALU.mult).then_inc(up_h, 1)
                with dve.Fori(0, 2) as i:
                    for n in range(4):
                        dve.wait_ge(used, C + B_DOWN + i * 12 + 3 * (n + 1))
                        x = X[:, bass.ds(i * 4 + n, 1), :]
                        stt(x, x, ALPHA, ps[:, n:n + 1, :], ALU.mult, ALU.add).then_inc(x2pre, 1)
                dve.drain()
                layer_norm(l, 1, "ln2_g")

            def inverse_root(i, cols=S):
                dve.wait_ge(rms_std, i + 1)
                v.reciprocal(RS[:, 0:cols], RS[:, 0:cols])
                dve.drain()

            def rms(i, src, dst, gain, cols=S):
                inverse_root(i, cols)
                for n in range(KT):
                    stt(dst[:, n, :], src[:, n, :], gain[:, n:n + 1], RS[:, 0:cols], ALU.mult, ALU.mult).then_inc(rms_y, 1)

            def residual(i, gain):
                inverse_root(i)
                for n in range(KT):
                    stt(T[:, n, :], N[:, n, :], gain[:, n:n + 1], RS[:], ALU.mult, ALU.mult)
                dve.drain()
                for n in range(KT):
                    tt(X[:, n, :], X[:, n, :], T[:, n, :], ALU.add).then_inc(xr2, 1)
                dve.drain()

            def gain(l, i):
                return par2("ln", (l * 6 + i) * KT, KT)

            def tail(l):
                rms(3 + 6 * l, X, N, gain(l, 2))

                def maxima2(qi):
                    dve.wait_ge(m_sc, l * ST + qi + 1)
                    v.tensor_reduce(AM[:, qi % 2, 0, :], ps[:, 2 * (qi % 2):2 * (qi % 2) + 2, :].rearrange("p b (h s) -> p (b h) s", h=2),
                                    AXX, ALU.max)
                    dve.drain()
                    ts(AM[:, qi % 2, 1, :], AM[:, qi % 2, 0, :], -((MT * P) ** -0.5), None, ALU.mult).then_inc(m_max, 1)

                maxima2(0)
                for qi in range(ST):
                    if qi + 1 < ST:
                        maxima2(qi + 1)
                    dve.wait_ge(m_exp, l * ST + qi + 1)
                    v.reciprocal(AM[:, qi % 2, 3, :], AM[:, qi % 2, 2, :])
                    dve.drain()
                    p = MP[:, qi % 2]
                    tt(p, p, AM[:, qi % 2, 3, :].unsqueeze(2).to_broadcast([P, MH, S2]), ALU.mult).then_inc(m_p, 1)
                residual(4 + 6 * l, gain(l, 3))
                rms(5 + 6 * l, X, N, gain(l, 4))
                with dve.Fori(0, 28 // RING) as i:
                    for j in range(RING):
                        dve.wait_ge(mup_r, i * RING + (l * F2T + j + 1))
                        t = T[:, j:j + 1, :]
                        tt(Z[:, bass.ds(i * RING + j, 1), :], t, t, ALU.mult).then_inc(mup, 1)
                for j in range(F2T - 28):
                    dve.wait_ge(mup_r, l * F2T + 28 + j + 1)
                    tt(Y[:, j, :], T[:, j, :], T[:, j, :], ALU.mult).then_inc(mup, 1)
                residual(6 + 6 * l, gain(l, 5))

            dve.drain()
            dve.wait_ge(par2_in, 16)
            rms(0, MN, MN, par2("mem_norm"), S2)
            rms(1, X, N, gain(0, 0))
            for n0 in (0, 4):
                dve.wait_ge(lru_in, 4 + KT + n0 + 4)
                for n in range(n0, n0 + 4):
                    ts(Z[:, 16 + n, :], Z[:, 8 + n, :], par2("conv_w", 3 * KT + n, 1), par2("conv_b", n, 1), ALU.mult, ALU.add)
                for k in (2, 1, 0):
                    dve.drain()
                    for n in range(n0, n0 + 4):
                        y = Z[:, 16 + n, 3 - k:S]
                        ins = stt(y, Z[:, 8 + n, 0:S - 3 + k], par2("conv_w", k * KT + n, 1), y, ALU.mult, ALU.add)
                        if k == 0:
                            ins.then_inc(lru_conv, 1)
            dve.drain()
            lam = par2("lam")
            ts(LRU[:, 2, :], lam, -1.0, None, ALU.mult)
            dve.drain()
            tt(LRU[:, 0, :], lam, LRU[:, 2, :], ALU.max).then_inc(lru_rate[0], 1)
            dve.wait_ge(lru_rate[1], 1)
            e, u, d, low = LRU[:, 1, :], LRU[:, 2, :], LRU[:, 0, :], LAM[:, 0:KT]
            ts(u, e, 1.0, None, ALU.add).then_inc(lru_rate[2], 1)
            dve.drain()
            ts(d, u, -1.0, 1e-30, ALU.add, ALU.max)
            ts(low, e, -0.5, 1.0, ALU.mult, ALU.add)
            dve.drain()
            v.reciprocal(d, d)
            tt(low, low, e, ALU.mult)
            dve.drain()
            tt(d, d, e, ALU.mult)
            dve.wait_ge(lru_rate[3], 1)
            dve.drain()
            tt(d, d, LRU[:, 3, :], ALU.mult)
            ts(u, lam, -1.0, 0.0, ALU.mult, ALU.max)
            dve.drain()
            tt(d, d, low, ALU.max)
            dve.drain()
            tt(d, d, u, ALU.add)
            dve.drain()
            ts(LRU[:, 2, :], d, LRU_C, None, ALU.mult)
            ts(LRU[:, 3, :], d, -LRU_C, None, ALU.mult).then_inc(lru_rate[4], 1)
            dve.drain()
            dve.wait_ge(lru_gate, 16)
            for n in range(KT):
                tt(T[:, n, :], T[:, n, :], Z[:, 16 + n, :], ALU.mult)
            for n0 in (0, 4):
                dve.drain()
                for n in range(n0, n0 + 4):
                    dve.wait_ge(lru_ea, 2 * n + 1)
                    ts(Z[:, 24 + n % 4, :], Z[:, 8 + n, :], 1.0, None, ALU.add)
                dve.drain()
                for n in range(n0, n0 + 4):
                    v.reciprocal(Z[:, 24 + n % 4, :], Z[:, 24 + n % 4, :])
                dve.drain()
                for n in range(n0, n0 + 4):
                    tt(Z[:, 8 + n, :], Z[:, 8 + n, :], Z[:, 24 + n % 4, :], ALU.mult).then_inc(lru_q, 1)
            for n0 in (0, 4):
                dve.drain()
                for n in range(n0, n0 + 4):
                    dve.wait_ge(lru_m, n + 1)
                    tt(T[:, n, :], T[:, n, :], Z[:, 8 + n, :], ALU.mult)
                dve.drain()
                for n in range(n0, n0 + 4):
                    v.tensor_tensor_scan(Z[:, 16 + n, :], Y[:, n, :], T[:, n, :], 0.0, ALU.mult, ALU.add)
                dve.drain()
                for n in range(n0, n0 + 4):
                    tt(Z[:, 16 + n, :], Z[:, 16 + n, :], Z[:, n, :], ALU.mult).then_inc(lru_y, 1)
            residual(2, gain(0, 1))
            tail(0)

            v.memset(STATE, 0.0)
            rms(7, X, N, gain(1, 0))
            dve.drain()
            tt(Y[:, 0:KT, 1:S], N[:, :, 0:S - 1], N[:, :, 1:S], ALU.subtract)
            ts(Y[:, 0:KT, 0:1], N[:, :, 0:1], -1.0, None, ALU.mult)
            dve.drain()
            for m, mu in enumerate((0, 2, 3, 1, 4, 5)):
                if 2 <= m < 5:
                    dve.wait_ge(used, B_RWKV + (m - 1) * KT)
                elif m == 5:
                    dve.wait_ge(lora, 1)
                for n in range(KT):
                    stt(MIX[m % 2][n], Y[:, n, :], par2("mu", mu * KT + n, 1), N[:, n, :], ALU.mult, ALU.add).then_inc(mix, 1)
            dve.wait_ge(cst2_in, 16)
            for n in range(KT):
                dve.wait_ge(lw, n + 1)
                t = YCF[:, 2 + n % 2, :]
                v.tensor_tensor_scan(t, cst2("reset"), N[:, n, :], 0.0, ALU.mult, ALU.add)
                dve.drain()
                t4 = t.rearrange("p (c t) -> p c t", c=RC)
                v.tensor_copy(MID[:, 0:2, n, :], t4[:, :, P // 2 - 1].unsqueeze(1).to_broadcast([P, 2, RC]))
                tt(MID[:, 2, n, :], t4[:, :, P - 1], t4[:, :, P // 2 - 1], ALU.subtract)
                tt(N[:, n, :].rearrange("p (c t) -> p c t", c=RC), t4, t4[:, :, P // 2 - 1:P // 2].to_broadcast([P, RC, P]),
                   ALU.subtract).then_inc(cum, 1)
            for n in range(KT):
                dve.wait_ge(kk_s[3], n + 1)
                dve.wait_ge(la, 3 + n + 1)
                r = Z[:, 26 + n % 2, :]
                ts(r, r, 1e-12, None, ALU.max)
                ts(YCF[:, n % 2, :], T[:, n, :], 1.0, par2("k_a", n, 1), ALU.subtract, ALU.mult)
                dve.drain()
                v.reciprocal(r, r)
                stt(Z[:, 8 + n, :], YCF[:, n % 2, :], 1.0, Z[:, 8 + n, :], ALU.add, ALU.mult)
                dve.drain()
                tt(Y[:, n, :], Y[:, n, :], r, ALU.mult)
                dve.drain()
                tt(T[:, n, :], T[:, n, :], Y[:, n, :], ALU.mult).then_inc(kk_s[4], 1)
            dve.wait_ge(mid_e, 1)
            dve.drain()
            pair = cst2("pair").rearrange("p (a t) -> p a t", a=2).unsqueeze(1).to_broadcast([P, 2, 2, P])
            ident4 = cst("ident").unsqueeze(1).to_broadcast([P, 4, P])

            def level(i):
                return cst2("levels", i * P, P).unsqueeze(1).to_broadcast([P, 4, P])

            with dve.Fori(0, RC) as c:
                for half in range(2):
                    def lane(L):
                        return ch[L], LANES[L], 4 * L, 2 * (2 * half + L), c * 2 + half

                    for L in range(2):
                        s, B, o, n0, it = lane(L)
                        dve.wait_ge(s["exp"], it + 1)
                        e, tsl = B["e"], bass.ds(c * P, P)
                        stt(B["ar"][:, :, 0, :], Y[:, n0:n0 + 2, tsl], -1.0, e[:, :, 0, 0:P], ALU.mult, ALU.mult)
                        tt(B["ar"][:, :, 1, :], Z[:, n0:n0 + 2, tsl], e[:, :, 0, 1:P + 1], ALU.mult)
                        tt(B["bk"][:, 0], T[:, n0:n0 + 2, tsl], e[:, :, 1, 0:P], ALU.mult)
                        tt(B["sh"], STATE[:, n0:n0 + 2, :], MID[:, 1, n0:n0 + 2, bass.ds(c, 1)].to_broadcast([P, 2, HD]), ALU.mult)
                        tt(B["bk"][:, 1], Z[:, 8 + n0:10 + n0, tsl], e[:, :, 1, 0:P], ALU.mult).then_inc(s["hat"], 1)
                    for L in range(2):
                        s, B, o, n0, it = lane(L)
                        dve.wait_ge(s["g1"], it + 1)
                        for r in range(2):
                            tt(B["g1"][:, r:4:2], ps[:, o + 2 + r, :].rearrange("p (n a t) -> p n a t", n=2, a=2), pair, ALU.mult)
                        dve.drain()
                        tt(B["g1"][:, :, 0, :], B["g1"][:, :, 0, :], ident4, ALU.add)
                        dve.drain()
                        tt(B["xt"], B["g1"][:, :, 0, :], level(0), ALU.mult).then_inc(s["x0t"], 1)
                    for L in range(2):
                        s, B, o, n0, it = lane(L)
                        dve.wait_ge(s["g2"], it + 1)
                        for r in range(2):
                            ins = tt(B["g2"][:, r:4:2], ps[:, o + r, :].rearrange("p (n a t) -> p n a t", n=2, a=2), pair, ALU.mult)
                        ins.then_inc(s["g2m"], 1)
                    for k in range(LEVELS):
                        for L in range(2):
                            s, B, o, n0, it = lane(L)
                            dve.wait_ge(s["z"], it * LEVELS + k + 1)
                            tt(B["z"], ps[:, o, :].rearrange("p (q t) -> p q t", q=4), level(k + 1), ALU.mult).then_inc(s["zm"], 1)
                    for L in range(2):
                        s, B, o, n0, it = lane(L)
                        dve.wait_ge(s["s"], it + 2)
                        for r in (0, HD):
                            tt(STATE[r:r + HD, n0:n0 + 2, :], ps[r:r + HD, o, 0:2 * P].rearrange("p (n i) -> p n i", n=2)[:, :, r:r + HD],
                               B["sh"][r:r + HD], ALU.add)
                        dve.drain()
                        st = STATE[:, n0:n0 + 2, :]
                        tt(st, st, MID[:, 2, n0:n0 + 2, bass.ds(c, 1)].to_broadcast([P, 2, HD]), ALU.mult).then_inc(s["sc"], 1)
                    dve.drain()
            for n in range(KT):
                o = 4 * (n % 2)
                dve.wait_ge(gn[0], n + 1)
                stt(T[:, n, :], ps[:, o, :], -1.0 / HD, T[:, n, :], ALU.mult, ALU.add).then_inc(gn[1], 1)
                if n >= 2:
                    dve.wait_ge(gn[7], n - 1)
                stt(Z[:, 24 + n % 2, :], Z[:, n, :], par2("r_k", n, 1), Z[:, 8 + n, :], ALU.mult, ALU.mult).then_inc(gn[5], 1)
                dve.wait_ge(gn[7], n + 1)
                tt(PT[:, 2 + n % 2, :], Z[:, 16 + n, :], ps[:, o + 2, :], ALU.mult)
                dve.wait_ge(gn[4], n + 1)
                v.reciprocal(PT[:, n % 2, :], PT[:, n % 2, :])
                dve.drain()
                stt(T[:, n, :], T[:, n, :], par2("gn_g", n, 1), PT[:, n % 2, :], ALU.mult, ALU.mult)
                dve.drain()
                stt(T[:, n, :], T[:, n, :], par2("gn_b", n, 1), PT[:, 2 + n % 2, :], ALU.add, ALU.add)
                dve.drain()
                dve.wait_ge(gn[8], n + 1)
                tt(Y[:, n, :], T[:, n, :], ps[:, o + 3, :], ALU.mult).then_inc(gn[9], 1)
            residual(8, gain(1, 1))
            tail(1)

        @block.gpsimd
        def _(pool):
            with pool.Fori(0, DEPTH) as l:
                pool.wait_ge(at_av, l * NHEADS + NHEADS)
                pool.sem_inc(nfree, 1)
                nc.gpsimd.memset(N[:], 0.0).then_inc(nzero, 1)


def _tiles(w):
    k, n = w.shape
    return w.reshape(k // P, P, n // P, P).transpose(2, 1, 0, 3)


def _blocks(w, nk):
    t = _tiles(w)
    t = np.concatenate([t, np.zeros((t.shape[0], P, nk - t.shape[2], P), w.dtype)], axis=2) if nk > t.shape[2] else t
    return t.reshape(t.shape[0], P, nk * P)


def _rows(w):
    k, n = w.shape
    full = np.zeros((k, 512), w.dtype)
    full[:, :n] = w
    return full.reshape(k // 256, 2, P, 512).transpose(0, 2, 1, 3).reshape(k // 256, P, CHUNK)


def _chunks(t):
    return t.reshape(-1, P, CHUNK) if t.shape[2] == CHUNK else \
        t.reshape(t.shape[0], P, t.shape[2] // CHUNK, CHUNK).transpose(0, 2, 1, 3).reshape(-1, P, CHUNK)


def _cols(v):
    return v.reshape(-1, P).T


def first_weights(i, l):
    w = i["w_in"][l]
    col = lambda s, n: w[:, s:s + n]
    q = col(3072, 512).reshape(D, NG, HPG, HD).transpose(0, 2, 1, 3).reshape(D, 512)
    kv = col(3584, 768).reshape(D, 6, P)
    g = col(4352, 24).reshape(D, NH, 3).transpose(0, 2, 1).reshape(D, 24)
    zw = np.concatenate([col(0, 1536), col(1536, 1024), q, kv[:, 0], kv[:, 1], kv[:, 2], kv[:, 4]], axis=1)
    out = [_chunks(_blocks(zw, KT)), _rows(col(2560, 512)), _rows(np.concatenate([kv[:, 3], kv[:, 5], g], axis=1))]
    phi = i["nsa_phi_w1"][l].reshape(2, 4, 8, HD, P).transpose(0, 1, 3, 2, 4).reshape(8, HD, CHUNK)
    out.append(np.concatenate([phi, phi], axis=1))
    for b in range(3):
        gates = _blocks(col(4376 + b * D, D), KT)
        br = _tiles(i["w_branch"][l][b]).reshape(4, 2, P, 4 * P).transpose(0, 2, 1, 3).reshape(4, P, CHUNK)
        for p in range(4):
            out += [gates[2 * p:2 * p + 2], br[p:p + 1]]
    out.append(_blocks(i["w_o"][l], KT))
    up = _blocks(i["ffn_w_up"][l], KT)
    out.append(up.reshape(2, FT, P, CHUNK).transpose(1, 0, 2, 3).reshape(2 * FT, P, CHUNK))
    out.append(_chunks(_blocks(i["ffn_w_down"][l], 24)))
    return np.concatenate(out)


def first_params(i, l):
    lam_init = 0.8 - 0.6 * math.exp(-0.3 * l)
    f = np.float32
    part = {
        "conv_a": _cols(i["conv_a_w"][l]), "subln": _cols(i["diff_subln"][l]),
        "ln1_g": _cols(i["ln1_g"][l]), "ln1_b": _cols(i["ln1_b"][l]),
        "ln2_g": _cols(i["ln2_g"][l]), "ln2_b": _cols(i["ln2_b"][l]),
        "up_w": _cols(i["ffn_conv_w"][l]), "up_b": _cols(i["ffn_conv_b"][l]),
        "pos": np.tile(i["nsa_cmp_pos"][l].transpose(2, 0, 1).reshape(HD, 2 * CMP_BLOCK), (2, 1)),
        "phi_w2k": np.tile(i["nsa_phi_w2"][l][0], (1, 2)), "phi_w2v": i["nsa_phi_w2"][l][1],
        "lam": np.tile(i["diff_lambda"][l].reshape(1, 4 * HD), (P, 1)),
        "lam_init": np.full((P, 1), lam_init, f), "lam_keep": np.full((P, 1), 1.0 - lam_init, f),
    }
    return np.concatenate([part[n] for n in PCOL], axis=1)


def second_weights(i):
    lin = lambda w: _chunks(_blocks(w, KT))
    zeros = lambda n: np.zeros((n, P, CHUNK), np.float32)

    def rows(w):
        return [_rows(w[:, h * 512:h * 512 + 512]) for h in range(2)]

    def tail(l):
        kv = i["c_w_kv_2"][l]
        return [lin(i["c_w_q_2"][l]), lin(kv[:, :D]), *rows(kv[:, D:]), lin(i["c_w_o_2"][l]),
                lin(i["m_w_up_2"][l]), _chunks(_blocks(i["m_w_down_2"][l], F2T))]

    gate = i["a_gate_w_2"][0].reshape(2, 2, 2, 2, P, 2, P).transpose(0, 1, 4, 2, 5, 3, 6).reshape(4, P, CHUNK)
    out = [lin(i["a_w_in_2"][0]), gate, lin(i["a_w_out_2"][0]), *tail(0)]
    out += [lin(i["b_w_rkv_2"][0][m]) for m in range(3)]
    thin = lambda w: w.reshape(KT, P, HD).transpose(1, 0, 2).reshape(P, KT * HD)
    tall = lambda w: np.concatenate([w, np.zeros((P - HD, D), w.dtype)])
    out.append(np.concatenate([thin(i["b_w1_2"][0]), thin(i["b_a1_2"][0])], axis=1)[None])
    out += [lin(i["b_g1_2"][0]), tall(i["b_w2_2"][0])[None], tall(i["b_a2_2"][0])[None], i["b_g2_2"][0][None], zeros(3)]
    return np.concatenate(out + [lin(i["b_w_o_2"][0]), *tail(1)])


def second_params(i):
    f = np.float32
    part = {
        "ln": _cols(i["ln_gains_2"]), "mem_norm": _cols(i["mem_norm_2"]), "conv_w": _cols(i["a_conv_w_2"]),
        "conv_b": _cols(i["a_conv_b_2"]), "b_in": _cols(i["a_b_in_2"]), "gate_b": _cols(i["a_gate_b_2"]),
        "lam": _cols(i["a_lambda_2"]), "b_out": _cols(i["a_b_out_2"]), "mu": _cols(i["b_mu_2"]),
        "w0": _cols(i["b_w0_2"]), "a0": _cols(i["b_a0_2"]), "k_k": _cols(i["b_k_k_2"]), "k_a": _cols(i["b_k_a_2"]),
        "r_k": _cols(i["b_r_k_2"]), "gn_g": _cols(i["b_gn_g_2"]), "gn_b": _cols(i["b_gn_b_2"]),
        "rms_eps": np.full((P, 1), RMS_EPS, f), "gn_eps": np.full((P, 1), GN_EPS, f),
    }
    return np.concatenate([part[n] for n in P2COL], axis=1)


def second_constants():
    f = np.float32
    k = np.arange(P)
    r, c = k[:, None], k[None, :]
    pair = np.concatenate([(r < c), (r <= c)], axis=1)
    eye = r == c
    levels = [(r // 2 == c // 2) & (r < c) | eye]
    for v in range(1, LEVELS + 1):
        b = 1 << v
        levels.append((r // (2 * b) == c // (2 * b)) & (r // b > c // b) | eye)
    part = {
        "pair": pair, "levels": np.concatenate(levels, axis=1), "reset": np.tile((np.arange(S) % P != 0)[None], (P, 1)),
        "ones": r // HD == c // HD,
    }
    return np.concatenate([part[n] for n in C2COL], axis=1).astype(f)


def constants():
    f = np.float32
    pos = np.arange(S, dtype=f)
    inv = (np.float32(500000.0) ** (-np.arange(0, 16, 2, dtype=f) / f(16))).astype(f)
    ang = (pos[:, None] * inv[None, :]).astype(f)
    cos, sin = np.ones((P, S), f), np.zeros((P, S), f)
    rot = np.zeros((P, P), f)
    for h in range(2):
        for d in range(8):
            a0, a1 = h * HD + d, h * HD + 8 + d
            cos[a0], cos[a1] = np.cos(ang[:, d]), np.cos(ang[:, d])
            sin[a0], sin[a1] = np.sin(ang[:, d]), np.sin(ang[:, d])
            rot[a1, a0], rot[a0, a1] = -1.0, 1.0
    t = np.arange(S).reshape(ST, P).T[:, :, None]
    valid = (np.arange(NCMP) * CMP_STRIDE + CMP_BLOCK - 1)[None, None, :] <= t
    k = np.arange(P)
    part = {
        "ident": np.eye(P, dtype=f), "rot": rot, "maskneg": np.where(k[None, :] > k[:, None], f(NEG), f(0)),
        "mean": np.full((P, P), 1.0 / D, f), "cmask": np.where(valid, f(0), f(NEG)).reshape(P, -1),
        "cvalid": valid.astype(f).reshape(P, -1), "cos": cos, "sin": sin, "eps": np.full((P, 1), LN_EPS, f),
    }
    return np.concatenate([part[n] for n in CCOL], axis=1).astype(f)


def kernel(**inputs):
    import concourse.bacc as bacc
    from concourse.bass_utils import run_bass_kernel_spmd

    i = {k: np.asarray(v) for k, v in inputs.items()}
    nc = bacc.Bacc("TRN2", target_bir_lowering=False, num_devices=1)
    arrays = {
        "x": i["x"][0].T.reshape(KT, P, S).transpose(1, 0, 2),
        "weights": np.concatenate([first_weights(i, l) for l in range(DEPTH)] + [second_weights(i)]),
        "par": np.stack([first_params(i, l) for l in range(DEPTH)]),
        "cst": constants(), "par2": second_params(i), "cst2": second_constants(),
        "mem": i["mem_2"][0].T.reshape(KT, P, S2).transpose(1, 0, 2),
    }
    arrays = {k: np.ascontiguousarray(v) for k, v in arrays.items()}
    aps = {k: nc.dram_tensor(f"in_{k}", v.shape, F32, kind="ExternalInput").ap() for k, v in arrays.items()}
    out = nc.dram_tensor("out_x", (P, KT, S), F32, kind="ExternalOutput").ap()
    build(nc, aps, out)
    r = run_bass_kernel_spmd(nc, [{f"in_{k}": v for k, v in arrays.items()}], core_ids=[0])
    return np.ascontiguousarray(r.results[0]["out_x"].transpose(1, 0, 2).reshape(D, S).T)[None]
```

```python
import concourse.bass as bass
from concourse import mybir
from concourse.alu_op_type import AluOpType as ALU
from contextlib import ExitStack
import math
import numpy as np

F32 = mybir.dt.float32
F32R = mybir.dt.float32r
ACT = mybir.ActivationFunctionType
AXX = mybir.AxisListType.X

P = 128
S = 512
D = 1024
KT = D // P
ST = S // P
DEPTH = 2
HD = 64
DH = 4
NH = 8
NG = 2
HPG = NH // NG
CMP_BLOCK, CMP_STRIDE = 32, 16
NCMP = (S - CMP_BLOCK) // CMP_STRIDE + 1
DFF = 2816
FT = DFF // P
ALPHA = (2 * DEPTH) ** 0.25
LN_EPS = 1e-5
NEG = -1e30
SCALE = HD ** -0.5

RING = 4
CHUNK = 8 * P
C_Z, C_DV, C_VSG, C_PHI, C_MERGE, C_WO, C_UP, C_DOWN = 28, 4, 4, 8, 36, 8, 2 * FT, 24
B_Z = 0
B_DV = B_Z + C_Z
B_VSG = B_DV + C_DV
B_PHI = B_VSG + C_VSG
B_MERGE = B_PHI + C_PHI
B_WO = B_MERGE + C_MERGE
B_UP = B_WO + C_WO
B_DOWN = B_UP + C_UP
CPL = B_DOWN + C_DOWN

Z_AB, Z_AC, Z_AV, Z_DQ, Z_DK, Z_NQ, Z_KC, Z_VC, Z_KS, Z_KW = 0, 4, 8, 12, 16, 20, 24, 25, 26, 27
ROPE_TILES = list(range(Z_DQ, Z_KC + 1)) + [Z_KS, Z_KW]
NR = len(ROPE_TILES)
VSG_N = 2 * P + 3 * NH

PCOL = {}
_at = 0
for _name, _n in (("conv_a", 12), ("subln", 1), ("ln1_g", 8), ("ln1_b", 8), ("ln2_g", 8), ("ln2_b", 8),
                  ("up_w", 2 * FT * 3), ("up_b", 2 * FT), ("pos", 2 * CMP_BLOCK), ("phi_w2k", P), ("phi_w2v", HD),
                  ("lam", 4 * HD), ("lam_init", 1), ("lam_keep", 1)):
    PCOL[_name] = (_at, _n)
    _at += _n
NPAR = _at

CCOL = {}
_at = 0
for _name, _n in (("ident", P), ("rot", P), ("maskneg", P), ("mean", P), ("cmask", ST * NCMP),
                  ("cvalid", ST * NCMP), ("cos", S), ("sin", S), ("eps", 1)):
    CCOL[_name] = (_at, _n)
    _at += _n
NCST = _at

S2 = 256
MH, MT = 4, 2
F2T = 4 * KT
RMS_EPS, GN_EPS = 1e-6, 64e-5
LRU_C = 8.0
K0 = math.exp(-0.5)
RC = S // P
LEVELS = 6
C_LRU_IN, C_LRU_GATE, C_LRU_OUT = 16, 4, 8
C_RKV, C_LORA, C_G2, C_RWO = 24, 4, 4, 8
C_MQ, C_MK, C_MV, C_MO = 8, 8, 8, 8
HALF = F2T // 2
C_HUP, C_HDN = HALF, 2 * KT
B_MFF = C_MQ + C_MK + C_MV + C_MO
C_TAIL = B_MFF + 2 * (C_HUP + C_HDN)
B_LRU = DEPTH * CPL
B_TAIL0 = B_LRU + C_LRU_IN + C_LRU_GATE + C_LRU_OUT
B_RWKV = B_TAIL0 + C_TAIL
B_TAIL1 = B_RWKV + C_RKV + C_LORA + C_G2 + C_RWO
N_CHUNKS = B_TAIL1 + C_TAIL

SPLIT_RUNS = ((B_LRU, C_LRU_IN), (B_LRU + C_LRU_IN + C_LRU_GATE, C_LRU_OUT + C_TAIL),
              (B_TAIL1 - C_RWO, C_RWO + C_TAIL))
SPL = CPL - C_PHI


def n_split(c):
    if c < CPL:
        return c if c <= B_PHI else c - C_PHI
    return DEPTH * SPL + sum(min(max(c - b, 0), n) for b, n in SPLIT_RUNS)


SRC = {n: KT * i for i, n in enumerate(("lru_in", "lru_out", "q0", "o0", "up0", "rwo", "q1", "o1", "up1"))}

P2COL = {}
_at = 0
for _name, _n in (("ln", 2 * 6 * KT), ("mem_norm", KT), ("conv_w", 4 * KT), ("conv_b", KT), ("b_in", 2 * KT),
                  ("gate_b", 2 * KT), ("lam", KT), ("b_out", KT), ("mu", 6 * KT), ("w0", KT), ("a0", KT), ("k_k", KT),
                  ("k_a", KT), ("r_k", KT), ("gn_g", KT), ("gn_b", KT), ("rms_eps", 1), ("gn_eps", 1)):
    P2COL[_name] = (_at, _n)
    _at += _n
NPAR2 = _at

C2COL = {}
_at = 0
for _name, _n in (("pair", 2 * P), ("levels", (LEVELS + 1) * P), ("reset", S), ("ones", P)):
    C2COL[_name] = (_at, _n)
    _at += _n
NCST2 = _at

UNITS = [("diff", qi, hp) for qi in range(ST) for hp in range(DH // 2)] + \
        [(b, qi, g) for b in (0, 1) for qi in range(ST) for g in range(NG)]
NU = len(UNITS)
HEADS_OF = [2 if kind == "diff" else 4 for kind, _, _ in UNITS]
HEADS_BEFORE = [sum(HEADS_OF[:u]) for u in range(NU + 1)]
NHEADS = HEADS_BEFORE[NU]


def build(nc, a, out, stop=None):
    ctx = ExitStack()
    with ctx:
        def sb(name, shape, dt=F32):
            return ctx.enter_context(nc.sbuf_tensor(name, shape, dt))

        def sem(name):
            return ctx.enter_context(nc.semaphore(name))

        ps = ctx.enter_context(nc.psum_tensor("ps", [P, 8, 512], F32))

        def both(name, shape):
            base = -(-nc.sbuf_base // 32) * 32
            whole = sb(name, shape)
            return whole, nc.alloc_sbuf_tensor_at(name + "_r", shape, F32R, offset=base)

        ARENA = 73
        arena_base = -(-nc.sbuf_base // 32) * 32
        sb("arena", [P, ARENA, S])

        def over(name, first, n, dt=F32):
            return nc.alloc_sbuf_tensor_at(name, [P, n, S], dt, offset=arena_base + first * S * 4)[:]

        ring, RL = both("ring", [P, RING, CHUNK])
        RHF, RH = both("rounded", [P, RING, CHUNK])
        X, XL = over("X", 0, KT), over("X_lo", 0, KT, F32R)
        AH = over("source_hi", 8, KT, F32R)
        XH, XHF = AH, AH.bitcast(F32)
        Z = over("Z", 16, 28)
        PROB, PT = Z[:, 0:8, :], Z[:, 8:12, :]
        Y, YL = over("Y", 44, 12), over("Y_lo", 44, 12, F32R)
        SCR = Y[:, 4:12, :]
        YB = over("YB", 56, ST).rearrange("p t (h d) -> p t h d", h=DH)
        YC = over("YC", 60, ST).rearrange("p t (h d) -> p t h d", h=NH)
        DV = over("DV", 64, ST)
        YH = over("Y_hi", 16, 12, F32R)
        YHF = YH.bitcast(F32)
        M, ML = over("M", 28, KT), over("M_lo", 28, KT, F32R)
        MR = over("M_hi", 44, KT, F32R)
        MRF = MR.bitcast(F32)
        T1 = over("T1", 60, KT)
        FH, FL, FHR = over("F", 16, FT), over("F_lo", 16, FT, F32R), over("F_hi", 16 + FT, FT, F32R)
        FHRF = FHR.bitcast(F32)
        T = over("T", 8, KT)
        N, NL = over("N", 56, KT), over("N_lo", 56, KT, F32R)
        ZL2 = over("Z_lo", 16, 28, F32R)
        HW, HL = over("H", 16, HALF), over("H_lo", 16, HALF, F32R)
        HR = over("H_hi", 16 + HALF, HALF, F32R)
        HRF = HR.bitcast(F32)
        PART = over("PART", 48, KT)
        MEMT, CST2T, RELU = over("MEM", 64, 4), over("CST2", 68, 4), over("RELU", 68, 4)
        MEM_HI, MEM_LO = over("MEM_hi", 40, 4, F32R), over("MEM_lo", 52, 4, F32R)
        VSG = sb("VSG", [P, ST, VSG_N])
        GSIG = sb("GSIG", [P, ST, 3, NH])
        RS = sb("RS", [P, S])
        CST = sb("CST", [P, NCST])
        PAR = sb("PAR", [P, NPAR])
        H = sb("PHI", [P, 2, NG, 32])
        KCC = sb("KCC", [P, 32])
        VCC = sb("VCC", [32, NG, HD])
        CS = sb("CS", [P, ST, NH, NCMP])
        CM = sb("CM", [P, 4, ST * NH])
        AM = sb("AM", [P, 2, 4, 4])
        LAM = sb("LAM", [P, 2 * HD + 8])
        MS = sb("MS", [P, 2, ST * DH])
        LE = sb("LE", [P, 2, 2, 2, P + 2])

        def cst(name):
            c, n = CCOL[name]
            return CST[:, c:c + n]

        def par(name, i=0, n=None):
            c, m = PCOL[name]
            return PAR[:, c + i:c + (m if n is None else i + n)]

        landed = [sem(f"landed{j}") for j in range(RING)]
        used = sem("used")
        x_in = sem("x_in")
        cst_in = sem("cst_in")
        par_in = sem("par_in")
        x_ready = sem("x_ready")
        out_done = sem("out_done")
        zc = sem("zc")
        tokc = sem("tokc")
        gsig = sem("gsig")
        rot = sem("rot")
        rope = sem("rope")
        cmpin = sem("cmpin")
        phih = sem("phih")
        phio = sem("phio")
        cmpkv = sem("cmpkv")
        cs_step = sem("cs_step")
        cs_tr = sem("cs_tr")
        cs_pt = sem("cs_pt")
        cs_av = sem("cs_av")
        cs_out = sem("cs_out")
        conv_p = sem("conv_p")
        conv_out = sem("conv_out")
        lam_d = sem("lam_d")
        lam_e = sem("lam_e")
        at_sc = sem("at_sc")
        at_max = sem("at_max")
        at_exp = sem("at_exp")
        at_comb = sem("at_comb")
        at_tr = sem("at_tr")
        at_pt = sem("at_pt")
        at_av = sem("at_av")
        at_out = sem("at_out")
        yb_step = sem("yb_step")
        ytr = sem("ytr")
        y_hi, y_lo = sem("y_hi"), sem("y_lo")
        m_hi, m_lo = sem("m_hi"), sem("m_lo")
        x0_hi = sem("x0_hi")
        w_hi, w_lo = sem("w_hi"), sem("w_lo")
        sg = sem("sg")
        mg = sem("mg")
        x1pre = sem("x1pre")
        x2pre = sem("x2pre")
        x1 = sem("x1")
        up_a = sem("up_a")
        up_c = sem("up_c")
        up_g = sem("up_g")
        up_h = sem("up_h")
        ln = {k: sem(f"ln_{k}") for k in ("mean", "xc", "sq", "var", "std", "y", "hi")}

        PAR2 = sb("PAR2", [P, NPAR2])
        LRU = sb("LRU", [P, 4, KT])
        MID = sb("MID", [P, 3, KT, RC])
        MN = MEMT.rearrange("p t n -> p (t n)").rearrange("p (k s) -> p k s", k=KT)
        CST2 = CST2T.rearrange("p t n -> p (t n)")
        MK = Z[:, 8:12, :].rearrange("p k s -> p (k s)").rearrange("p (k s) -> p k s", k=KT)
        MV = Z[:, 12:16, :].rearrange("p k s -> p (k s)").rearrange("p (k n) -> p k n", k=2)
        MNH, MNL = [t.rearrange("p t n -> p (t n)").rearrange("p (k s) -> p k s", k=KT) for t in (MEM_HI, MEM_LO)]
        MNHF = MNH.bitcast(F32)
        MP = T[:, 0:4, :].rearrange("p k s -> p (k s)").rearrange("p (u h s) -> p u h s", u=2, h=MH)
        SPARE = RHF[:].rearrange("p j (e s) -> p (j e) s", e=2)
        LT, YCF = SPARE[:, 0:4, :], SPARE[:, 4:8, :]
        VSGF = VSG[:].rearrange("p t n -> p (t n)")
        CSF = CS[:].rearrange("p t h n -> p (t h n)")
        cos0 = CCOL["cos"][0]
        MIX = [[T[:, n, :] for n in range(KT)], [SPARE[:, n, :] for n in range(KT)]]
        TW, TA_, TG = Y[0:HD, 8, :], Y[0:HD, 9, :], Y[:, 10, :]
        LANES = []
        for L in range(2):
            wide = Z[:, 24:28, :].rearrange("p k s -> p (k s)") if L == 0 else LT.rearrange("p k s -> p (k s)")
            single = [Y[:, 8, :], Y[:, 9, :], YCF[:, 0, :], YCF[:, 1, :], VSGF[:, 0:S], CST[:, cos0:cos0 + S]] if L == 0 else \
                     [YCF[:, 2, :], YCF[:, 3, :], VSGF[:, S:2 * S], Y[:, 11, :], CST[:, cos0 + S:cos0 + 2 * S], RS[:]]
            LANES.append(dict(
                ar=single[0].rearrange("p (n a t) -> p n a t", n=2, a=2),
                bk=single[1].rearrange("p (a n t) -> p a n t", a=2, n=2),
                pu=single[1].rearrange("p (a q i) -> p a q i", a=2, q=4),
                e=LE[:, L], z=single[2].rearrange("p (q t) -> p q t", q=4),
                g1=wide[:, 0:1024].rearrange("p (q a t) -> p q a t", q=4, a=2),
                g2=wide[:, 1024:2048].rearrange("p (q a t) -> p q a t", q=4, a=2),
                x=single[3].rearrange("p (q t) -> p q t", q=4), xt=single[4].rearrange("p (q t) -> p q t", q=4),
                bktok=single[5].rearrange("p (a n c) -> p a n c", a=2, n=2),
                vtok=CSF[:, L * 256:L * 256 + 256].rearrange("p (n c) -> p n c", n=2),
                sh=CSF[:, 512 + L * P:512 + L * P + P].rearrange("p (n i) -> p n i", n=2)))
        GN_STD, GN_BONUS = [Y[:, 8, :], Y[:, 9, :]], [Y[:, 11, :], VSGF[:, 0:S]]
        STATE = PAR[:, 0:KT * HD].rearrange("p (n i) -> p n i", n=KT)

        def par2(name, i=0, n=None):
            c, m = P2COL[name]
            return PAR2[:, c + i:c + (m if n is None else i + n)]

        def cst2(name, i=0, n=None):
            c, m = C2COL[name]
            return CST2[:, c + i:c + (m if n is None else i + n)]

        par2_in = sem("par2_in")
        cst2_in = sem("cst2_in")
        mem_in = sem("mem_in")
        xr2 = sem("xr2")
        t_ready = sem("t_ready")
        rms_sq, rms_var, rms_std, rms_y = [sem(f"rms_{k}") for k in ("sq", "var", "std", "y")]
        NORMED = {i: KT * (at + 1) for at, i in enumerate((0, 1, 3, 5, 7, 9, 11))}
        lru_in = sem("lru_in")
        lru_conv = sem("lru_conv")
        lru_gate = sem("lru_gate")
        lru_rate = sem("lru_rate")
        lru_ea = sem("lru_ea")
        lru_q = sem("lru_q")
        lru_m = sem("lru_m")
        lru_y = sem("lru_y")
        mq = sem("mq")
        mv = sem("mv")
        m_sc, m_max, m_exp, m_p, m_tr, m_pt, m_o = [sem(f"m_{k}") for k in ("sc", "max", "exp", "p", "tr", "pt", "o")]
        src_hi, src_lo = sem("src_hi"), sem("src_lo")
        mem_hi, mem_lo = sem("mem_hi"), sem("mem_lo")
        mup_r = sem("mup_r")
        mup = sem("mup")
        mix = sem("mix")
        rkv = sem("rkv")
        lora = sem("lora")
        lw = sem("lw")
        la = sem("la")
        kk_s = [sem(f"kk_{k}") for k in ("raw", "sq", "sum", "rt", "done")]
        cum = sem("cum")
        mid_e = sem("mid_e")
        ch = [{k: sem(f"ch{L}_{k}") for k in ("exp", "hat", "tr", "tok", "g1", "g2", "g2m", "x0t", "x0", "z", "zm", "x", "xc",
                                              "p", "pc", "u", "uc", "s", "yc", "sc")} for L in range(2)]
        gn = [sem(f"gn_{k}") for k in ("mean", "yc", "sq", "var", "std", "bp", "bonus", "sum", "g", "out")]

        block = ctx.enter_context(nc.Block())

        @block.sync
        def _(sp):
            sp.dma_start(X[:], a["x"]).then_inc(x_in, 16)
            for j in range(RING):
                sp.dma_start(ring[:, j, :], a["weights"][j]).then_inc(landed[j], 16)
            sp.dma_start(CST[:], a["cst"]).then_inc(cst_in, 16)
            sp.dma_start(PAR2[:], a["par2"]).then_inc(par2_in, 16)
            with sp.Fori(1, N_CHUNKS // RING) as q:
                for j in range(RING):
                    sp.wait_ge(used, q * RING + (j + 1 - RING))
                    sp.dma_start(ring[:, j, :], a["weights"][bass.ds(q * RING + j, 1)]
                                 .rearrange("a p c -> (a p) c")).then_inc(landed[j], 16)
            sp.wait_ge(xr2, 7 * KT)
            sp.dma_start(out, X).then_inc(out_done, 16)
            sp.wait_ge(out_done, 16)

        @block.tensor
        def _(pe):
            mm = nc.tensor.matmul

            def arrived(quad, j):
                pe.wait_ge(landed[j], quad * 16 + 16)

            def three(o, lh, ll, rh, rl, start, stop):
                mm(o, lh, rh, start=start, stop=False)
                mm(o, ll, rh, start=False, stop=False)
                return mm(o, lh, rl, start=False, stop=stop)

            def w(j, k):
                return ring[:, j, k * P:k * P + P]

            def wh(j, k):
                return RH[:, j, k * P:k * P + P]

            def wl(j, k):
                return RL[:, j, k * P:k * P + P]

            def first_quad(split, bank, hi, lo, ready, base, step=1, banks_free=None):
                for k in range(KT):
                    pe.wait_ge(ready, base + step * (k + 1))
                    for j in range(2):
                        if k == 0:
                            pe.wait_ge(w_lo, split + (j + 1))
                            if banks_free is not None:
                                pe.wait_ge(banks_free[0], banks_free[1] + (j + 1))
                        ins = three(ps[:, bank + j, :], wh(j, k), wl(j, k), hi[:, k, :], lo[:, k, :], k == 0, k == KT - 1)
                        if k == KT - 1:
                            ins.then_inc(used, 1)
                for j in range(2, RING):
                    if banks_free is not None:
                        pe.wait_ge(banks_free[0], banks_free[1] + (j + 1))
                    product(split + j, j, bank + j, hi, lo)

            def product(split, j, bank, hi, lo):
                pe.wait_ge(w_lo, split + 1)
                for k in range(KT):
                    ins = three(ps[:, bank, :], wh(j, k), wl(j, k), hi[:, k, :], lo[:, k, :], k == 0, k == KT - 1)
                ins.then_inc(used, 1)

            def tokens(split, banks, n):
                for j in range(RING):
                    pe.wait_ge(w_lo, split + (j + 1))
                    for t in range(ST):
                        for e in range(2):
                            k, c = 2 * j + e, slice(t * P, t * P + P)
                            ins = three(ps[:, banks + t, 0:n], XH[:, k, c], XL[:, k, c], RH[:, j, e * 512:e * 512 + n],
                                        RL[:, j, e * 512:e * 512 + n], k == 0, k == KT - 1)
                    ins.then_inc(used, 1)

            def layer_norm(l, i, pre, pre_base):
                s, at = ln, l * 2 + i
                for n in range(KT):
                    pe.wait_ge(pre, l * KT + pre_base + n + 1)
                    ins = mm(ps[:, 4, :], cst("mean"), X[:, n, :], start=(n == 0), stop=(n == KT - 1))
                ins.then_inc(s["mean"], 1)
                for n in range(KT):
                    pe.wait_ge(s["sq"], at * KT + n + 1)
                    ins = mm(ps[:, 5, :], cst("mean"), T1[:, n, :], start=(n == 0), stop=(n == KT - 1))
                ins.then_inc(s["var"], 1)

            def scores(l, u):
                kind, qi, which = UNITS[u]
                W = (qi + 1) * P
                if u > 0:
                    pe.wait_ge(at_exp, l * NU + u)
                for m in range(4):
                    if kind == "diff":
                        h, o = 2 * which + m // 2, (m % 2) * HD
                        q, k = Z[o:o + HD, Z_DQ + h, qi * P:W], Z[o:o + HD, Z_DK + h, 0:W]
                    else:
                        o = which * HD
                        q, k = Z[o:o + HD, Z_NQ + m, qi * P:W], Z[o:o + HD, Z_KS + kind, 0:W]
                    mm(ps[:, m, 0:W], q, k, start=True, stop=False)
                    ins = mm(ps[:, m, qi * P:W], cst("ident"), cst("maskneg"), start=False, stop=True)
                ins.then_inc(at_sc, 1)

            def turn(l, u, i):
                kind, qi, which = UNITS[u]
                t = HEADS_BEFORE[u] + i
                if i == 0:
                    if kind == "diff":
                        pe.wait_ge(at_comb, l * (NU // 3) + u + 1)
                    else:
                        pe.wait_ge(at_exp, l * NU + u + 1)
                if t >= 2:
                    pe.wait_ge(at_pt, l * NHEADS + t - 1)
                m = 2 * i if kind == "diff" else i
                for kb in range(qi + 1):
                    ins = nc.tensor.transpose(ps[:, 4 + t % 2, kb * P:kb * P + P],
                                              PROB[:, (u % 2) * 4 + m, kb * P:kb * P + P], cst("ident"))
                ins.then_inc(at_tr, 1)

            def values(l, u, i):
                kind, qi, which = UNITS[u]
                t = HEADS_BEFORE[u] + i
                if i == 0 and u >= 2:
                    pe.wait_ge(at_out, l * NU + u - 1)
                pe.wait_ge(at_pt, l * NHEADS + t + 1)
                for kb in range(qi + 1):
                    if kind == "diff":
                        h = 2 * which + i
                        o, v = ps[:, 6 + u % 2, i * P:i * P + P], DV[:, kb, h * P:h * P + P]
                    else:
                        c = kind * P + which * HD
                        o, v = ps[:, 6 + u % 2, i * HD:i * HD + HD], VSG[:, kb, c:c + HD]
                    ins = mm(o, PT[:, t % 4, kb * P:kb * P + P], v, start=(kb == 0), stop=(kb == qi))
                ins.then_inc(at_av, 1)

            pe.wait_ge(x_in, 16)
            pe.wait_ge(cst_in, 16)
            with pe.Fori(0, DEPTH) as l:
                Q = l * (CPL // RING)
                W0 = l * SPL
                first_quad(W0, 0, XH, XL, x_ready, l * 16, 2, (zc, l * C_Z))
                with pe.Fori(1, C_Z // RING) as i:
                    for j in range(RING):
                        pe.wait_ge(zc, l * C_Z + i * RING + (j + 1))
                        product(W0 + i * RING + j, j, j, XH, XL)
                tokens(W0 + B_DV, 4, DH * P)
                pe.wait_ge(zc, l * C_Z + C_Z + 4)
                for r, t in enumerate(ROPE_TILES):
                    if r >= 4:
                        pe.wait_ge(rope, l * NR + r - 3)
                    mm(ps[:, r % 4, :], cst("rot"), Z[:, t, :], start=True, stop=True).then_inc(rot, 1)
                pe.wait_ge(tokc, l * 8 + 4)
                tokens(W0 + B_VSG, 4, VSG_N)
                pe.wait_ge(rope, l * NR + NR)
                pe.wait_ge(cmpin, l * 4 + 4)
                for c in range(C_PHI):
                    kv = c // 4
                    arrived(Q + (B_PHI + c) // RING, c % RING)
                    for e in range(8):
                        p = (c % 4) * 8 + e
                        for g in range(NG):
                            src = SCR[g * HD:g * HD + HD, 2 * kv + p // 16, p:p + CMP_STRIDE * (NCMP - 1) + 1:CMP_STRIDE]
                            ins = mm(ps[:, 2 * kv + g, 0:NCMP], ring[g * HD:g * HD + HD, c % RING, e * P:e * P + P], src,
                                     start=(p == 0), stop=(p == CMP_BLOCK - 1))
                    ins.then_inc(used, 1)
                pe.wait_ge(phih, l * 4 + 4)
                pe.wait_ge(tokc, l * 8 + 8)
                for g in range(NG):
                    mm(ps[:, 4, g * 32:g * 32 + NCMP], par("phi_w2k"), H[:, 0, g, 0:NCMP], start=True, stop=True)
                    ins = mm(ps[0:NCMP, 5, g * HD:g * HD + HD], H[:, 1, g, 0:NCMP], par("phi_w2v"), start=True, stop=True)
                ins.then_inc(phio, 1)
                pe.wait_ge(cmpkv, l + 1)
                for qi in range(ST):
                    for g in range(NG):
                        for r in range(HPG):
                            c = qi * P + r * 32
                            ins = mm(ps[:, g, c:c + NCMP], Z[g * HD:g * HD + HD, Z_NQ + r, qi * P:qi * P + P],
                                     KCC[g * HD:g * HD + HD, 0:NCMP], start=True, stop=True)
                ins.then_inc(cs_step, 1)
                pe.wait_ge(cs_step, l * 4 + 4)
                for qi in range(ST):
                    b = 2 + 2 * (qi % 3)
                    if qi == 3:
                        pe.wait_ge(cs_pt, l * ST + 1)
                    for h in range(NH):
                        ins = nc.tensor.transpose(ps[0:NCMP, b + h // 4, (h % 4) * P:(h % 4) * P + P], CS[:, qi, h, :], cst("ident"))
                    ins.then_inc(cs_tr, 1)
                for qi in range(ST):
                    pe.wait_ge(cs_pt, l * ST + qi + 1)
                    if qi >= 2:
                        pe.wait_ge(cs_out, l * ST + qi - 1)
                    for h in range(NH):
                        e = SCR[0:NCMP, qi * 2 + h // 4, (h % 4) * P:(h % 4) * P + P]
                        ins = mm(ps[:, qi % 2, h * HD:h * HD + HD], e, VCC[0:NCMP, h // HPG, :], start=True, stop=True)
                    ins.then_inc(cs_av, 1)
                pe.wait_ge(cs_out, l * ST + ST)
                scores(l, 0)
                for u in range(NU):
                    if u + 1 < NU:
                        scores(l, u + 1)
                    n = HEADS_OF[u]
                    turn(l, u, 0)
                    for i in range(n):
                        if i + 1 < n:
                            turn(l, u, i + 1)
                        values(l, u, i)
                pe.wait_ge(at_out, l * NU + NU)
                for c in range(4):
                    for t in range(ST):
                        ins = nc.tensor.transpose(ps[:, c, t * P:t * P + P],
                                                  YC[:, t, 2 * c:2 * c + 2, :].rearrange("p h d -> p (h d)"), cst("ident"))
                    ins.then_inc(ytr, 1)
                pe.wait_ge(yb_step, l * 4 + 4)
                for c in range(4):
                    for t in range(ST):
                        ins = nc.tensor.transpose(ps[:, 4 + c, t * P:t * P + P], YB[:, t, c, :], cst("ident"))
                    ins.then_inc(ytr, 1)
                with pe.Fori(0, 3) as b:
                    pe.wait_ge(y_lo, l * 12 + 12)
                    for p in range(4):
                        for e in range(2):
                            c = 3 * p + e
                            pe.wait_ge(sg, l * 24 + b * 8 + (2 * p + e + 1))
                            product(W0 + b * 12 + (n_split(B_MERGE) + c), c % RING, (2 * p + e) % 4, XH, XL)
                        c = 3 * p + 2
                        pe.wait_ge(w_lo, W0 + b * 12 + (n_split(B_MERGE) + c + 1))
                        for e in range(2):
                            pe.wait_ge(mg, l * 24 + b * 8 + (2 * p + e + 1))
                            for k in range(4):
                                hi, lo = [t[:, bass.ds(b * 4 + k, 1), :].rearrange("p a t -> p (a t)") for t in (YH, YL)]
                                ins = three(ps[:, 4 + (2 * p + e) % 4, :], wh(c % RING, e * 4 + k), wl(c % RING, e * 4 + k),
                                            hi, lo, k == 0, k == 3)
                        ins.then_inc(used, 1)
                first_quad(W0 + n_split(B_WO), 0, MR, ML, m_lo, l * KT)
                for j in range(RING):
                    pe.wait_ge(x1pre, l * KT + RING + (j + 1))
                    product(W0 + (n_split(B_WO) + RING + j), j, j, MR, ML)
                layer_norm(l, 0, x1pre, 4)
                first_quad(W0 + n_split(B_UP), 0, XH, XL, x1, l * KT, 1, (up_c, l * C_UP))
                with pe.Fori(1, C_UP // RING) as i:
                    for j in range(RING):
                        pe.wait_ge(up_c, l * C_UP + i * RING + (j + 1))
                        product(W0 + i * RING + (n_split(B_UP) + j), j, j, XH, XL)
                with pe.Fori(0, 2) as i:
                    pe.wait_ge(up_h, l * FT + FT + 2)
                    for n in range(4):
                        pe.wait_ge(x2pre, l * KT + i * 4 + (n + 1))
                        for c in range(3):
                            f = 3 * n + c
                            pe.wait_ge(w_lo, W0 + i * 12 + (n_split(B_DOWN) + f + 1))
                            for k in range(8 * c, min(8 * c + 8, FT)):
                                ins = three(ps[:, n, :], wh(f % RING, k - 8 * c), wl(f % RING, k - 8 * c), FHR[:, k, :], FL[:, k, :],
                                            k == 0, k == FT - 1)
                            ins.then_inc(used, 1)
                layer_norm(l, 1, x2pre, 4)

            def rms(i, bank_cols=S, sq=None):
                for n in range(KT):
                    pe.wait_ge(rms_sq, i * KT + n + 1)
                    src = T[:, n, 0:bank_cols]
                    ins = mm(ps[:, 5, 0:bank_cols], cst("mean"), src, start=(n == 0), stop=(n == KT - 1))
                ins.then_inc(rms_var, 1)

            def gemm(first, tiles, hi, lo, free, base, src, bank=0):
                first_quad(n_split(first), bank, hi, lo, src_lo, src, 1, (free, base))
                if tiles > RING:
                    with pe.Fori(1, tiles // RING) as i:
                        for j in range(RING):
                            pe.wait_ge(free, i * RING + (base + j + 1))
                            product(i * RING + (n_split(first) + j), j, bank + j, hi, lo)

            def tail(l):
                B = B_TAIL0 if l == 0 else B_TAIL1
                rms(3 + 6 * l)
                gemm(B, C_MQ, AH, NL, mq, l * 16, SRC[f"q{l}"])
                pe.wait_ge(mem_lo, l + 1)
                with pe.Fori(0, C_MK // RING) as i:
                    for j in range(RING):
                        pe.wait_ge(mq, i * RING + (l * 16 + 8 + j + 1))
                        pe.wait_ge(w_lo, i * RING + (n_split(B + C_MQ) + j + 1))
                        for k in range(KT):
                            ins = three(ps[:, j, 0:S2], wh(j, k), wl(j, k), MNH[:, k, :], MNL[:, k, :], k == 0, k == KT - 1)
                        ins.then_inc(used, 1)
                for c in range(C_MV):
                    half, j = c // 4, c % 4
                    pe.wait_ge(w_lo, n_split(B + C_MQ + C_MK + c) + 1)
                    for t in range(2):
                        for e in range(2):
                            k, r = 2 * j + e, slice(e * 512, e * 512 + 512)
                            ins = three(ps[:, 4 + 2 * half + t, :], MNH[:, k, t * P:t * P + P], MNL[:, k, t * P:t * P + P],
                                        RH[:, j, r], RL[:, j, r], k == 0, k == KT - 1)
                    ins.then_inc(used, 1)
                pe.wait_ge(mq, l * 16 + 20)

                def scores2(qi):
                    if qi >= 2:
                        pe.wait_ge(m_exp, l * ST + qi - 1)
                    for h in range(MH):
                        for k in range(MT):
                            ins = mm(ps[:, 2 * (qi % 2) + h // 2, (h % 2) * S2:(h % 2) * S2 + S2],
                                     Z[:, h * MT + k, qi * P:qi * P + P], MK[:, h * MT + k, :], start=(k == 0), stop=(k == MT - 1))
                    ins.then_inc(m_sc, 1)

                scores2(0)
                for qi in range(ST):
                    if qi + 1 < ST:
                        scores2(qi + 1)
                    if qi == 0:
                        pe.wait_ge(mv, l * 4 + 4)
                    pe.wait_ge(m_p, l * ST + qi + 1)
                    for kb in range(2):
                        if qi >= 2:
                            pe.wait_ge(m_pt, l * 2 * ST + 2 * (qi - 2) + kb + 1)
                        for h in range(MH):
                            ins = nc.tensor.transpose(ps[:, 4 + 2 * (qi % 2) + kb, h * P:h * P + P],
                                                      MP[:, qi % 2, h, kb * P:kb * P + P], cst("ident"))
                        ins.then_inc(m_tr, 1)
                pe.wait_ge(m_pt, l * 2 * ST + 2 * ST)
                for c in range(KT):
                    h = c // MT
                    if c >= 4:
                        pe.wait_ge(src_lo, SRC[f"o{l}"] + c - 3)
                    for kb in range(2):
                        ins = mm(ps[:, c % 4, :], MV[:, kb, c * P:c * P + P], Z[:, 16 + 2 * h + kb, :], start=(kb == 0), stop=(kb == 1))
                    ins.then_inc(m_o, 1)
                gemm(B + C_MQ + C_MK + C_MV, C_MO, AH, YL, t_ready, l * 32 + 8, SRC[f"o{l}"], 4)
                rms(4 + 6 * l)
                rms(5 + 6 * l)
                for h in range(2):
                    U = B + B_MFF + h * (C_HUP + C_HDN)
                    gemm(U, C_HUP, AH, NL, mup, l * F2T + h * HALF, SRC[f"up{l}"], 4)
                    with pe.Fori(0, 2) as i:
                        pe.wait_ge(mup, l * F2T + h * HALF + HALF + 4)
                        for n in range(4):
                            pe.wait_ge(t_ready, i * 4 + (l * 32 + 16 + h * KT + n + 1))
                            for c in range(2):
                                j = (2 * n + c) % RING
                                pe.wait_ge(w_lo, i * 8 + (n_split(U + C_HUP) + 2 * n + c + 1))
                                for k in range(8):
                                    ins = three(ps[:, n, :], wh(j, k), wl(j, k), HR[:, 8 * c + k, :], HL[:, 8 * c + k, :],
                                                c == 0 and k == 0, c == 1 and k == 7)
                                ins.then_inc(used, 1)
                rms(6 + 6 * l)

            rms(0, S2)
            rms(1)
            gemm(B_LRU, C_LRU_IN, AH, NL, lru_in, 0, SRC["lru_in"])
            pe.wait_ge(lru_conv, KT)
            pe.wait_ge(lru_in, 20)
            for c in range(C_LRU_GATE):
                arrived((B_LRU + C_LRU_IN + c) // RING, c)
                if c >= 2:
                    pe.wait_ge(lru_gate, 4 * (c - 1))
                for b in range(4):
                    k0 = (c % 2) * 4 + (b // 2) * 2
                    for k in range(2):
                        ins = mm(ps[:, 4 * (c % 2) + b, :], w(c, b * 2 + k), Z[:, 16 + k0 + k, :], start=(k == 0), stop=(k == 1))
                ins.then_inc(used, 1)
            gemm(B_LRU + C_LRU_IN + C_LRU_GATE, C_LRU_OUT, AH, ZL2[:, 16:24, :], t_ready, 0, SRC["lru_out"])
            rms(2)
            tail(0)

            rms(7)
            for m in range(3):
                pe.wait_ge(mix, KT * (m + 1))
                for n in range(KT):
                    c = m * KT + n
                    pe.wait_ge(rkv, c + 1)
                    arrived((B_RWKV + c) // RING, c % RING)
                    for k in range(KT):
                        ins = mm(ps[:, c % 4, :], w(c % RING, k), MIX[m % 2][k], start=(k == 0), stop=(k == KT - 1))
                    ins.then_inc(used, 1)
            QL = (B_RWKV + C_RKV) // RING
            pe.wait_ge(mix, 4 * KT)
            arrived(QL, 0)
            for k in range(KT):
                ins = mm(ps[0:HD, 4, :], ring[:, 0, k * HD:k * HD + HD], MIX[1][k], start=(k == 0), stop=(k == KT - 1))
            ins.then_inc(lora, 1)
            pe.wait_ge(mix, 5 * KT)
            for k in range(KT):
                ins = mm(ps[0:HD, 5, :], ring[:, 0, 512 + k * HD:512 + k * HD + HD], MIX[0][k], start=(k == 0), stop=(k == KT - 1))
            ins.then_inc(used, 1)
            pe.wait_ge(mix, 6 * KT)
            arrived(QL, 1)
            for k in range(KT):
                ins = mm(ps[:, 6, :], w(1, k), MIX[1][k], start=(k == 0), stop=(k == KT - 1))
            ins.then_inc(used, 1)
            arrived(QL, 2)
            pe.wait_ge(rkv, 3 * KT + 4)
            pe.wait_ge(la, 1)
            for n in range(KT):
                if n >= 4:
                    pe.wait_ge(lw, n - 3)
                ins = mm(ps[:, n % 4, :], ring[0:HD, 2, n * P:n * P + P], TW, start=True, stop=True)
                ins.then_inc(lora, 1)
            arrived(QL, 3)
            pe.wait_ge(la, 3)
            for n in range(KT):
                if n >= 4:
                    pe.wait_ge(la, 3 + n - 3)
                ins = mm(ps[:, 4 + n % 4, :], ring[0:HD, 3, n * P:n * P + P], TA_, start=True, stop=True)
                ins.then_inc(lora, 1)
            pe.wait_ge(lw, KT)
            pe.wait_ge(la, 3 + KT)
            pe.sem_inc(used, 2)
            pe.wait_ge(cst2_in, 16)
            for n in range(KT):
                pe.wait_ge(kk_s[1], n + 1)
                if n >= 4:
                    pe.wait_ge(kk_s[3], n - 3)
                mm(ps[:, n % 4, :], cst2("ones"), Z[:, 24 + n % 2, :], start=True, stop=True).then_inc(kk_s[2], 1)

            def chain(c, half, L):
                s, B, o = ch[L], LANES[L], 4 * L
                return s, B, o, c * 2 + half

            with pe.Fori(0, RC) as c:
                for half in range(2):
                    for L in range(2):
                        s, B, o, it = chain(c, half, L)
                        pe.wait_ge(s["hat"], it + 1)
                        for e in range(2):
                            for n in range(2):
                                ins = nc.tensor.transpose(ps[:, o, (2 * e + n) * P:(2 * e + n) * P + P], B["bk"][:, e, n, :], cst("ident"))
                        for n in range(2):
                            ins = nc.tensor.transpose(ps[:, o + 1, n * P:n * P + P], B["x"][:, n, :], cst("ident"))
                        ins.then_inc(s["tr"], 1)
                        for q in range(4):
                            r, n = (q % 2) * HD, q // 2
                            ins = mm(ps[:, o + 2 + q % 2, n * 2 * P:n * 2 * P + 2 * P], B["bk"][r:r + HD, 0, n, :],
                                     B["ar"][r:r + HD, n, :, :].rearrange("p a t -> p (a t)"), start=True, stop=True)
                        ins.then_inc(s["g1"], 1)
                    for L in range(2):
                        s, B, o, it = chain(c, half, L)
                        pe.wait_ge(s["tok"], it + 1)
                        for q in range(4):
                            r, n = (q % 2) * HD, q // 2
                            ins = mm(ps[:, o + q % 2, n * 2 * P:n * 2 * P + 2 * P], B["bk"][r:r + HD, 1, n, :],
                                     B["ar"][r:r + HD, n, :, :].rearrange("p a t -> p (a t)"), start=True, stop=True)
                        ins.then_inc(s["g2"], 1)
                    for L in range(2):
                        s, B, o, it = chain(c, half, L)
                        pe.wait_ge(s["x0t"], it + 1)
                        for q in range(4):
                            ins = nc.tensor.transpose(ps[:, o + 2, q * P:q * P + P], B["xt"][:, q, :], cst("ident"))
                        ins.then_inc(s["x0"], 1)
                    for v in range(LEVELS):
                        for L in range(2):
                            s, B, o, it = chain(c, half, L)
                            if v == 0:
                                pe.wait_ge(s["g2m"], it + 1)
                            pe.wait_ge(s["xc"], it * (2 * LEVELS + 1) + 2 * v + 1)
                            for q in range(4):
                                ins = mm(ps[:, o, q * P:q * P + P], B["g1"][:, q, 0, :], B["x"][:, q, :], start=True, stop=True)
                            ins.then_inc(s["z"], 1)
                        for L in range(2):
                            s, B, o, it = chain(c, half, L)
                            pe.wait_ge(s["zm"], it * LEVELS + v + 1)
                            for q in range(4):
                                ins = mm(ps[:, o + 1, q * P:q * P + P], B["xt"][:, q, :], B["z"][:, q, :], start=True, stop=True)
                            ins.then_inc(s["x"], 1)
                            for q in range(4):
                                ins = mm(ps[:, o + 2, q * P:q * P + P], B["z"][:, q, :], B["xt"][:, q, :], start=True, stop=True)
                            ins.then_inc(s["x"], 1)
                    for L in range(2):
                        s, B, o, it = chain(c, half, L)
                        pe.wait_ge(s["xc"], it * (2 * LEVELS + 1) + 2 * LEVELS + 1)
                        for q in range(4):
                            r, n = (q % 2) * HD, q // 2
                            mm(ps[:, o + q % 2, n * HD:n * HD + HD], B["ar"][r:r + HD, n, 0, :], B["sh"][r:r + HD, n, :], start=True, stop=False)
                            ins = mm(ps[:, o + q % 2, n * HD:n * HD + HD], B["g2"][:, q, 0, :], B["vtok"][:, n, r:r + HD], start=False, stop=True)
                        ins.then_inc(s["p"], 1)
                    for L in range(2):
                        s, B, o, it = chain(c, half, L)
                        pe.wait_ge(s["pc"], it + 1)
                        for q in range(4):
                            ins = mm(ps[:, o + 2, q * HD:q * HD + HD], B["xt"][:, q, :], B["pu"][:, 0, q, :], start=True, stop=True)
                        ins.then_inc(s["u"], 1)
                    for L in range(2):
                        s, B, o, it = chain(c, half, L)
                        pe.wait_ge(s["uc"], it + 1)
                        for n in range(2):
                            y = ps[:, o, n * P:n * P + P]
                            mm(y, B["bktok"][:, 0, n, :], B["pu"][:, 1, 2 * n:2 * n + 2, :].rearrange("p q i -> p (q i)"), start=True, stop=False)
                            mm(y, B["bktok"][:, 1, n, :], B["vtok"][:, n, :], start=False, stop=True)
                        for q in range(4):
                            r, n = (q % 2) * HD, q // 2
                            y = ps[r:r + HD, o + 3, n * P:n * P + P]
                            mm(y, B["sh"][r:r + HD, n, :], B["ar"][r:r + HD, n, 1, :], start=True, stop=False)
                            mm(y, B["pu"][:, 1, q, :], B["g1"][:, q, 1, :], start=False, stop=False)
                            ins = mm(y, B["vtok"][:, n, r:r + HD], B["g2"][:, q, 1, :], start=False, stop=True)
                        ins.then_inc(s["s"], 1)

            for L in range(2):
                pe.wait_ge(ch[L]["yc"], 2 * RC)
                pe.wait_ge(ch[L]["sc"], 2 * RC)
            for j in range(RING - 1):
                arrived((B_RWKV + C_RKV + C_LORA) // RING, j)
            pe.sem_inc(used, RING - 1)
            arrived((B_RWKV + C_RKV + C_LORA) // RING, RING - 1)
            for n in range(KT):
                if n >= 2:
                    pe.wait_ge(gn[9], n - 1)
                o = 4 * (n % 2)
                mm(ps[:, o, :], cst2("ones"), T[:, n, :], start=True, stop=True).then_inc(gn[0], 1)
                pe.wait_ge(gn[5], n + 1)
                mm(ps[:, o + 2, :], cst2("ones"), Z[:, 24 + n % 2, :], start=True, stop=True).then_inc(gn[7], 1)
                ins = mm(ps[:, o + 3, :], w(RING - 1, n), TG, start=True, stop=True)
                ins.then_inc(gn[8], 1)
                pe.wait_ge(gn[2], n + 1)
                mm(ps[:, o + 1, :], cst2("ones"), Z[:, 26 + n % 2, :], start=True, stop=True).then_inc(gn[3], 1)
            pe.wait_ge(gn[9], KT)
            pe.sem_inc(used, 1)
            gemm(B_RWKV + C_RKV + C_LORA + C_G2, C_RWO, AH, YL, t_ready, 32, SRC["rwo"])
            rms(8)
            tail(1)

        @block.scalar
        def _(act):
            av = nc.scalar.activation

            def round_chunk(quad, j):
                act.wait_ge(landed[j], quad * 16 + 16)
                av(RH[:, j, :], ring[:, j, :], ACT.Copy).then_inc(w_hi, 1)

            def ahead(quad, j, end=None):
                if end is None or quad * RING + j + 3 < end:
                    round_chunk(quad + (j + 3) // RING, (j + 3) % RING)

            def round_run(quad, before):
                act.wait_ge(used, before)
                for j in range(RING - 1):
                    round_chunk(quad, j)

            def layer_norm(l, i, bias):
                s, at = ln, l * 2 + i
                for n in range(KT):
                    act.wait_ge(s["xc"], at * KT + n + 1)
                    av(T1[:, n, :], X[:, n, :], ACT.Square).then_inc(s["sq"], 1)
                act.wait_ge(s["var"], at + 1)
                av(RS[:], ps[:, 5, :], ACT.Sqrt, bias=cst("eps")).then_inc(s["std"], 1)
                for n in range(KT):
                    act.wait_ge(s["y"], at * KT + n + 1)
                    av(XH[:, n, :], X[:, n, :], ACT.Identity, bias=par(bias, n, 1)).then_inc(s["hi"], 1)

            act.sem_inc(zc, 4)
            act.sem_inc(sg, 4)
            act.sem_inc(mg, 4)
            act.sem_inc(x1pre, 4)
            act.sem_inc(x2pre, 4)
            act.sem_inc(up_c, 4)
            act.sem_inc(up_h, 2)
            for free in (lru_in, t_ready, mq, mup, rkv):
                act.sem_inc(free, 4)
            for L in range(2):
                act.sem_inc(ch[L]["s"], 1)
            act.wait_ge(x_in, 16)
            for j in range(RING - 1):
                round_chunk(0, j)
            for n in range(KT):
                av(XH[:, n, :], X[:, n, :], ACT.Copy).then_inc(x0_hi, 1)
            act.wait_ge(cst_in, 16)
            with act.Fori(0, DEPTH) as l:
                C, Q = l * CPL, l * (CPL // RING)
                act.wait_ge(x_ready, l * 16 + 16)
                act.dma_start(PAR[:], a["par"][bass.ds(l, 1)].rearrange("a p c -> (a p) c")).then_inc(par_in, 16)
                with act.Fori(0, C_Z // RING) as i:
                    for j in range(RING):
                        act.wait_ge(used, C + i * RING + (j + 1))
                        ahead(Q + i, j)
                        av(Z[:, bass.ds(i * RING + j, 1), :], ps[:, j:j + 1, :], ACT.Copy).then_inc(zc, 1)
                for j in range(RING):
                    act.wait_ge(used, C + B_DV + j + 1)
                    ahead(Q + B_DV // RING, j)
                for t in range(ST):
                    av(DV[:, t, :], ps[:, 4 + t, :], ACT.Copy).then_inc(tokc, 1)
                act.wait_ge(used, C + B_VSG + 1)
                ahead(Q + B_VSG // RING, 0)
                act.wait_ge(used, C + B_VSG + C_VSG)
                for t in range(ST):
                    av(VSG[:, t, :], ps[:, 4 + t, 0:VSG_N], ACT.Copy).then_inc(tokc, 1)
                act.wait_ge(tokc, l * 8 + 8)
                av(GSIG[:].rearrange("p t b h -> p t (b h)"), VSG[:, :, 2 * P:VSG_N], ACT.Sigmoid).then_inc(gsig, 1)
                act.wait_ge(used, C + B_PHI + C_PHI)
                for kv in range(2):
                    for g in range(NG):
                        av(H[:, kv, g, 0:NCMP], ps[:, 2 * kv + g, 0:NCMP], ACT.Gelu).then_inc(phih, 1)
                act.wait_ge(lam_d, l + 1)
                av(LAM[:, 2 * HD + 2:2 * HD + 4], LAM[:, 2 * HD:2 * HD + 2], ACT.Exp).then_inc(lam_e, 1)
                act.wait_ge(cs_step, l * 4 + 2)
                av(CS[:], CS[:], ACT.Exp, scale=SCALE).then_inc(cs_step, 1)
                round_run(Q + B_MERGE // RING, C + B_MERGE)
                for qi in range(ST):
                    act.wait_ge(cs_tr, l * ST + qi + 1)
                    b = 2 + 2 * (qi % 3)
                    av(SCR[0:NCMP, 2 * qi:2 * qi + 2, :], ps[0:NCMP, b:b + 2, :], ACT.Copy).then_inc(cs_pt, 1)
                for u in range(NU):
                    W = (UNITS[u][1] + 1) * P
                    act.wait_ge(at_max, l * NU + u + 1)
                    if u >= 2:
                        act.wait_ge(at_av, l * NHEADS + HEADS_BEFORE[u - 1])
                    for m in range(4):
                        ins = av(PROB[:, (u % 2) * 4 + m, 0:W], ps[:, m, 0:W], ACT.Exp, bias=AM[:, u % 2, 1, m:m + 1],
                                 scale=SCALE, accum_out=AM[:, u % 2, 2, m:m + 1])
                    ins.then_inc(at_exp, 1)
                act.wait_ge(at_out, l * NU + NU)
                av(SCR[:, 0:4, :], YB.rearrange("p t h d -> p t (h d)"), ACT.Square).then_inc(yb_step, 1)
                for c in range(4):
                    av(YH[:, c, :], Y[:, c, :], ACT.Copy).then_inc(y_hi, 1)
                act.wait_ge(yb_step, l * 4 + 2)
                av(MS[:, 1, :], MS[:, 0, :], ACT.Sqrt, bias=cst("eps"), scale=1.0 / P).then_inc(yb_step, 1)
                for c in range(8):
                    act.wait_ge(ytr, l * 8 + c + 1)
                    if c < 4:
                        av(YH[:, 8 + c, :], ps[:, c, :], ACT.Copy).then_inc(y_hi, 1)
                    else:
                        av(YH[:, c, :], ps[:, c, :], ACT.Copy, scale=LAM[:, 2 * HD + 6:2 * HD + 7]).then_inc(y_hi, 1)
                with act.Fori(0, 3) as b:
                    for c in range(12):
                        act.wait_ge(used, C + B_MERGE + b * 12 + (c + 1))
                        ahead(Q + B_MERGE // RING + b * 3 + c // RING, c % RING)
                        if c % 3 < 2:
                            n = 2 * (c // 3) + c % 3
                            act.wait_ge(mg, l * 24 + b * 8 + (n + 1))
                            av(T1[:, n % 4, :], ps[:, n % 4, :], ACT.Sigmoid).then_inc(sg, 1)
                for n in range(KT):
                    act.wait_ge(mg, l * 24 + 4 + 16 + n + 1)
                    av(MR[:, n, :], M[:, n, :], ACT.Copy).then_inc(m_hi, 1)
                for c in range(C_WO):
                    act.wait_ge(used, C + B_WO + c + 1)
                    ahead(Q + (B_WO + c) // RING, c % RING)
                layer_norm(l, 0, "ln1_b")
                with act.Fori(0, C_UP // RING) as i:
                    for e in range(2):
                        act.wait_ge(up_h, l * FT + i * 2 + (e + 1))
                        for v in range(2):
                            j = 2 * e + v
                            act.wait_ge(used, C + B_UP + i * RING + (j + 1))
                            ahead(Q + B_UP // RING + i, j)
                            f = i * 2 + (e + v * FT)
                            av(T1[:, j, :], ps[:, j, :], ACT.Identity, bias=PAR[:, bass.ds(f + PCOL["up_b"][0], 1)],
                               scale=PAR[:, bass.ds(f + (PCOL["up_w"][0] + 2 * 2 * FT), 1)]).then_inc(up_a, 1)
                        act.wait_ge(up_c, l * C_UP + i * RING + (2 * e + 5))
                        av(T1[:, 4 + e, :], T1[:, 2 * e, :], ACT.Gelu).then_inc(up_g, 1)
                with act.Fori(0, C_DOWN // RING) as i:
                    for j in range(RING):
                        act.wait_ge(used, C + B_DOWN + i * RING + (j + 1))
                        ahead(Q + B_DOWN // RING + i, j)
                layer_norm(l, 1, "ln2_b")

            def rms(i, src, ready, base, cols=S):
                for n in range(KT):
                    if ready is not None:
                        act.wait_ge(ready, base + n + 1)
                    av(T[:, n, 0:cols], src[:, n, :], ACT.Square).then_inc(rms_sq, 1)
                act.wait_ge(rms_var, i + 1)
                if i == 1:
                    act.wait_ge(rms_y, NORMED[0])
                av(RS[:, 0:cols], ps[:, 5, 0:cols], ACT.Sqrt, bias=par2("rms_eps")).then_inc(rms_std, 1)

            def copies(first, tiles, dst, at, done, func=ACT.Copy, cols=S, bias=None, bank=0, split=True, end=None):
                def quad(i):
                    for j in range(RING):
                        act.wait_ge(used, i * RING + (first + j + 1))
                        if split:
                            ahead(i + first // RING, j, end)
                        kw = {} if bias is None else {"bias": PAR2[:, bass.ds(i * RING + (bias + j), 1)]}
                        av(dst[:, bass.ds(i * RING + (at + j), 1), :], ps[:, bank + j:bank + j + 1, 0:cols], func, **kw).then_inc(done, 1)

                with act.Fori(0, tiles // RING - (end is not None)) as i:
                    quad(i)
                if end is not None:
                    quad(tiles // RING - 1)

            def rounded(hi, src, ready, base):
                for n in range(KT):
                    act.wait_ge(ready, base + n + 1)
                    av(hi[:, n, :], src[:, n, :], ACT.Copy).then_inc(src_hi, 1)

            def tail(l):
                B = B_TAIL0 if l == 0 else B_TAIL1
                av(MNH, MN, ACT.Copy).then_inc(mem_hi, 1)
                rms(3 + 6 * l, X, xr2, 3 * KT * l + KT)
                rounded(AH, N, rms_y, NORMED[3 + 6 * l] - KT)
                copies(B, C_MQ, Z, 0, mq)
                copies(B + C_MQ, C_MK, MK, 0, mq, cols=S2)
                for c in range(C_MV):
                    act.wait_ge(used, B + C_MQ + C_MK + c + 1)
                    ahead((B + C_MQ + C_MK + c) // RING, c % RING)
                    if c % RING == RING - 1:
                        half = c // RING
                        for t in range(2):
                            av(MV[:, t, half * 512:half * 512 + 512], ps[:, 4 + 2 * half + t, :], ACT.Copy).then_inc(mv, 1)

                def exps(qi):
                    act.wait_ge(m_max, l * ST + qi + 1)
                    if qi >= 2:
                        act.wait_ge(m_tr, l * 2 * ST + 2 * (qi - 1))
                    for h in range(MH):
                        ins = av(MP[:, qi % 2, h, :], ps[:, 2 * (qi % 2) + h // 2, (h % 2) * S2:(h % 2) * S2 + S2], ACT.Exp,
                                 bias=AM[:, qi % 2, 1, h:h + 1], scale=(MT * P) ** -0.5, accum_out=AM[:, qi % 2, 2, h:h + 1])
                    ins.then_inc(m_exp, 1)

                exps(0)
                for qi in range(ST):
                    if qi + 1 < ST:
                        exps(qi + 1)
                    for kb in range(2):
                        act.wait_ge(m_tr, l * 2 * ST + 2 * qi + kb + 1)
                        av(Z[:, 16 + kb:24:2, qi * P:qi * P + P],
                           ps[:, 4 + 2 * (qi % 2) + kb, :].rearrange("p (h q) -> p h q", h=MH), ACT.Copy).then_inc(m_pt, 1)
                for c in range(KT):
                    act.wait_ge(m_o, l * KT + c + 1)
                    av(AH[:, c, :], ps[:, c % 4, :], ACT.Copy).then_inc(src_hi, 1)
                copies(B + C_MQ + C_MK + C_MV, C_MO, N, 0, t_ready, bank=4)
                rms(4 + 6 * l, N, t_ready, 4 + l * 32 + 8)
                rms(5 + 6 * l, X, xr2, 3 * KT * l + 2 * KT)
                rounded(AH, N, rms_y, NORMED[5 + 6 * l] - KT)
                for h in range(2):
                    U = B + B_MFF + h * (C_HUP + C_HDN)
                    with act.Fori(0, C_HUP // RING) as i:
                        for j in range(RING):
                            act.wait_ge(used, i * RING + (U + j + 1))
                            ahead(i + U // RING, j)
                            act.wait_ge(mup, i * RING + (l * F2T + h * HALF + j + 1))
                            av(RELU[:, j, :], ps[:, 4 + j, :], ACT.Relu).then_inc(mup_r, 1)
                    for c in range(C_HDN):
                        act.wait_ge(used, U + C_HUP + c + 1)
                        ahead((U + C_HUP + c) // RING, c % RING, B + C_TAIL)
                        if h == 0 and c % 2:
                            n = c // 2
                            av(PART[:, n, :], ps[:, n % 4, :], ACT.Copy).then_inc(t_ready, 1)
                rms(6 + 6 * l, N, t_ready, 4 + l * 32 + 24)

            act.wait_ge(x_ready, 16 * (DEPTH + 1))
            act.dma_start(MN, a["mem"]).then_inc(mem_in, 16)
            act.wait_ge(par2_in, 16)
            act.wait_ge(mem_in, 16)
            act.wait_ge(xr2, KT)
            rms(0, MN, None, 0, S2)
            rms(1, X, None, 0)
            rounded(AH, N, rms_y, NORMED[1] - KT)
            copies(B_LRU, KT, Z, 0, lru_in, ACT.Gelu_apprx_tanh, bias=P2COL["b_in"][0])
            copies(B_LRU + KT, KT, Z, 8, lru_in, ACT.Identity, bias=P2COL["b_in"][0] + KT, end=B_LRU + C_LRU_IN)
            act.wait_ge(lru_rate, 1)
            av(LRU[:, 1, :], LRU[:, 0, :], ACT.Exp, scale=-1.0).then_inc(lru_rate, 1)
            act.wait_ge(lru_rate, 3)
            av(LRU[:, 3, :], LRU[:, 2, :], ACT.Ln).then_inc(lru_rate, 1)
            for c in range(C_LRU_GATE):
                act.wait_ge(used, B_LRU + C_LRU_IN + c + 1)
                for b in range(4):
                    n = (c % 2) * 4 + b
                    av((Y if c < 2 else T)[:, n, :], ps[:, 4 * (c % 2) + b, :], ACT.Sigmoid,
                       bias=par2("gate_b", (c // 2) * KT + n, 1)).then_inc(lru_gate, 1)
            round_run((B_LRU + C_LRU_IN + C_LRU_GATE) // RING, B_LRU + C_LRU_IN + C_LRU_GATE)
            act.wait_ge(lru_gate, 16)
            act.wait_ge(lru_rate, 5)
            for n in range(KT):
                av(Z[:, 8 + n, :], Y[:, n, :], ACT.Tanh, scale=LRU[:, 2, n:n + 1]).then_inc(lru_ea, 1)
                av(Y[:, n, :], Y[:, n, :], ACT.Exp, scale=LRU[:, 3, n:n + 1]).then_inc(lru_ea, 1)
            for n in range(KT):
                act.wait_ge(lru_q, n + 1)
                av(Z[:, 8 + n, :], Z[:, 8 + n, :], ACT.Sqrt, scale=2.0).then_inc(lru_m, 1)
            rounded(AH, Z[:, 16:24, :], lru_y, 0)
            copies(B_LRU + C_LRU_IN + C_LRU_GATE, C_LRU_OUT, N, 0, t_ready, ACT.Identity, bias=P2COL["b_out"][0])
            rms(2, N, t_ready, 4)
            tail(0)

            act.dma_start(CST2[:, 0:NCST2], a["cst2"]).then_inc(cst2_in, 16)
            rms(7, X, xr2, 3 * KT)
            copies(B_RWKV, C_RKV, Z, 0, rkv, split=False)
            LB = B_RWKV + C_RKV
            act.wait_ge(lora, 1)
            av(TW, ps[0:HD, 4, :], ACT.Tanh).then_inc(la, 1)
            act.wait_ge(used, LB + 1)
            av(TA_, ps[0:HD, 5, :], ACT.Copy).then_inc(la, 1)
            act.wait_ge(used, LB + 2)
            av(TG, ps[:, 6, :], ACT.Sigmoid).then_inc(la, 1)
            for n in range(KT):
                act.wait_ge(lora, 2 + n)
                av(N[:, n, :], ps[:, n % 4, :], ACT.Sigmoid, bias=par2("w0", n, 1)).then_inc(lw, 1)
            for n in range(KT):
                act.wait_ge(lora, 2 + KT + n)
                av(T[:, n, :], ps[:, 4 + n % 4, :], ACT.Sigmoid, bias=par2("a0", n, 1)).then_inc(la, 1)

            def root(n):
                act.wait_ge(kk_s[2], n + 1)
                if n >= 2:
                    act.wait_ge(kk_s[4], n - 1)
                av(Z[:, 26 + n % 2, :], ps[:, n % 4, :], ACT.Sqrt).then_inc(kk_s[3], 1)

            for n in range(KT):
                av(Y[:, n, :], Z[:, 8 + n, :], ACT.Copy, scale=par2("k_k", n, 1)).then_inc(kk_s[0], 1)
                if n >= 2:
                    act.wait_ge(kk_s[2], n - 1)
                av(Z[:, 24 + n % 2, :], Z[:, 8 + n, :], ACT.Square, scale=par2("k_k", n, 1)).then_inc(kk_s[1], 1)
                if n >= 1:
                    root(n - 1)
            root(KT - 1)
            act.wait_ge(cum, KT)
            av(MID[:, 1:3], MID[:, 1:3], ACT.Exp, scale=-K0).then_inc(mid_e, 1)
            act.wait_ge(kk_s[4], KT)
            with act.Fori(0, RC) as c:
                for half in range(2):
                    def lane(L):
                        return ch[L], LANES[L], 4 * L, 2 * (2 * half + L), c * 2 + half

                    for L in range(2):
                        s, B, o, n0, it = lane(L)
                        act.wait_ge(s["s"], it + 1)
                        lws = N[:, n0:n0 + 2, bass.ds(c * P, P)]
                        av(B["e"][:, :, 0, 1:P + 1], lws, ACT.Exp, scale=-K0)
                        av(B["e"][:, :, 1, 0:P], lws, ACT.Exp, scale=K0)
                        av(B["e"][:, :, 0, 0:1], MID[:, 0, n0:n0 + 2, bass.ds(c, 1)], ACT.Exp, scale=K0)
                        av(B["x"][:, 0:2, :], Z[:, 16 + n0:18 + n0, bass.ds(c * P, P)], ACT.Copy).then_inc(s["exp"], 1)
                    for L in range(2):
                        s, B, o, n0, it = lane(L)
                        act.wait_ge(s["tr"], it + 1)
                        av(B["bktok"].rearrange("p a n c -> p (a n c)"), ps[:, o, :], ACT.Copy)
                        av(B["vtok"].rearrange("p n c -> p (n c)"), ps[:, o + 1, 0:2 * P], ACT.Copy).then_inc(s["tok"], 1)
                    for L in range(2):
                        s, B, o, n0, it = lane(L)
                        act.wait_ge(s["x0"], it + 1)
                        av(B["x"].rearrange("p q t -> p (q t)"), ps[:, o + 2, :], ACT.Copy).then_inc(s["xc"], 1)
                    for v in range(LEVELS):
                        for L in range(2):
                            s, B, o, n0, it = lane(L)
                            for e, t in enumerate(("x", "xt")):
                                act.wait_ge(s["x"], it * (2 * LEVELS) + 2 * v + e + 1)
                                av(B[t].rearrange("p q t -> p (q t)"), ps[:, o + 1 + e, :], ACT.Copy).then_inc(s["xc"], 1)
                    for L in range(2):
                        s, B, o, n0, it = lane(L)
                        act.wait_ge(s["p"], it + 1)
                        for r in range(2):
                            ins = av(B["pu"][:, 0, r:4:2, :], ps[:, o + r, 0:2 * HD].rearrange("p (n i) -> p n i", n=2), ACT.Copy)
                        ins.then_inc(s["pc"], 1)
                    for L in range(2):
                        s, B, o, n0, it = lane(L)
                        act.wait_ge(s["u"], it + 1)
                        av(B["pu"][:, 1].rearrange("p q i -> p (q i)"), ps[:, o + 2, 0:4 * HD], ACT.Copy).then_inc(s["uc"], 1)
                    for L in range(2):
                        s, B, o, n0, it = lane(L)
                        act.wait_ge(s["s"], it + 2)
                        av(T[:, n0:n0 + 2, bass.ds(c * P, P)], ps[:, o + 3, 0:2 * P].rearrange("p (n t) -> p n t", n=2),
                           ACT.Copy).then_inc(s["yc"], 1)
            round_run((B_RWKV + C_RKV + C_LORA + C_G2) // RING, B_RWKV + C_RKV + C_LORA + C_G2 - 1)
            for n in range(KT):
                act.wait_ge(gn[1], n + 1)
                av(Z[:, 26 + n % 2, :], T[:, n, :], ACT.Square).then_inc(gn[2], 1)
                act.wait_ge(gn[3], n + 1)
                av(GN_STD[n % 2], ps[:, 4 * (n % 2) + 1, :], ACT.Sqrt, bias=par2("gn_eps"), scale=1.0 / HD).then_inc(gn[4], 1)
            rounded(AH, Y, gn[9], 0)
            copies(B_RWKV + C_RKV + C_LORA + C_G2, C_RWO, N, 0, t_ready)
            rms(8, N, t_ready, 4 + 32)
            tail(1)

        @block.vector
        def _(dve):
            v = nc.vector
            tt, ts, stt = v.tensor_tensor, v.tensor_scalar, v.scalar_tensor_tensor

            def remainder(lo, whole, hi, done, each=1):
                tt(lo, whole, hi, ALU.subtract).then_inc(done, each)

            def layer_norm(l, i, gain, bias, done, each):
                s, at = ln, l * 2 + i
                dve.wait_ge(s["mean"], at + 1)
                for n in range(KT):
                    tt(X[:, n, :], X[:, n, :], ps[:, 4, :], ALU.subtract).then_inc(s["xc"], 1)
                dve.wait_ge(s["std"], at + 1)
                v.reciprocal(RS[:], RS[:])
                dve.drain()
                for n in range(KT):
                    stt(X[:, n, :], X[:, n, :], par(gain, n, 1), RS[:], ALU.mult, ALU.mult).then_inc(s["y"], 1)
                for n in range(KT):
                    dve.wait_ge(s["hi"], at * KT + n + 1)
                    stt(XL[:, n, :], X[:, n, :], par(bias, n, 1), XHF[:, n, :], ALU.add, ALU.subtract).then_inc(done, each)

            def whole_residual(x, xl, xh, out, done):
                stt(x, xl.bitcast(F32), ALPHA, out, ALU.mult, ALU.add)
                dve.drain()
                stt(x, xh, ALPHA, x, ALU.mult, ALU.add).then_inc(done, 1)

            def maxima(l, u):
                W = (UNITS[u][1] + 1) * P
                dve.wait_ge(at_sc, l * NU + u + 1)
                v.tensor_reduce(AM[:, u % 2, 0, :], ps[:, 0:4, 0:W], AXX, ALU.max)
                dve.drain()
                ts(AM[:, u % 2, 1, :], AM[:, u % 2, 0, :], -SCALE, None, ALU.mult).then_inc(at_max, 1)

            def factors(l, u):
                kind, qi, which = UNITS[u]
                W = (qi + 1) * P
                dve.wait_ge(at_exp, l * NU + u + 1)
                v.reciprocal(AM[:, u % 2, 3, :], AM[:, u % 2, 2, :])
                dve.drain()
                if kind == "diff":
                    ts(AM[:, u % 2, 3, 1:4:2], AM[:, u % 2, 3, 1:4:2], LAM[:, 2 * HD + 5:2 * HD + 6], None, ALU.mult)
                    dve.drain()
                    for i in range(2):
                        b = (u % 2) * 4 + 2 * i
                        ts(PROB[:, b + 1, 0:W], PROB[:, b + 1, 0:W], AM[:, u % 2, 3, 2 * i + 1:2 * i + 2], None, ALU.mult)
                    dve.drain()
                    for i in range(2):
                        b = (u % 2) * 4 + 2 * i
                        ins = stt(PROB[:, b, 0:W], PROB[:, b, 0:W], AM[:, u % 2, 3, 2 * i:2 * i + 1], PROB[:, b + 1, 0:W], ALU.mult, ALU.add)
                    ins.then_inc(at_comb, 1)
                else:
                    tt(AM[:, u % 2, 3, :], AM[:, u % 2, 3, :], GSIG[:, qi, 1 + kind, which * HPG:which * HPG + HPG], ALU.mult)

            def turned(l, u):
                W = (UNITS[u][1] + 1) * P
                for i in range(HEADS_OF[u]):
                    t = HEADS_BEFORE[u] + i
                    dve.wait_ge(at_tr, l * NHEADS + t + 1)
                    if t >= 4:
                        dve.wait_ge(at_av, l * NHEADS + t - 3)
                    v.tensor_copy(PT[:, t % 4, 0:W], ps[:, 4 + t % 2, 0:W]).then_inc(at_pt, 1)

            def outputs(l, u):
                kind, qi, which = UNITS[u]
                dve.wait_ge(at_av, l * NHEADS + HEADS_BEFORE[u + 1])
                if kind == "diff":
                    v.tensor_copy(YB[:, qi, 2 * which:2 * which + 2, :],
                                  ps[:, 6 + u % 2, 0:2 * P].rearrange("p (h d) -> p h d", h=2)).then_inc(at_out, 1)
                else:
                    o = RS[:, 0:HPG * HD].rearrange("p (h d) -> p h d", h=HPG)
                    tt(o, ps[:, 6 + u % 2, 0:HPG * HD].rearrange("p (h d) -> p h d", h=HPG),
                       AM[:, u % 2, 3, :].unsqueeze(2).to_broadcast([P, HPG, HD]), ALU.mult)
                    dve.drain()
                    y = YC[:, qi, which * HPG:which * HPG + HPG, :]
                    tt(y, y, o, ALU.add).then_inc(at_out, 1)

            for n in range(KT):
                dve.wait_ge(x0_hi, n + 1)
                remainder(XL[:, n, :], X[:, n, :], XHF[:, n, :], x_ready, 2)
            dve.wait_ge(cst_in, 16)
            with dve.Fori(0, DEPTH) as l:
                C = l * CPL
                dve.wait_ge(par_in, l * 16 + 16)
                lam4 = par("lam").rearrange("p (a b d) -> p a b d", a=2, b=2)
                tt(LAM[:, 0:2 * HD].rearrange("p (a d) -> p a d", a=2), lam4[:, :, 0, :], lam4[:, :, 1, :], ALU.mult)
                dve.drain()
                v.tensor_reduce(LAM[:, 2 * HD:2 * HD + 2], LAM[:, 0:2 * HD].rearrange("p (a d) -> p a d", a=2), AXX, ALU.add).then_inc(lam_d, 1)
                ts(LAM[:, 2 * HD + 6:2 * HD + 7], par("subln"), par("lam_keep"), None, ALU.mult)
                for r, t in enumerate(ROPE_TILES):
                    dve.wait_ge(rot, l * NR + r + 1)
                    tt(SCR[:, 4 + r % 2, :], ps[:, r % 4, :], cst("sin"), ALU.mult)
                    tt(Z[:, t, :], Z[:, t, :], cst("cos"), ALU.mult)
                    dve.drain()
                    tt(Z[:, t, :], Z[:, t, :], SCR[:, 4 + r % 2, :], ALU.add).then_inc(rope, 1)
                    if t == Z_KC:
                        dve.drain()
                        for kv in range(2):
                            for half in range(2):
                                p0 = PCOL["pos"][0] + kv * CMP_BLOCK + half * CMP_STRIDE
                                tt(SCR[:, 2 * kv + half, :].rearrange("p (n s) -> p n s", s=CMP_STRIDE),
                                   Z[:, Z_KC + kv, :].rearrange("p (n s) -> p n s", s=CMP_STRIDE),
                                   PAR[:, p0:p0 + CMP_STRIDE].unsqueeze(1).to_broadcast([P, S // CMP_STRIDE, CMP_STRIDE]),
                                   ALU.add).then_inc(cmpin, 1)
                dve.drain()
                for c in range(4):
                    tt(SCR[:, 4 + c, :], Z[:, Z_AC + c, :], Z[:, Z_AV + c, :], ALU.mult)
                dve.drain()
                for c in range(4):
                    ts(Y[:, c, :], SCR[:, 4 + c, :], par("conv_a", 8 + c, 1), None, ALU.mult)
                for k in (1, 0):
                    dve.drain()
                    for c in range(4):
                        y = Y[:, c, 2 - k:S]
                        stt(y, SCR[:, 4 + c, 0:S - 2 + k], par("conv_a", 4 * k + c, 1), y, ALU.mult, ALU.add)
                dve.drain()
                for c in range(4):
                    tt(Y[:, c, :], Y[:, c, :], Z[:, Z_AB + c, :], ALU.mult).then_inc(conv_out, 1)
                dve.wait_ge(phio, l + 1)
                for g in range(NG):
                    o = g * HD
                    v.tensor_copy(KCC[o:o + HD, 0:NCMP], ps[o:o + HD, 4, g * 32:g * 32 + NCMP])
                v.tensor_copy(VCC[0:NCMP, :, :], ps[0:NCMP, 5, 0:NG * HD].rearrange("p (g d) -> p g d", g=NG)).then_inc(cmpkv, 1)
                dve.wait_ge(lam_e, l + 1)
                tt(LAM[:, 2 * HD + 4:2 * HD + 5], LAM[:, 2 * HD + 3:2 * HD + 4], LAM[:, 2 * HD + 2:2 * HD + 3], ALU.subtract)
                dve.drain()
                tt(LAM[:, 2 * HD + 5:2 * HD + 6], LAM[:, 2 * HD + 4:2 * HD + 5], par("lam_init"), ALU.subtract)
                dve.wait_ge(cs_step, l * 4 + 1)
                cm = cst("cmask").rearrange("p (t n) -> p t n", t=ST)
                cv = cst("cvalid").rearrange("p (t n) -> p t n", t=ST)
                for qi in range(ST):
                    for g in range(NG):
                        tt(CS[:, qi, g * HPG:g * HPG + HPG, :],
                           ps[:, g, qi * P:qi * P + P].rearrange("p (h n) -> p h n", h=HPG)[:, :, 0:NCMP],
                           cm[:, qi].unsqueeze(1).to_broadcast([P, HPG, NCMP]), ALU.add)
                dve.drain()
                csf = CS[:].rearrange("p t h n -> p (t h) n")
                v.tensor_reduce(CM[:, 0, :], csf, AXX, ALU.max)
                dve.drain()
                tt(csf, csf, CM[:, 0, :].unsqueeze(2).to_broadcast([P, ST * NH, NCMP]), ALU.subtract).then_inc(cs_step, 1)
                dve.wait_ge(cs_step, l * 4 + 3)
                v.tensor_reduce(CM[:, 1, :], csf, AXX, ALU.add)
                dve.drain()
                for qi in range(ST):
                    ins = tt(CS[:, qi], CS[:, qi], cv[:, qi].unsqueeze(1).to_broadcast([P, NH, NCMP]), ALU.mult)
                ins.then_inc(cs_step, 1)
                v.reciprocal(CM[:, 2, :], CM[:, 1, :])
                dve.drain()
                dve.wait_ge(gsig, l + 1)
                tt(CM[:, 3, :].rearrange("p (t h) -> p t h", t=ST), CM[:, 2, :].rearrange("p (t h) -> p t h", t=ST), GSIG[:, :, 0, :], ALU.mult)
                dve.drain()
                for qi in range(ST):
                    dve.wait_ge(cs_av, l * ST + qi + 1)
                    tt(YC[:, qi], ps[:, qi % 2, :].rearrange("p (h d) -> p h d", h=NH),
                       CM[:, 3, qi * NH:qi * NH + NH].unsqueeze(2).to_broadcast([P, NH, HD]), ALU.mult).then_inc(cs_out, 1)
                dve.drain()
                maxima(l, 0)
                for u in range(NU):
                    factors(l, u)
                    if u + 1 < NU:
                        maxima(l, u + 1)
                    turned(l, u)
                    outputs(l, u)
                dve.wait_ge(yb_step, l * 4 + 1)
                v.tensor_reduce(MS[:, 0, :], SCR[:, 0:4, :].rearrange("p t (h d) -> p (t h) d", h=DH), AXX, ALU.add).then_inc(yb_step, 1)
                for c in range(4):
                    dve.wait_ge(y_hi, l * 12 + c + 1)
                    remainder(YL[:, c, :], Y[:, c, :], YHF[:, c, :], y_lo)
                dve.wait_ge(yb_step, l * 4 + 3)
                v.reciprocal(MS[:, 1, :], MS[:, 1, :])
                dve.drain()
                ybf = YB.rearrange("p t h d -> p (t h) d")
                tt(ybf, ybf, MS[:, 1, :].unsqueeze(2).to_broadcast([P, ST * DH, P]), ALU.mult).then_inc(yb_step, 1)
                v.memset(M, 0.0)
                for c in range(8):
                    dve.wait_ge(y_hi, l * 12 + 4 + c + 1)
                    if c < 4:
                        remainder(YL[:, 8 + c, :], ps[:, c, :], YHF[:, 8 + c, :], y_lo)
                    else:
                        stt(YL[:, c, :], ps[:, c, :], LAM[:, 2 * HD + 6:2 * HD + 7], YHF[:, c, :], ALU.mult, ALU.subtract).then_inc(y_lo, 1)
                dve.drain()
                with dve.Fori(0, 3) as b:
                    for n in range(KT):
                        dve.wait_ge(sg, l * 24 + b * 8 + (n + 5))
                        dve.wait_ge(used, C + B_MERGE + b * 12 + 3 * (n // 2) + 3)
                        tt(T1[:, 4 + n % 4, :], T1[:, n % 4, :], ps[:, 4 + n % 4, :], ALU.mult)
                        dve.drain()
                        tt(M[:, n, :], M[:, n, :], T1[:, 4 + n % 4, :], ALU.add).then_inc(mg, 1)
                for n in range(KT):
                    dve.wait_ge(m_hi, l * KT + n + 1)
                    remainder(ML[:, n, :], M[:, n, :], MRF[:, n, :], m_lo)
                with dve.Fori(0, 2) as i:
                    for j in range(RING):
                        dve.wait_ge(used, C + B_WO + i * RING + (j + 1))
                        t = bass.ds(i * RING + j, 1)
                        whole_residual(X[:, t, :], XL[:, t, :], XHF[:, t, :], ps[:, j:j + 1, :], x1pre)
                dve.drain()
                layer_norm(l, 0, "ln1_g", "ln1_b", x1, 1)
                with dve.Fori(0, C_UP // RING) as i:
                    for e in range(2):
                        for b in range(2):
                            j = 2 * e + b
                            dve.wait_ge(up_a, l * C_UP + i * RING + (j + 1))
                            f = i * 2 + (e + b * FT)
                            for k in (1, 0):
                                y = T1[:, j, 2 - k:S]
                                ins = stt(y, ps[:, j, 0:S - 2 + k], PAR[:, bass.ds(f + (PCOL["up_w"][0] + k * 2 * FT), 1)], y, ALU.mult, ALU.add)
                                if k:
                                    dve.drain()
                            ins.then_inc(up_c, 1)
                        dve.drain()
                        dve.wait_ge(up_g, l * FT + i * 2 + (e + 1))
                        t = bass.ds(i * 2 + e, 1)
                        tt(FH[:, t, :], T1[:, 4 + e:5 + e, :], T1[:, 2 * e + 1:2 * e + 2, :], ALU.mult)
                        dve.drain()
                        v.tensor_copy(FHR[:, t, :], FH[:, t, :])
                        dve.drain()
                        remainder(FL[:, t, :], FH[:, t, :], FHRF[:, t, :], up_h)
                with dve.Fori(0, 2) as i:
                    for n in range(4):
                        dve.wait_ge(used, C + B_DOWN + i * 12 + 3 * (n + 1))
                        t = bass.ds(i * 4 + n, 1)
                        whole_residual(X[:, t, :], XL[:, t, :], XHF[:, t, :], ps[:, n:n + 1, :], x2pre)
                dve.drain()
                layer_norm(l, 1, "ln2_g", "ln2_b", x_ready, 2)

            def inverse_root(i, cols=S):
                dve.wait_ge(rms_std, i + 1)
                v.reciprocal(RS[:, 0:cols], RS[:, 0:cols])
                dve.drain()

            def rms(i, src, dst, gain, cols=S):
                inverse_root(i, cols)
                for n in range(KT):
                    stt(dst[:, n, :], src[:, n, :], gain[:, n:n + 1], RS[:, 0:cols], ALU.mult, ALU.mult).then_inc(rms_y, 1)

            def residual(i, gain):
                inverse_root(i)
                for n in range(KT):
                    stt(T[:, n, :], N[:, n, :], gain[:, n:n + 1], RS[:], ALU.mult, ALU.mult)
                dve.drain()
                for n in range(KT):
                    tt(X[:, n, :], X[:, n, :], T[:, n, :], ALU.add).then_inc(xr2, 1)
                dve.drain()

            def remainders(lo, whole, base):
                for n in range(KT):
                    dve.wait_ge(src_hi, base + n + 1)
                    remainder(lo[:, n, :], whole[:, n, :], XHF[:, n, :], src_lo)

            def gain(l, i):
                return par2("ln", (l * 6 + i) * KT, KT)

            def tail(l):
                dve.wait_ge(mem_hi, l + 1)
                remainder(MNL, MN, MNHF, mem_lo)
                rms(3 + 6 * l, X, N, gain(l, 2))
                remainders(NL, N, SRC[f"q{l}"])

                def maxima2(qi):
                    dve.wait_ge(m_sc, l * ST + qi + 1)
                    v.tensor_reduce(AM[:, qi % 2, 0, :], ps[:, 2 * (qi % 2):2 * (qi % 2) + 2, :].rearrange("p b (h s) -> p (b h) s", h=2),
                                    AXX, ALU.max)
                    dve.drain()
                    ts(AM[:, qi % 2, 1, :], AM[:, qi % 2, 0, :], -((MT * P) ** -0.5), None, ALU.mult).then_inc(m_max, 1)

                maxima2(0)
                for qi in range(ST):
                    if qi + 1 < ST:
                        maxima2(qi + 1)
                    dve.wait_ge(m_exp, l * ST + qi + 1)
                    v.reciprocal(AM[:, qi % 2, 3, :], AM[:, qi % 2, 2, :])
                    dve.drain()
                    p = MP[:, qi % 2]
                    tt(p, p, AM[:, qi % 2, 3, :].unsqueeze(2).to_broadcast([P, MH, S2]), ALU.mult).then_inc(m_p, 1)
                for c in range(KT):
                    dve.wait_ge(src_hi, SRC[f"o{l}"] + c + 1)
                    remainder(YL[:, c, :], ps[:, c % 4, :], XHF[:, c, :], src_lo)
                residual(4 + 6 * l, gain(l, 3))
                rms(5 + 6 * l, X, N, gain(l, 4))
                remainders(NL, N, SRC[f"up{l}"])
                for h in range(2):
                    with dve.Fori(0, C_HUP // RING) as i:
                        for j in range(RING):
                            dve.wait_ge(mup_r, i * RING + (l * F2T + h * HALF + j + 1))
                            r, t = RELU[:, j:j + 1, :], bass.ds(i * RING + j, 1)
                            tt(HW[:, t, :], r, r, ALU.mult)
                            dve.drain()
                            v.tensor_copy(HR[:, t, :], HW[:, t, :])
                            dve.drain()
                            remainder(HL[:, t, :], HW[:, t, :], HRF[:, t, :], mup)
                U = B_TAIL0 if l == 0 else B_TAIL1
                for n in range(KT):
                    dve.wait_ge(used, U + C_TAIL - C_HDN + 2 * n + 2)
                    tt(N[:, n, :], PART[:, n, :], ps[:, n % 4, :], ALU.add).then_inc(t_ready, 1)
                residual(6 + 6 * l, gain(l, 5))

            for n in range(KT):
                dve.wait_ge(x_ready, 16 * DEPTH + 2 * n + 2)
                tt(X[:, n, :], XL[:, n, :].bitcast(F32), XHF[:, n, :], ALU.add).then_inc(xr2, 1)
            dve.drain()
            dve.wait_ge(par2_in, 16)
            rms(0, MN, MN, par2("mem_norm"), S2)
            rms(1, X, N, gain(0, 0))
            remainders(NL, N, SRC["lru_in"])
            for n0 in (0, 4):
                dve.wait_ge(lru_in, 4 + KT + n0 + 4)
                for n in range(n0, n0 + 4):
                    ts(Z[:, 16 + n, :], Z[:, 8 + n, :], par2("conv_w", 3 * KT + n, 1), par2("conv_b", n, 1), ALU.mult, ALU.add)
                for k in (2, 1, 0):
                    dve.drain()
                    for n in range(n0, n0 + 4):
                        y = Z[:, 16 + n, 3 - k:S]
                        ins = stt(y, Z[:, 8 + n, 0:S - 3 + k], par2("conv_w", k * KT + n, 1), y, ALU.mult, ALU.add)
                        if k == 0:
                            ins.then_inc(lru_conv, 1)
            dve.drain()
            lam = par2("lam")
            ts(LRU[:, 2, :], lam, -1.0, None, ALU.mult)
            dve.drain()
            tt(LRU[:, 0, :], lam, LRU[:, 2, :], ALU.max).then_inc(lru_rate, 1)
            dve.wait_ge(lru_rate, 2)
            e, u, d, low = LRU[:, 1, :], LRU[:, 2, :], LRU[:, 0, :], LAM[:, 0:KT]
            ts(u, e, 1.0, None, ALU.add).then_inc(lru_rate, 1)
            dve.drain()
            ts(d, u, -1.0, 1e-30, ALU.add, ALU.max)
            ts(low, e, -0.5, 1.0, ALU.mult, ALU.add)
            dve.drain()
            v.reciprocal(d, d)
            tt(low, low, e, ALU.mult)
            dve.drain()
            tt(d, d, e, ALU.mult)
            dve.wait_ge(lru_rate, 4)
            dve.drain()
            tt(d, d, LRU[:, 3, :], ALU.mult)
            ts(u, lam, -1.0, 0.0, ALU.mult, ALU.max)
            dve.drain()
            tt(d, d, low, ALU.max)
            dve.drain()
            tt(d, d, u, ALU.add)
            dve.drain()
            ts(LRU[:, 2, :], d, LRU_C, None, ALU.mult)
            ts(LRU[:, 3, :], d, -LRU_C, None, ALU.mult).then_inc(lru_rate, 1)
            dve.drain()
            dve.wait_ge(lru_gate, 16)
            for n in range(KT):
                tt(T[:, n, :], T[:, n, :], Z[:, 16 + n, :], ALU.mult)
            for n0 in (0, 4):
                dve.drain()
                for n in range(n0, n0 + 4):
                    dve.wait_ge(lru_ea, 2 * n + 1)
                    ts(Z[:, 24 + n % 4, :], Z[:, 8 + n, :], 1.0, None, ALU.add)
                dve.drain()
                for n in range(n0, n0 + 4):
                    v.reciprocal(Z[:, 24 + n % 4, :], Z[:, 24 + n % 4, :])
                dve.drain()
                for n in range(n0, n0 + 4):
                    tt(Z[:, 8 + n, :], Z[:, 8 + n, :], Z[:, 24 + n % 4, :], ALU.mult).then_inc(lru_q, 1)
            for n0 in (0, 4):
                dve.drain()
                for n in range(n0, n0 + 4):
                    dve.wait_ge(lru_m, n + 1)
                    tt(T[:, n, :], T[:, n, :], Z[:, 8 + n, :], ALU.mult)
                dve.drain()
                for n in range(n0, n0 + 4):
                    v.tensor_tensor_scan(Z[:, 16 + n, :], Y[:, n, :], T[:, n, :], 0.0, ALU.mult, ALU.add)
                dve.drain()
                for n in range(n0, n0 + 4):
                    tt(Z[:, 16 + n, :], Z[:, 16 + n, :], Z[:, n, :], ALU.mult).then_inc(lru_y, 1)
            remainders(ZL2[:, 16:24, :], Z[:, 16:24, :], SRC["lru_out"])
            residual(2, gain(0, 1))
            tail(0)

            v.memset(STATE, 0.0)
            rms(7, X, N, gain(1, 0))
            dve.drain()
            tt(Y[:, 0:KT, 1:S], N[:, :, 0:S - 1], N[:, :, 1:S], ALU.subtract)
            ts(Y[:, 0:KT, 0:1], N[:, :, 0:1], -1.0, None, ALU.mult)
            dve.drain()
            for m, mu in enumerate((0, 2, 3, 1, 4, 5)):
                if 2 <= m < 5:
                    dve.wait_ge(used, B_RWKV + (m - 1) * KT)
                elif m == 5:
                    dve.wait_ge(lora, 1)
                for n in range(KT):
                    stt(MIX[m % 2][n], Y[:, n, :], par2("mu", mu * KT + n, 1), N[:, n, :], ALU.mult, ALU.add).then_inc(mix, 1)
            dve.wait_ge(cst2_in, 16)
            for n in range(KT):
                dve.wait_ge(lw, n + 1)
                t = YCF[:, 2 + n % 2, :]
                v.tensor_tensor_scan(t, cst2("reset"), N[:, n, :], 0.0, ALU.mult, ALU.add)
                dve.drain()
                t4 = t.rearrange("p (c t) -> p c t", c=RC)
                v.tensor_copy(MID[:, 0:2, n, :], t4[:, :, P // 2 - 1].unsqueeze(1).to_broadcast([P, 2, RC]))
                tt(MID[:, 2, n, :], t4[:, :, P - 1], t4[:, :, P // 2 - 1], ALU.subtract)
                tt(N[:, n, :].rearrange("p (c t) -> p c t", c=RC), t4, t4[:, :, P // 2 - 1:P // 2].to_broadcast([P, RC, P]),
                   ALU.subtract).then_inc(cum, 1)
            for n in range(KT):
                dve.wait_ge(kk_s[3], n + 1)
                dve.wait_ge(la, 3 + n + 1)
                r = Z[:, 26 + n % 2, :]
                ts(r, r, 1e-12, None, ALU.max)
                ts(YCF[:, n % 2, :], T[:, n, :], 1.0, par2("k_a", n, 1), ALU.subtract, ALU.mult)
                dve.drain()
                v.reciprocal(r, r)
                stt(Z[:, 8 + n, :], YCF[:, n % 2, :], 1.0, Z[:, 8 + n, :], ALU.add, ALU.mult)
                dve.drain()
                tt(Y[:, n, :], Y[:, n, :], r, ALU.mult)
                dve.drain()
                tt(T[:, n, :], T[:, n, :], Y[:, n, :], ALU.mult).then_inc(kk_s[4], 1)
            dve.wait_ge(mid_e, 1)
            dve.drain()
            pair = cst2("pair").rearrange("p (a t) -> p a t", a=2).unsqueeze(1).to_broadcast([P, 2, 2, P])
            ident4 = cst("ident").unsqueeze(1).to_broadcast([P, 4, P])

            def level(i):
                return cst2("levels", i * P, P).unsqueeze(1).to_broadcast([P, 4, P])

            with dve.Fori(0, RC) as c:
                for half in range(2):
                    def lane(L):
                        return ch[L], LANES[L], 4 * L, 2 * (2 * half + L), c * 2 + half

                    for L in range(2):
                        s, B, o, n0, it = lane(L)
                        dve.wait_ge(s["exp"], it + 1)
                        e, tsl = B["e"], bass.ds(c * P, P)
                        stt(B["ar"][:, :, 0, :], Y[:, n0:n0 + 2, tsl], -1.0, e[:, :, 0, 0:P], ALU.mult, ALU.mult)
                        tt(B["ar"][:, :, 1, :], Z[:, n0:n0 + 2, tsl], e[:, :, 0, 1:P + 1], ALU.mult)
                        tt(B["bk"][:, 0], T[:, n0:n0 + 2, tsl], e[:, :, 1, 0:P], ALU.mult)
                        tt(B["sh"], STATE[:, n0:n0 + 2, :], MID[:, 1, n0:n0 + 2, bass.ds(c, 1)].to_broadcast([P, 2, HD]), ALU.mult)
                        tt(B["bk"][:, 1], Z[:, 8 + n0:10 + n0, tsl], e[:, :, 1, 0:P], ALU.mult).then_inc(s["hat"], 1)
                    for L in range(2):
                        s, B, o, n0, it = lane(L)
                        dve.wait_ge(s["g1"], it + 1)
                        for r in range(2):
                            tt(B["g1"][:, r:4:2], ps[:, o + 2 + r, :].rearrange("p (n a t) -> p n a t", n=2, a=2), pair, ALU.mult)
                        dve.drain()
                        tt(B["g1"][:, :, 0, :], B["g1"][:, :, 0, :], ident4, ALU.add)
                        dve.drain()
                        tt(B["xt"], B["g1"][:, :, 0, :], level(0), ALU.mult).then_inc(s["x0t"], 1)
                    for L in range(2):
                        s, B, o, n0, it = lane(L)
                        dve.wait_ge(s["g2"], it + 1)
                        for r in range(2):
                            ins = tt(B["g2"][:, r:4:2], ps[:, o + r, :].rearrange("p (n a t) -> p n a t", n=2, a=2), pair, ALU.mult)
                        ins.then_inc(s["g2m"], 1)
                    for k in range(LEVELS):
                        for L in range(2):
                            s, B, o, n0, it = lane(L)
                            dve.wait_ge(s["z"], it * LEVELS + k + 1)
                            tt(B["z"], ps[:, o, :].rearrange("p (q t) -> p q t", q=4), level(k + 1), ALU.mult).then_inc(s["zm"], 1)
                    for L in range(2):
                        s, B, o, n0, it = lane(L)
                        dve.wait_ge(s["s"], it + 2)
                        for r in (0, HD):
                            tt(STATE[r:r + HD, n0:n0 + 2, :], ps[r:r + HD, o, 0:2 * P].rearrange("p (n i) -> p n i", n=2)[:, :, r:r + HD],
                               B["sh"][r:r + HD], ALU.add)
                        dve.drain()
                        st = STATE[:, n0:n0 + 2, :]
                        tt(st, st, MID[:, 2, n0:n0 + 2, bass.ds(c, 1)].to_broadcast([P, 2, HD]), ALU.mult).then_inc(s["sc"], 1)
                    dve.drain()
            for n in range(KT):
                o = 4 * (n % 2)
                dve.wait_ge(gn[0], n + 1)
                stt(T[:, n, :], ps[:, o, :], -1.0 / HD, T[:, n, :], ALU.mult, ALU.add).then_inc(gn[1], 1)
                if n >= 2:
                    dve.wait_ge(gn[7], n - 1)
                stt(Z[:, 24 + n % 2, :], Z[:, n, :], par2("r_k", n, 1), Z[:, 8 + n, :], ALU.mult, ALU.mult).then_inc(gn[5], 1)
                dve.wait_ge(gn[7], n + 1)
                tt(GN_BONUS[n % 2], Z[:, 16 + n, :], ps[:, o + 2, :], ALU.mult)
                dve.wait_ge(gn[4], n + 1)
                v.reciprocal(GN_STD[n % 2], GN_STD[n % 2])
                dve.drain()
                stt(T[:, n, :], T[:, n, :], par2("gn_g", n, 1), GN_STD[n % 2], ALU.mult, ALU.mult)
                dve.drain()
                stt(T[:, n, :], T[:, n, :], par2("gn_b", n, 1), GN_BONUS[n % 2], ALU.add, ALU.add)
                dve.drain()
                dve.wait_ge(gn[8], n + 1)
                tt(Y[:, n, :], T[:, n, :], ps[:, o + 3, :], ALU.mult).then_inc(gn[9], 1)
            remainders(YL, Y, SRC["rwo"])
            residual(8, gain(1, 1))
            tail(1)

        @block.gpsimd
        def _(pool):
            def remainders(split, quads):
                with pool.Fori(0, quads) as i:
                    for j in range(RING):
                        pool.wait_ge(w_hi, split + i * RING + (j + 1))
                        nc.gpsimd.tensor_tensor(RL[:, j, :], ring[:, j, :], RH[:, j, :].bitcast(F32), ALU.subtract).then_inc(w_lo, 1)

            with pool.Fori(0, DEPTH) as l:
                remainders(l * SPL, B_PHI // RING)
                remainders(l * SPL + B_PHI, (CPL - B_MERGE) // RING)
            for first, n in SPLIT_RUNS:
                remainders(n_split(first), n // RING)


def _tiles(w):
    k, n = w.shape
    return w.reshape(k // P, P, n // P, P).transpose(2, 1, 0, 3)


def _blocks(w, nk):
    t = _tiles(w)
    t = np.concatenate([t, np.zeros((t.shape[0], P, nk - t.shape[2], P), w.dtype)], axis=2) if nk > t.shape[2] else t
    return t.reshape(t.shape[0], P, nk * P)


def _rows(w):
    k, n = w.shape
    full = np.zeros((k, 512), w.dtype)
    full[:, :n] = w
    return full.reshape(k // 256, 2, P, 512).transpose(0, 2, 1, 3).reshape(k // 256, P, CHUNK)


def _chunks(t):
    return t.reshape(-1, P, CHUNK) if t.shape[2] == CHUNK else \
        t.reshape(t.shape[0], P, t.shape[2] // CHUNK, CHUNK).transpose(0, 2, 1, 3).reshape(-1, P, CHUNK)


def _cols(v):
    return v.reshape(-1, P).T


def first_weights(i, l):
    w = i["w_in"][l]
    col = lambda s, n: w[:, s:s + n]
    q = col(3072, 512).reshape(D, NG, HPG, HD).transpose(0, 2, 1, 3).reshape(D, 512)
    kv = col(3584, 768).reshape(D, 6, P)
    g = col(4352, 24).reshape(D, NH, 3).transpose(0, 2, 1).reshape(D, 24)
    zw = np.concatenate([col(0, 1536), col(1536, 1024), q, kv[:, 0], kv[:, 1], kv[:, 2], kv[:, 4]], axis=1)
    out = [_chunks(_blocks(zw, KT)), _rows(col(2560, 512)), _rows(np.concatenate([kv[:, 3], kv[:, 5], g], axis=1))]
    phi = i["nsa_phi_w1"][l].reshape(2, 4, 8, HD, P).transpose(0, 1, 3, 2, 4).reshape(8, HD, CHUNK)
    out.append(np.concatenate([phi, phi], axis=1))
    for b in range(3):
        gates = _blocks(col(4376 + b * D, D), KT)
        br = _tiles(i["w_branch"][l][b]).reshape(4, 2, P, 4 * P).transpose(0, 2, 1, 3).reshape(4, P, CHUNK)
        for p in range(4):
            out += [gates[2 * p:2 * p + 2], br[p:p + 1]]
    out.append(_blocks(i["w_o"][l], KT))
    up = _blocks(i["ffn_w_up"][l], KT)
    out.append(up.reshape(2, FT, P, CHUNK).transpose(1, 0, 2, 3).reshape(2 * FT, P, CHUNK))
    out.append(_chunks(_blocks(i["ffn_w_down"][l], 24)))
    return np.concatenate(out)


def first_params(i, l):
    lam_init = 0.8 - 0.6 * math.exp(-0.3 * l)
    f = np.float32
    part = {
        "conv_a": _cols(i["conv_a_w"][l]), "subln": _cols(i["diff_subln"][l]),
        "ln1_g": _cols(i["ln1_g"][l]), "ln1_b": _cols(i["ln1_b"][l]),
        "ln2_g": _cols(i["ln2_g"][l]), "ln2_b": _cols(i["ln2_b"][l]),
        "up_w": _cols(i["ffn_conv_w"][l]), "up_b": _cols(i["ffn_conv_b"][l]),
        "pos": np.tile(i["nsa_cmp_pos"][l].transpose(2, 0, 1).reshape(HD, 2 * CMP_BLOCK), (2, 1)),
        "phi_w2k": np.tile(i["nsa_phi_w2"][l][0], (1, 2)), "phi_w2v": i["nsa_phi_w2"][l][1],
        "lam": np.tile(i["diff_lambda"][l].reshape(1, 4 * HD), (P, 1)),
        "lam_init": np.full((P, 1), lam_init, f), "lam_keep": np.full((P, 1), 1.0 - lam_init, f),
    }
    return np.concatenate([part[n] for n in PCOL], axis=1)


def second_weights(i):
    lin = lambda w: _chunks(_blocks(w, KT))
    zeros = lambda n: np.zeros((n, P, CHUNK), np.float32)

    def rows(w):
        return [_rows(w[:, h * 512:h * 512 + 512]) for h in range(2)]

    def tail(l):
        kv = i["c_w_kv_2"][l]
        up = lin(i["m_w_up_2"][l])
        down = _blocks(i["m_w_down_2"][l], F2T).reshape(KT, P, 2, 2, CHUNK).transpose(2, 0, 3, 1, 4).reshape(2, C_HDN, P, CHUNK)
        return [lin(i["c_w_q_2"][l]), lin(kv[:, :D]), *rows(kv[:, D:]), lin(i["c_w_o_2"][l]),
                up[:HALF], down[0], up[HALF:], down[1]]

    gate = i["a_gate_w_2"][0].reshape(2, 2, 2, 2, P, 2, P).transpose(0, 1, 4, 2, 5, 3, 6).reshape(4, P, CHUNK)
    out = [lin(i["a_w_in_2"][0]), gate, lin(i["a_w_out_2"][0]), *tail(0)]
    out += [lin(i["b_w_rkv_2"][0][m]) for m in range(3)]
    thin = lambda w: w.reshape(KT, P, HD).transpose(1, 0, 2).reshape(P, KT * HD)
    tall = lambda w: np.concatenate([w, np.zeros((P - HD, D), w.dtype)])
    out.append(np.concatenate([thin(i["b_w1_2"][0]), thin(i["b_a1_2"][0])], axis=1)[None])
    out += [lin(i["b_g1_2"][0]), tall(i["b_w2_2"][0])[None], tall(i["b_a2_2"][0])[None], zeros(3), i["b_g2_2"][0][None]]
    return np.concatenate(out + [lin(i["b_w_o_2"][0]), *tail(1)])


def second_params(i):
    f = np.float32
    part = {
        "ln": _cols(i["ln_gains_2"]), "mem_norm": _cols(i["mem_norm_2"]), "conv_w": _cols(i["a_conv_w_2"]),
        "conv_b": _cols(i["a_conv_b_2"]), "b_in": _cols(i["a_b_in_2"]), "gate_b": _cols(i["a_gate_b_2"]),
        "lam": _cols(i["a_lambda_2"]), "b_out": _cols(i["a_b_out_2"]), "mu": _cols(i["b_mu_2"]),
        "w0": _cols(i["b_w0_2"]), "a0": _cols(i["b_a0_2"]), "k_k": _cols(i["b_k_k_2"]), "k_a": _cols(i["b_k_a_2"]),
        "r_k": _cols(i["b_r_k_2"]), "gn_g": _cols(i["b_gn_g_2"]), "gn_b": _cols(i["b_gn_b_2"]),
        "rms_eps": np.full((P, 1), RMS_EPS, f), "gn_eps": np.full((P, 1), GN_EPS, f),
    }
    return np.concatenate([part[n] for n in P2COL], axis=1)


def second_constants():
    f = np.float32
    k = np.arange(P)
    r, c = k[:, None], k[None, :]
    pair = np.concatenate([(r < c), (r <= c)], axis=1)
    eye = r == c
    levels = [(r // 2 == c // 2) & (r < c) | eye]
    for v in range(1, LEVELS + 1):
        b = 1 << v
        levels.append((r // (2 * b) == c // (2 * b)) & (r // b > c // b) | eye)
    part = {
        "pair": pair, "levels": np.concatenate(levels, axis=1), "reset": np.tile((np.arange(S) % P != 0)[None], (P, 1)),
        "ones": r // HD == c // HD,
    }
    return np.concatenate([part[n] for n in C2COL], axis=1).astype(f)


def constants():
    f = np.float32
    pos = np.arange(S, dtype=f)
    inv = (np.float32(500000.0) ** (-np.arange(0, 16, 2, dtype=f) / f(16))).astype(f)
    ang = (pos[:, None] * inv[None, :]).astype(f)
    cos, sin = np.ones((P, S), f), np.zeros((P, S), f)
    rot = np.zeros((P, P), f)
    for h in range(2):
        for d in range(8):
            a0, a1 = h * HD + d, h * HD + 8 + d
            cos[a0], cos[a1] = np.cos(ang[:, d]), np.cos(ang[:, d])
            sin[a0], sin[a1] = np.sin(ang[:, d]), np.sin(ang[:, d])
            rot[a1, a0], rot[a0, a1] = -1.0, 1.0
    t = np.arange(S).reshape(ST, P).T[:, :, None]
    valid = (np.arange(NCMP) * CMP_STRIDE + CMP_BLOCK - 1)[None, None, :] <= t
    k = np.arange(P)
    part = {
        "ident": np.eye(P, dtype=f), "rot": rot, "maskneg": np.where(k[None, :] > k[:, None], f(NEG), f(0)),
        "mean": np.full((P, P), 1.0 / D, f), "cmask": np.where(valid, f(0), f(NEG)).reshape(P, -1),
        "cvalid": valid.astype(f).reshape(P, -1), "cos": cos, "sin": sin, "eps": np.full((P, 1), LN_EPS, f),
    }
    return np.concatenate([part[n] for n in CCOL], axis=1).astype(f)


def kernel(**inputs):
    import concourse.bacc as bacc
    from concourse.bass_utils import run_bass_kernel_spmd

    i = {k: np.asarray(v) for k, v in inputs.items()}
    nc = bacc.Bacc("TRN2", target_bir_lowering=False, num_devices=1)
    arrays = {
        "x": i["x"][0].T.reshape(KT, P, S).transpose(1, 0, 2),
        "weights": np.concatenate([first_weights(i, l) for l in range(DEPTH)] + [second_weights(i)]),
        "par": np.stack([first_params(i, l) for l in range(DEPTH)]),
        "cst": constants(), "par2": second_params(i), "cst2": second_constants(),
        "mem": i["mem_2"][0].T.reshape(KT, P, S2).transpose(1, 0, 2),
    }
    arrays = {k: np.ascontiguousarray(v) for k, v in arrays.items()}
    aps = {k: nc.dram_tensor(f"in_{k}", v.shape, F32, kind="ExternalInput").ap() for k, v in arrays.items()}
    out = nc.dram_tensor("out_x", (P, KT, S), F32, kind="ExternalOutput").ap()
    build(nc, aps, out)
    r = run_bass_kernel_spmd(nc, [{f"in_{k}": v for k, v in arrays.items()}], core_ids=[0])
    return np.ascontiguousarray(r.results[0]["out_x"].transpose(1, 0, 2).reshape(D, S).T)[None]
```

```python
import concourse.bass as bass
from concourse import mybir
from concourse.alu_op_type import AluOpType as ALU
from contextlib import ExitStack
import math
import numpy as np

F32 = mybir.dt.float32
F32R = mybir.dt.float32r
ACT = mybir.ActivationFunctionType
AXX = mybir.AxisListType.X

P = 128
S = 512
D = 1024
KT = D // P
ST = S // P
DEPTH = 2
HD = 64
DH = 4
NH = 8
NG = 2
HPG = NH // NG
CMP_BLOCK, CMP_STRIDE = 32, 16
NCMP = (S - CMP_BLOCK) // CMP_STRIDE + 1
DFF = 2816
FT = DFF // P
ALPHA = (2 * DEPTH) ** 0.25
LN_EPS = 1e-5
NEG = -1e30
SCALE = HD ** -0.5

RING = 4
CHUNK = 8 * P
C_Z, C_DV, C_VSG, C_PHI, C_MERGE, C_WO, C_UP, C_DOWN = 28, 4, 4, 4, 36, 8, 2 * FT, 24
B_Z = 0
B_VSG = B_Z + C_Z
B_DV = B_VSG + C_VSG
B_PHI = B_DV + C_DV // 2
B_DV2 = B_PHI + C_PHI
B_MERGE = B_DV2 + C_DV // 2
B_WO = B_MERGE + C_MERGE
B_UP = B_WO + C_WO
B_DOWN = B_UP + C_UP
CPL = B_DOWN + C_DOWN

Z_AB, Z_AC, Z_AV, Z_DQ, Z_DK, Z_NQ, Z_KC, Z_VC, Z_KS, Z_KW = 0, 4, 8, 12, 16, 20, 24, 25, 26, 27
ROPE_TILES = list(range(Z_DQ, Z_KC + 1)) + [Z_KS, Z_KW]
NR = len(ROPE_TILES)
VSG_N = 2 * P + 3 * NH

PCOL = {}
_at = 0
for _name, _n in (("conv_a", 12), ("subln", 1), ("ln1_g", 8), ("ln1_b", 8), ("ln2_g", 8), ("ln2_b", 8),
                  ("up_w", 2 * FT * 3), ("up_b", 2 * FT), ("pos", 2 * CMP_BLOCK), ("phi_w2k", P), ("phi_w2v", HD),
                  ("lam", 4 * HD), ("lam_init", 1), ("lam_keep", 1)):
    PCOL[_name] = (_at, _n)
    _at += _n
NPAR = _at

CCOL = {}
_at = 0
for _name, _n in (("ident", P), ("rot", P), ("maskneg", P), ("mean", P), ("cmask", ST * NCMP),
                  ("cvalid", ST * NCMP), ("cos", S), ("sin", S), ("eps", 1)):
    CCOL[_name] = (_at, _n)
    _at += _n
NCST = _at

S2 = 256
MH, MT = 4, 2
F2T = 4 * KT
RMS_EPS, GN_EPS = 1e-6, 64e-5
LRU_C = 8.0
K0 = math.exp(-0.5)
RC = S // P
LEVELS = 6
C_LRU_IN, C_LRU_GATE, C_LRU_OUT = 16, 4, 8
C_RKV, C_LORA, C_G2, C_RWO = 24, 4, 4, 8
C_MQ, C_MK, C_MV, C_MO = 8, 8, 8, 8
HALF = F2T // 2
C_HUP, C_HDN = HALF, 2 * KT
B_MFF = C_MQ + C_MK + C_MV + C_MO
C_TAIL = B_MFF + 2 * (C_HUP + C_HDN)
B_LRU = DEPTH * CPL
B_TAIL0 = B_LRU + C_LRU_IN + C_LRU_GATE + C_LRU_OUT
B_RWKV = B_TAIL0 + C_TAIL
B_LORA = B_RWKV + KT
B_V = B_LORA + C_LORA
B_R = B_V + KT
B_G2 = B_R + KT
B_TAIL1 = B_RWKV + C_RKV + C_LORA + C_G2 + C_RWO
N_CHUNKS = B_TAIL1 + C_TAIL

SPLIT_RUNS = ((B_LRU, C_LRU_IN), (B_LRU + C_LRU_IN + C_LRU_GATE, C_LRU_OUT + C_TAIL),
              (B_TAIL1 - C_RWO, C_RWO + C_TAIL))
SPL = CPL - C_PHI


def n_split(c):
    if c < CPL:
        return c if c <= B_PHI else c - C_PHI
    return DEPTH * SPL + sum(min(max(c - b, 0), n) for b, n in SPLIT_RUNS)


SRC = {n: KT * i for i, n in enumerate(("lru_in", "lru_out", "q0", "o0", "up0", "rwo", "q1", "o1", "up1"))}

NHR = D // HD

P2COL = {}
_at = 0
for _name, _n in (("ln", 2 * 6 * KT), ("mem_norm", KT), ("conv_w", 4 * KT), ("conv_b", KT), ("b_in", 2 * KT),
                  ("gate_b", 2 * KT), ("lam", KT), ("b_out", KT), ("mu", 6 * KT), ("w0", KT), ("a0", KT), ("k_k", KT),
                  ("k_a", KT), ("r_k", KT), ("gn_g", KT), ("gn_b", KT), ("rms_eps", 1), ("gn_eps", 1)):
    P2COL[_name] = (_at, _n)
    _at += _n
NPAR2 = _at

C2COL = {}
_at = 0
for _name, _n in (("pair", 2 * P), ("levels", (LEVELS + 1) * P), ("reset", S), ("ones", P), ("center", P), ("sel", 2 * NHR - 2)):
    C2COL[_name] = (_at, _n)
    _at += _n
NCST2 = _at

UNITS = [("diff", qi, hp) for qi in range(ST) for hp in range(DH // 2)] + \
        [(b, qi, g) for b in (0, 1) for qi in range(ST) for g in range(NG)]
NU = len(UNITS)
HEADS_OF = [2 if kind == "diff" else 4 for kind, _, _ in UNITS]
HEADS_BEFORE = [sum(HEADS_OF[:u]) for u in range(NU + 1)]
NHEADS = HEADS_BEFORE[NU]
U_SEL = DH // 2 * ST
U_CS = U_SEL - ST
NGATE = 3 * KT
assert NU == NGATE
B_BR = B_MERGE + NGATE


def build(nc, a, out, stop=None):
    ctx = ExitStack()
    with ctx:
        def sb(name, shape, dt=F32):
            return ctx.enter_context(nc.sbuf_tensor(name, shape, dt))

        def sem(name):
            return ctx.enter_context(nc.semaphore(name))

        ps = ctx.enter_context(nc.psum_tensor("ps", [P, 8, 512], F32))

        def both(name, shape):
            base = -(-nc.sbuf_base // 32) * 32
            whole = sb(name, shape)
            return whole, nc.alloc_sbuf_tensor_at(name + "_r", shape, F32R, offset=base)

        ARENA = 73
        arena_base = -(-nc.sbuf_base // 32) * 32
        sb("arena", [P, ARENA, S])

        def over(name, first, n, dt=F32):
            return nc.alloc_sbuf_tensor_at(name, [P, n, S], dt, offset=arena_base + first * S * 4)[:]

        ring, RL = both("ring", [P, RING, CHUNK])
        RHF, RH = both("rounded", [P, RING, CHUNK])
        X, XL = over("X", 0, KT), over("X_lo", 0, KT, F32R)
        AH = over("source_hi", 8, KT, F32R)
        XH, XHF = AH, AH.bitcast(F32)
        Z = over("Z", 16, 28)
        PROB, PT = Z[:, 0:8, :], Z[:, 8:12, :]
        Y, YL = over("Y", 44, 12), over("Y_lo", 44, 12, F32R)
        SCR = Y[:, 4:12, :]
        YB = over("YB", 56, ST).rearrange("p t (h d) -> p t h d", h=DH)
        YC = over("YC", 60, ST).rearrange("p t (h d) -> p t h d", h=NH)
        DV = over("DV", 64, ST)
        def tiles(*parts):
            return [t[:, i, :] for t in parts for i in range(t.shape[1])]

        SWAP = over("SWAP", 68, 2)
        NB = NG * NCMP
        BLK = SCR[:, 0:4, :].rearrange("p t s -> p (t s)")[:, 0:2 * 2 * 8 * NB].rearrange("p (a h e b) -> p a h e b", a=2, h=2, e=8)
        HB = SCR[0:NB, 6, 0:2 * P].rearrange("p (a h) -> p a h", a=2)
        YH = tiles(over("Y_hi_a", 28, 4, F32R), over("Y_hi", 16, 8, F32R))
        YLs = tiles(over("Y_lo_a", 44, 4, F32R), over("Y_lo_b", 24, 4, F32R), over("Y_lo_c", 36, 4, F32R))
        RS = sb("RS", [P, S])
        G0 = tiles(over("G0_a", 68, 5), over("G0_b", 53, 3))
        GATES = G0 + tiles(over("G1_a", 64, 4), over("G1_b", 32, 4), over("G2_a", 48, 4), over("G2_b", 40, 2), over("G2_c", 52, 1)) + [RS[:]]
        M, ML = G0, tiles(over("M_lo_a", 68, 5, F32R), over("M_lo_b", 53, 3, F32R))
        MR = tiles(over("M_hi", 56, KT, F32R))
        T1 = over("T1", 60, KT)
        FH, FL, FHR = over("F", 16, FT), over("F_lo", 16, FT, F32R), over("F_hi", 16 + FT, FT, F32R)
        FHRF = FHR.bitcast(F32)
        T = over("T", 8, KT)
        N, NL = over("N", 56, KT), over("N_lo", 56, KT, F32R)
        ZL2 = over("Z_lo", 16, 28, F32R)
        HW, HL = over("H", 16, HALF), over("H_lo", 16, HALF, F32R)
        HR = over("H_hi", 16 + HALF, HALF, F32R)
        HRF = HR.bitcast(F32)
        PART = over("PART", 48, KT)
        MEMT, CST2T, RELU = over("MEM", 64, 4), over("CST2", 68, 4), over("RELU", 68, 4)
        MEM_HI, MEM_LO = over("MEM_hi", 40, 4, F32R), over("MEM_lo", 52, 4, F32R)
        VSG = sb("VSG", [P, ST, VSG_N])
        CONST_R = sb("CONST_R", [P, 2 * P], F32R)
        GSIG = sb("GSIG", [P, ST, 3, NH])
        CST = sb("CST", [P, NCST])
        PAR = sb("PAR", [P, NPAR])
        H = sb("PHI", [P, 2, NG, NCMP])
        KCC = sb("KCC", [P, 32])
        VCC = sb("VCC", [32, NG, HD])
        CS = sb("CS", [P, ST, NH, NCMP])
        CM = sb("CM", [P, 4, ST * NH])
        AM = sb("AM", [P, 2, 4, 4])
        LAM = sb("LAM", [P, 2 * HD + 8])
        MS = sb("MS", [P, 2, ST * DH])
        LE = sb("LE", [P, 2, 2, 2, P + 2])

        def cst(name):
            c, n = CCOL[name]
            return CST[:, c:c + n]

        def par(name, i=0, n=None):
            c, m = PCOL[name]
            return PAR[:, c + i:c + (m if n is None else i + n)]

        landed = [sem(f"landed{j}") for j in range(RING)]
        used = sem("used")
        x_in = [sem(f"x_in{h}") for h in range(2)]
        cst_in = sem("cst_in")
        par_in = sem("par_in")
        x_ready = sem("x_ready")
        out_done = sem("out_done")
        zc = sem("zc")
        tokc = sem("tokc")
        gsig = sem("gsig")
        rot = sem("rot")
        rope = sem("rope")
        cmpin = sem("cmpin")
        cmp_step = sem("cmp_step")
        cs_step = sem("cs_step")
        cs_tr = sem("cs_tr")
        cs_pt = sem("cs_pt")
        cs_av = sem("cs_av")
        cs_out = sem("cs_out")
        conv_p = sem("conv_p")
        conv_out = sem("conv_out")
        lam_step = sem("lam_step")
        at_sc = sem("at_sc")
        at_max = sem("at_max")
        at_exp = sem("at_exp")
        at_comb = sem("at_comb")
        at_tr = sem("at_tr")
        at_pta, at_ptd = sem("at_pta"), sem("at_ptd")
        at_av = sem("at_av")
        at_out = sem("at_out")
        yb_step = sem("yb_step")
        ytr = sem("ytr")
        y_hi, y_lo = sem("y_hi"), sem("y_lo")
        m_hi, m_lo = sem("m_hi"), sem("m_lo")
        x0_hi = sem("x0_hi")
        const_r = sem("const_r")
        w_hi, w_lo = sem("w_hi"), sem("w_lo")
        sg = sem("sg")
        kv_swap = sem("kv_swap")
        mg = sem("mg")
        x1pre = sem("x1pre")
        x2pre = sem("x2pre")
        x1 = sem("x1")
        up_a = sem("up_a")
        up_c = sem("up_c")
        up_g = sem("up_g")
        up_h = sem("up_h")
        ln = {k: sem(f"ln_{k}") for k in ("mean", "xc", "sq", "var", "std", "y", "hi")}

        PAR2 = sb("PAR2", [P, NPAR2])
        LRU = sb("LRU", [P, 4, KT])
        MID = sb("MID", [P, 3, KT, RC])
        YC_ADD = LE[:].rearrange("p a b c t -> p (a b c t)")[:, 0:HPG * HD]
        MN = MEMT.rearrange("p t n -> p (t n)").rearrange("p (k s) -> p k s", k=KT)
        CST2 = CST2T.rearrange("p t n -> p (t n)")
        MK = Z[:, 8:12, :].rearrange("p k s -> p (k s)").rearrange("p (k s) -> p k s", k=KT)
        MV = Z[:, 12:16, :].rearrange("p k s -> p (k s)").rearrange("p (k n) -> p k n", k=2)
        MNH, MNL = [t.rearrange("p t n -> p (t n)").rearrange("p (k s) -> p k s", k=KT) for t in (MEM_HI, MEM_LO)]
        MNHF = MNH.bitcast(F32)
        MP = T[:, 0:4, :].rearrange("p k s -> p (k s)").rearrange("p (u h s) -> p u h s", u=2, h=MH)
        SPARE = RHF[:].rearrange("p j (e s) -> p (j e) s", e=2)
        LT, YCF = SPARE[:, 0:4, :], SPARE[:, 4:8, :]
        VSGF = VSG[:].rearrange("p t n -> p (t n)")
        CSF = CS[:].rearrange("p t h n -> p (t h n)")
        cos0 = CCOL["cos"][0]
        MIX = [[T[:, n, :] for n in range(KT)], [SPARE[:, n, :] for n in range(KT)]]
        TW, TA_, TG = Y[0:HD, 8, :], Y[0:HD, 9, :], Y[:, 10, :]
        LANES = []
        for L in range(2):
            wide = Z[:, 24:28, :].rearrange("p k s -> p (k s)") if L == 0 else LT.rearrange("p k s -> p (k s)")
            single = [Y[:, 8, :], Y[:, 9, :], YCF[:, 0, :], YCF[:, 1, :], VSGF[:, 0:S], CST[:, cos0:cos0 + S]] if L == 0 else \
                     [YCF[:, 2, :], YCF[:, 3, :], VSGF[:, S:2 * S], Y[:, 11, :], CST[:, cos0 + S:cos0 + 2 * S], RS[:]]
            LANES.append(dict(
                ar=single[0].rearrange("p (n a t) -> p n a t", n=2, a=2),
                bk=single[1].rearrange("p (a n t) -> p a n t", a=2, n=2),
                pu=single[1].rearrange("p (a q i) -> p a q i", a=2, q=4),
                e=LE[:, L], z=single[2].rearrange("p (q t) -> p q t", q=4),
                g1=wide[:, 0:1024].rearrange("p (q a t) -> p q a t", q=4, a=2),
                g2=wide[:, 1024:2048].rearrange("p (q a t) -> p q a t", q=4, a=2),
                x=single[3].rearrange("p (q t) -> p q t", q=4), xt=single[4].rearrange("p (q t) -> p q t", q=4),
                bktok=single[5].rearrange("p (a n c) -> p a n c", a=2, n=2),
                vtok=CSF[:, L * 256:L * 256 + 256].rearrange("p (n c) -> p n c", n=2),
                sh=CSF[:, 512 + L * P:512 + L * P + P].rearrange("p (n i) -> p n i", n=2)))
        ROWS = VSGF[0:NHR, 0:S]
        CAST = LE[:].rearrange("p a b c t -> p (a b c t)")[0:NHR, 0:D]
        TMP = [RS[:], over("TMP", 72, 1)[:, 0, :]]
        STATE = PAR[:, 0:KT * HD].rearrange("p (n i) -> p n i", n=KT)

        def par2(name, i=0, n=None):
            c, m = P2COL[name]
            return PAR2[:, c + i:c + (m if n is None else i + n)]

        def cst2(name, i=0, n=None):
            c, m = C2COL[name]
            return CST2[:, c + i:c + (m if n is None else i + n)]

        par2_in = sem("par2_in")
        cst2_in = sem("cst2_in")
        mem_in = sem("mem_in")
        xr2 = sem("xr2")
        t_ready = sem("t_ready")
        rms_sq, rms_var, rms_std, rms_y = [sem(f"rms_{k}") for k in ("sq", "var", "std", "y")]
        NORMED = {i: KT * (at + 1) for at, i in enumerate((0, 1, 3, 5, 7, 9, 11))}
        lru_in = sem("lru_in")
        lru_conv = sem("lru_conv")
        lru_gate = sem("lru_gate")
        lru_rate = sem("lru_rate")
        lru_ea = sem("lru_ea")
        lru_q = sem("lru_q")
        lru_m = sem("lru_m")
        lru_y = sem("lru_y")
        mq = sem("mq")
        mv = sem("mv")
        m_sc, m_max, m_exp, m_p, m_tr, m_pt, m_o = [sem(f"m_{k}") for k in ("sc", "max", "exp", "p", "tr", "pt", "o")]
        src_hi, src_lo = sem("src_hi"), sem("src_lo")
        mem_hi, mem_lo = sem("mem_hi"), sem("mem_lo")
        mup_r = sem("mup_r")
        mup = sem("mup")
        mix = sem("mix")
        rkv = sem("rkv")
        lora = sem("lora")
        lw = sem("lw")
        la = sem("la")
        kk = {k: sem(f"kk_{k}") for k in ("sq", "sum", "root", "cast", "done")}
        cum = sem("cum")
        mid_e = sem("mid_e")
        ch = [{k: sem(f"ch{L}_{k}") for k in ("exp", "hat", "tr", "tok", "g1", "g2", "g2m", "x0t", "x0", "z", "zm", "x", "xc",
                                              "p", "pc", "u", "uc", "s", "yc", "sc")} for L in range(2)]
        gn = {k: sem(f"gn_{k}") for k in ("center", "sq", "yc", "var", "rk", "bonus", "bout", "root", "cast", "out")}

        block = ctx.enter_context(nc.Block())

        @block.sync
        def _(sp):
            for j in range(RING):
                sp.dma_start(ring[:, j, :], a["weights"][j]).then_inc(landed[j], 16)
                if j < 2:
                    half = slice(j * KT // 2, (j + 1) * KT // 2)
                    sp.dma_start(X[:, half, :], a["x"][:, half, :]).then_inc(x_in[j], 16)
            sp.dma_start(CST[:], a["cst"]).then_inc(cst_in, 16)
            sp.dma_start(PAR2[:], a["par2"]).then_inc(par2_in, 16)
            with sp.Fori(1, N_CHUNKS // RING) as q:
                for j in range(RING):
                    sp.wait_ge(used, q * RING + (j + 1 - RING))
                    sp.dma_start(ring[:, j, :], a["weights"][bass.ds(q * RING + j, 1)]
                                 .rearrange("a p c -> (a p) c")).then_inc(landed[j], 16)
            for n in range(0, KT, 2):
                sp.wait_ge(xr2, 6 * KT + n + 2)
                sp.dma_start(out[:, n:n + 2, :], X[:, n:n + 2, :]).then_inc(out_done, 16)
            sp.wait_ge(out_done, KT // 2 * 16)

        @block.tensor
        def _(pe):
            mm = nc.tensor.matmul

            def arrived(quad, j):
                pe.wait_ge(landed[j], quad * 16 + 16)

            def three(o, lh, ll, rh, rl, start, stop):
                mm(o, lh, rh, start=start, stop=False)
                mm(o, ll, rh, start=False, stop=False)
                return mm(o, lh, rl, start=False, stop=stop)

            def tile(t, k):
                return t[k] if isinstance(t, list) else t[:, k, :]

            def w(j, k):
                return ring[:, j, k * P:k * P + P]

            def wh(j, k):
                return RH[:, j, k * P:k * P + P]

            def wl(j, k):
                return RL[:, j, k * P:k * P + P]

            def first_quad(split, bank, hi, lo, ready, base, step=1, banks_free=None):
                for k in range(KT):
                    pe.wait_ge(ready, base + step * (k + 1))
                    for j in range(2):
                        if k == 0:
                            pe.wait_ge(w_lo, split + (j + 1))
                            if banks_free is not None:
                                pe.wait_ge(banks_free[0], banks_free[1] + (j + 1))
                        ins = three(ps[:, bank + j, :], wh(j, k), wl(j, k), tile(hi, k), tile(lo, k), k == 0, k == KT - 1)
                        if k == KT - 1:
                            ins.then_inc(used, 1)
                for j in range(2, RING):
                    if banks_free is not None:
                        pe.wait_ge(banks_free[0], banks_free[1] + (j + 1))
                    product(split + j, j, bank + j, hi, lo)

            def product(split, j, bank, hi, lo):
                pe.wait_ge(w_lo, split + 1)
                for k in range(KT):
                    ins = three(ps[:, bank, :], wh(j, k), wl(j, k), tile(hi, k), tile(lo, k), k == 0, k == KT - 1)
                ins.then_inc(used, 1)

            def tokens(split, j, part, n):
                pe.wait_ge(w_lo, split + 1)
                for t in range(ST):
                    for e in range(2):
                        k, c = 2 * part + e, slice(t * P, t * P + P)
                        ins = three(ps[:, t, 0:n], XH[:, k, c], XL[:, k, c], RH[:, j, e * 512:e * 512 + n],
                                    RL[:, j, e * 512:e * 512 + n], k == 0, k == KT - 1)
                ins.then_inc(used, 1)

            def layer_norm(l, i, pre, pre_base):
                s, at = ln, l * 2 + i
                pe.wait_ge(pre, l * KT + pre_base + KT)
                mm(ps[:, 4, :], cst("mean"), RS[:], start=True, stop=True).then_inc(s["mean"], 1)
                for n in range(KT):
                    pe.wait_ge(s["sq"], at * KT + n + 1)
                    ins = mm(ps[:, 5, :], cst("mean"), T1[:, n, :], start=(n == 0), stop=(n == KT - 1))
                ins.then_inc(s["var"], 1)

            def scores(l, u):
                kind, qi, which = UNITS[u]
                W = (qi + 1) * P
                if u > 0:
                    pe.wait_ge(at_exp, l * NU + u)
                for m in range(4):
                    if kind == "diff":
                        h, o = 2 * which + m // 2, (m % 2) * HD
                        q, k = Z[o:o + HD, Z_DQ + h, qi * P:W], Z[o:o + HD, Z_DK + h, 0:W]
                    else:
                        o = which * HD
                        q, k = Z[o:o + HD, Z_NQ + m, qi * P:W], Z[o:o + HD, Z_KS + kind, 0:W]
                    mm(ps[:, m, 0:W], q, k, start=True, stop=False)
                    ins = mm(ps[:, m, qi * P:W], CONST_R[:, 0:P], CONST_R[:, P:2 * P], start=False, stop=True)
                ins.then_inc(at_sc, 1)

            def turn(l, u, i):
                kind, qi, which = UNITS[u]
                t = HEADS_BEFORE[u] + i
                if i == 0:
                    if kind == "diff":
                        pe.wait_ge(at_comb, l * (NU // 3) + u + 1)
                    else:
                        pe.wait_ge(at_exp, l * NU + u + 1)
                if i >= 2:
                    pe.wait_ge(at_pta, l * 2 * NU + 2 * u + i - 1)
                elif U_CS <= u < U_SEL:
                    pe.wait_ge(cs_pt, l * ST + u - U_CS + 1)
                elif u > U_SEL:
                    pe.wait_ge(at_ptd, l * 2 * (NU - U_SEL) + 2 * (u - 1 - U_SEL) + i + 1)
                elif u > 0:
                    pe.wait_ge(at_pta, l * 2 * NU + 2 * (u - 1) + i + 1)
                m = 2 * i if kind == "diff" else i
                for kb in range(qi + 1):
                    ins = nc.tensor.transpose(ps[:, 4 + t % 2, kb * P:kb * P + P],
                                              PROB[:, (u % 2) * 4 + m, kb * P:kb * P + P], cst("ident"))
                ins.then_inc(at_tr, 1)

            def values(l, u, i):
                kind, qi, which = UNITS[u]
                t = HEADS_BEFORE[u] + i
                if i == 0:
                    if u == 0:
                        pe.wait_ge(cs_step, l * 4 + 2)
                    elif U_CS <= u < U_SEL:
                        pe.wait_ge(cs_out, l * ST + u - U_CS + 1)
                    else:
                        pe.wait_ge(at_out, l * NU + u)
                if i < 2:
                    pe.wait_ge(at_pta, l * 2 * NU + 2 * u + i + 1)
                else:
                    pe.wait_ge(at_ptd, l * 2 * (NU - U_SEL) + 2 * (u - U_SEL) + i - 1)
                for kb in range(qi + 1):
                    if kind == "diff":
                        h = 2 * which + i
                        o, v = ps[:, 6, i * P:i * P + P], DV[:, kb, h * P:h * P + P]
                    else:
                        c = kind * P + which * HD
                        o, v = ps[:, 6, i * HD:i * HD + HD], VSG[:, kb, c:c + HD]
                    ins = mm(o, PT[:, t % 4, kb * P:kb * P + P], v, start=(kb == 0), stop=(kb == qi))
                ins.then_inc(at_av, 1)

            with pe.Fori(0, DEPTH) as l:
                Q = l * (CPL // RING)
                W0 = l * SPL
                first_quad(W0, 0, XH, XL, x_ready, l * 16, 2, (zc, l * C_Z))
                with pe.Fori(1, Z_DQ // RING) as i:
                    for j in range(RING):
                        pe.wait_ge(zc, l * C_Z + i * RING + (j + 1))
                        product(W0 + i * RING + j, j, j, XH, XL)

                def rotate(r0, r1):
                    for r in range(r0, r1):
                        if r >= 4:
                            pe.wait_ge(rope, l * NR + r - 3)
                        mm(ps[:, 4 + r % 4, :], cst("rot"), Z[:, ROPE_TILES[r], :], start=True, stop=True).then_inc(rot, 1)

                pe.wait_ge(cst_in, 16)
                pe.wait_ge(const_r, 1)
                for q in range(Z_DQ // RING, C_Z // RING):
                    for j in range(RING):
                        pe.wait_ge(zc, l * C_Z + q * RING + (j + 1))
                        product(W0 + q * RING + j, j, j, XH, XL)
                    if q > Z_DQ // RING:
                        rotate((q - 1) * RING - Z_DQ, q * RING - Z_DQ)
                pe.wait_ge(zc, l * C_Z + C_Z + 4)
                for j in range(RING):
                    tokens(W0 + (B_VSG + j), j, j, VSG_N)
                rotate(Z_KC - Z_DQ, NR)
                pe.wait_ge(tokc, l * 8 + 4)
                for j in range(2):
                    tokens(W0 + (B_DV + j), j, j, DH * P)
                pe.wait_ge(rope, l * NR + NR)
                pe.wait_ge(cmpin, l + 1)
                for c in range(C_PHI):
                    kv, j = c // 2, (B_PHI + c) % RING
                    arrived(Q + (B_PHI + c) // RING, j)
                    for e in range(8):
                        ins = mm(ps[0:NB, 4 + kv, 0:P], BLK[:, kv, c % 2, e, :], w(j, e),
                                 start=(c % 2 == 0 and e == 0), stop=(c % 2 == 1 and e == 7))
                    ins.then_inc(used, 1)
                tokens(W0 + n_split(B_DV2), 2, 2, DH * P)
                pe.wait_ge(cmp_step, l * 6 + 2)
                tokens(W0 + n_split(B_DV2 + 1), 3, 3, DH * P)
                for kv in range(2):
                    ins = nc.tensor.transpose(ps[:, 6, kv * NB:kv * NB + NB], HB[:, kv, :], cst("ident")[0:NB, 0:NB])
                ins.then_inc(cmp_step, 1)
                pe.wait_ge(tokc, l * 8 + 8)
                scores(l, 0)
                pe.wait_ge(cmp_step, l * 6 + 4)
                for g in range(NG):
                    mm(ps[:, 4, g * 32:g * 32 + NCMP], par("phi_w2k"), H[:, 0, g, :], start=True, stop=True)
                    ins = mm(ps[0:NCMP, 5, g * HD:g * HD + HD], H[:, 1, g, :], par("phi_w2v"), start=True, stop=True)
                ins.then_inc(cmp_step, 1)
                pe.wait_ge(cmp_step, l * 6 + 6)
                for qi in range(ST):
                    for g in range(NG):
                        for r in range(HPG):
                            c = qi * P + r * 32
                            ins = mm(ps[:, 6 + g, c:c + NCMP], Z[g * HD:g * HD + HD, Z_NQ + r, qi * P:qi * P + P],
                                     KCC[g * HD:g * HD + HD, 0:NCMP], start=True, stop=True)
                ins.then_inc(cs_step, 1)

                def turn_cs(u, qi):
                    pe.wait_ge(cs_step, l * 4 + 4)
                    pe.wait_ge(at_pta, l * 2 * NU + 2 * u)
                    for h in range(NH):
                        ins = nc.tensor.transpose(ps[0:NCMP, 4 + h // 4, (h % 4) * P:(h % 4) * P + P], CS[:, qi, h, :], cst("ident"))
                    ins.then_inc(cs_tr, 1)

                def values_cs(u, qi):
                    pe.wait_ge(cs_pt, l * ST + qi + 1)
                    pe.wait_ge(at_out, l * NU + u)
                    for h in range(NH):
                        e = SCR[0:NCMP, qi % 2 * 2 + h // 4, (h % 4) * P:(h % 4) * P + P]
                        ins = mm(ps[:, 6, h * HD:h * HD + HD], e, VCC[0:NCMP, h // HPG, :], start=True, stop=True)
                    ins.then_inc(cs_av, 1)

                for u in range(NU):
                    if u + 1 < NU:
                        scores(l, u + 1)
                    if U_CS <= u < U_SEL:
                        turn_cs(u, u - U_CS)
                    if u == 0:
                        pe.wait_ge(cs_step, l * 4 + 2)
                    else:
                        pe.wait_ge(sg, l * NGATE + u)
                    product(W0 + (n_split(B_MERGE) + u), u % RING, 7, XH, XL)
                    if U_CS <= u < U_SEL:
                        values_cs(u, u - U_CS)
                    n = HEADS_OF[u]
                    turn(l, u, 0)
                    for i in range(n):
                        if i + 1 < n:
                            turn(l, u, i + 1)
                        values(l, u, i)
                pe.wait_ge(yb_step, l * 4 + 4)
                for c in range(4):
                    for t in range(ST):
                        ins = nc.tensor.transpose(ps[:, c, t * P:t * P + P], YB[:, t, c, :], cst("ident"))
                    ins.then_inc(ytr, 1)
                pe.wait_ge(at_out, l * NU + NU)
                pe.wait_ge(sg, l * NGATE + NGATE)
                for c in range(4):
                    for t in range(ST):
                        ins = nc.tensor.transpose(ps[:, 4 + c, t * P:t * P + P],
                                                  YC[:, t, 2 * c:2 * c + 2, :].rearrange("p h d -> p (h d)"), cst("ident"))
                    ins.then_inc(ytr, 1)
                def branch(b, p, c):
                    pe.wait_ge(w_lo, W0 + (n_split(B_BR) + c + 1))
                    for e in range(2):
                        n = 2 * p + e
                        pe.wait_ge(mg, l * 24 + b * 8 + n + 1)
                        for k in range(4):
                            ins = three(ps[:, n % 4, :], wh(c % RING, e * 4 + k), wl(c % RING, e * 4 + k),
                                        YH[b * 4 + k], YLs[b * 4 + k], k == 0, k == 3)
                    ins.then_inc(used, 1)

                pe.wait_ge(y_lo, l * 12 + 8)
                for b in range(3):
                    if b == 2:
                        pe.wait_ge(y_lo, l * 12 + 12)
                    for p in range(4):
                        branch(b, p, 4 * b + p)
                first_quad(W0 + n_split(B_WO), 0, MR, ML, m_lo, l * KT)
                for j in range(RING):
                    pe.wait_ge(x1pre, l * KT + RING + (j + 1))
                    product(W0 + (n_split(B_WO) + RING + j), j, j, MR, ML)
                layer_norm(l, 0, x1pre, 4)
                first_quad(W0 + n_split(B_UP), 0, XH, XL, x1, l * KT, 1, (up_c, l * C_UP))
                with pe.Fori(1, C_UP // RING) as i:
                    for j in range(RING):
                        pe.wait_ge(up_c, l * C_UP + i * RING + (j + 1))
                        product(W0 + i * RING + (n_split(B_UP) + j), j, j, XH, XL)
                with pe.Fori(0, 2) as i:
                    for n in range(4):
                        pe.wait_ge(up_c, l * C_UP + C_UP + n + 1)
                        pe.wait_ge(x2pre, l * KT + i * 4 + (n + 1))
                        for c in range(3):
                            f = 3 * n + c
                            pe.wait_ge(up_h, l * FT + min(8 * c + 8, FT) + 2)
                            pe.wait_ge(w_lo, W0 + i * 12 + (n_split(B_DOWN) + f + 1))
                            for k in range(8 * c, min(8 * c + 8, FT)):
                                ins = three(ps[:, n, :], wh(f % RING, k - 8 * c), wl(f % RING, k - 8 * c), FHR[:, k, :], FL[:, k, :],
                                            k == 0, k == FT - 1)
                            ins.then_inc(used, 1)
                layer_norm(l, 1, x2pre, 4)

            def rms_out(i):
                pe.wait_ge(rms_sq, i * KT + KT)
                mm(ps[:, 5, :], cst("mean"), RS[:], start=True, stop=True).then_inc(rms_var, 1)

            def rms(i, bank_cols=S):
                for n in range(KT):
                    pe.wait_ge(rms_sq, i * KT + n + 1)
                    src = T[:, n, 0:bank_cols]
                    ins = mm(ps[:, 5, 0:bank_cols], cst("mean"), src, start=(n == 0), stop=(n == KT - 1))
                ins.then_inc(rms_var, 1)

            def gemm(first, tiles, hi, lo, free, base, src, bank=0):
                first_quad(n_split(first), bank, hi, lo, src_lo, src, 1, (free, base))
                if tiles > RING:
                    with pe.Fori(1, tiles // RING) as i:
                        for j in range(RING):
                            pe.wait_ge(free, i * RING + (base + j + 1))
                            product(i * RING + (n_split(first) + j), j, bank + j, hi, lo)

            def tail(l):
                B = B_TAIL0 if l == 0 else B_TAIL1
                rms(3 + 6 * l)
                gemm(B, C_MQ, AH, NL, mq, l * 16, SRC[f"q{l}"])
                pe.wait_ge(mem_lo, l + 1)
                with pe.Fori(0, C_MK // RING) as i:
                    for j in range(RING):
                        pe.wait_ge(mq, i * RING + (l * 16 + 8 + j + 1))
                        pe.wait_ge(w_lo, i * RING + (n_split(B + C_MQ) + j + 1))
                        for k in range(KT):
                            ins = three(ps[:, j, 0:S2], wh(j, k), wl(j, k), MNH[:, k, :], MNL[:, k, :], k == 0, k == KT - 1)
                        ins.then_inc(used, 1)
                for c in range(C_MV):
                    half, j = c // 4, c % 4
                    pe.wait_ge(w_lo, n_split(B + C_MQ + C_MK + c) + 1)
                    for t in range(2):
                        for e in range(2):
                            k, r = 2 * j + e, slice(e * 512, e * 512 + 512)
                            ins = three(ps[:, 4 + 2 * half + t, :], MNH[:, k, t * P:t * P + P], MNL[:, k, t * P:t * P + P],
                                        RH[:, j, r], RL[:, j, r], k == 0, k == KT - 1)
                    ins.then_inc(used, 1)
                pe.wait_ge(mq, l * 16 + 20)

                def scores2(qi):
                    if qi >= 2:
                        pe.wait_ge(m_exp, l * ST + qi - 1)
                    for h in range(MH):
                        for k in range(MT):
                            ins = mm(ps[:, 2 * (qi % 2) + h // 2, (h % 2) * S2:(h % 2) * S2 + S2],
                                     Z[:, h * MT + k, qi * P:qi * P + P], MK[:, h * MT + k, :], start=(k == 0), stop=(k == MT - 1))
                    ins.then_inc(m_sc, 1)

                scores2(0)
                for qi in range(ST):
                    if qi + 1 < ST:
                        scores2(qi + 1)
                    if qi == 0:
                        pe.wait_ge(mv, l * 4 + 4)
                    pe.wait_ge(m_p, l * ST + qi + 1)
                    for kb in range(2):
                        if qi >= 2:
                            pe.wait_ge(m_pt, l * 2 * ST + 2 * (qi - 2) + kb + 1)
                        for h in range(MH):
                            ins = nc.tensor.transpose(ps[:, 4 + 2 * (qi % 2) + kb, h * P:h * P + P],
                                                      MP[:, qi % 2, h, kb * P:kb * P + P], cst("ident"))
                        ins.then_inc(m_tr, 1)
                pe.wait_ge(m_pt, l * 2 * ST + 2 * ST)
                for c in range(KT):
                    h = c // MT
                    if c >= 4:
                        pe.wait_ge(src_lo, SRC[f"o{l}"] + c - 3)
                    for kb in range(2):
                        ins = mm(ps[:, c % 4, :], MV[:, kb, c * P:c * P + P], Z[:, 16 + 2 * h + kb, :], start=(kb == 0), stop=(kb == 1))
                    ins.then_inc(m_o, 1)
                gemm(B + C_MQ + C_MK + C_MV, C_MO, AH, YL, t_ready, l * 32 + 8, SRC[f"o{l}"], 4)
                rms_out(4 + 6 * l)
                rms(5 + 6 * l)
                for h in range(2):
                    U = B + B_MFF + h * (C_HUP + C_HDN)
                    gemm(U, C_HUP, AH, NL, mup, l * F2T + h * HALF, SRC[f"up{l}"], 4)
                    with pe.Fori(0, 2) as i:
                        for n in range(4):
                            pe.wait_ge(t_ready, i * 4 + (l * 32 + 16 + h * KT + n + 1))
                            for c in range(2):
                                j = (2 * n + c) % RING
                                pe.wait_ge(mup, l * F2T + h * HALF + 8 * c + 8 + 4)
                                pe.wait_ge(w_lo, i * 8 + (n_split(U + C_HUP) + 2 * n + c + 1))
                                for k in range(8):
                                    ins = three(ps[:, n, :], wh(j, k), wl(j, k), HR[:, 8 * c + k, :], HL[:, 8 * c + k, :],
                                                c == 0 and k == 0, c == 1 and k == 7)
                                ins.then_inc(used, 1)
                rms_out(6 + 6 * l)

            rms(0)
            gemm(B_LRU, C_LRU_IN, AH, NL, lru_in, 0, SRC["lru_in"])
            rms(1, S2)
            pe.wait_ge(lru_conv, KT)
            pe.wait_ge(lru_in, 20)
            for c in range(C_LRU_GATE):
                arrived((B_LRU + C_LRU_IN + c) // RING, c)
                if c == 1:
                    pe.wait_ge(rms_std, 2)
                if c >= 2:
                    pe.wait_ge(lru_gate, 4 * (c - 1))
                for b in range(4):
                    k0 = (c % 2) * 4 + (b // 2) * 2
                    for k in range(2):
                        ins = mm(ps[:, 4 * (c % 2) + b, :], w(c, b * 2 + k), Z[:, 16 + k0 + k, :], start=(k == 0), stop=(k == 1))
                ins.then_inc(used, 1)
            gemm(B_LRU + C_LRU_IN + C_LRU_GATE, C_LRU_OUT, AH, ZL2[:, 16:24, :], t_ready, 0, SRC["lru_out"])
            rms_out(2)
            tail(0)

            rms(7)
            def rkv_tile(first, n, turn, src):
                c = first + n
                pe.wait_ge(rkv, turn + 1)
                arrived(c // RING, c % RING)
                for k in range(KT):
                    ins = mm(ps[:, c % 4, :], w(c % RING, k), src[k], start=(k == 0), stop=(k == KT - 1))
                ins.then_inc(used, 1)

            def head_sums(bank, n, src):
                o = NHR - 2 - 2 * n
                return mm(ps[0:NHR, bank, :], cst2("sel", o, NHR), src, start=(n == 0), stop=(n == KT - 1))

            def head_cast(bank, n):
                return mm(ps[:, bank, :], CAST[:, n * P:n * P + P], ROWS, start=True, stop=True)

            for k in range(KT):
                pe.wait_ge(mix, k + 1)
                for n in range(RING):
                    if k == 0:
                        pe.wait_ge(rkv, n + 1)
                        arrived(B_RWKV // RING, n)
                    ins = mm(ps[:, n, :], w(n, k), MIX[0][k], start=(k == 0), stop=(k == KT - 1))
                    if k == KT - 1:
                        ins.then_inc(used, 1)
            for n in range(RING, KT):
                rkv_tile(B_RWKV, n, n, MIX[0])
            QL = B_LORA // RING
            pe.wait_ge(mix, 2 * KT)
            arrived(QL, 0)
            for k in range(KT):
                ins = mm(ps[0:HD, 4, :], ring[:, 0, k * HD:k * HD + HD], MIX[1][k], start=(k == 0), stop=(k == KT - 1))
            ins.then_inc(lora, 1)
            pe.wait_ge(mix, 3 * KT)
            for k in range(KT):
                ins = mm(ps[0:HD, 5, :], ring[:, 0, 512 + k * HD:512 + k * HD + HD], MIX[0][k], start=(k == 0), stop=(k == KT - 1))
            ins.then_inc(used, 1)
            pe.wait_ge(mix, 4 * KT)
            arrived(QL, 1)
            for k in range(KT):
                ins = mm(ps[:, 6, :], w(1, k), MIX[1][k], start=(k == 0), stop=(k == KT - 1))
            ins.then_inc(used, 1)
            arrived(QL, 2)
            pe.wait_ge(rkv, KT + 4)
            pe.wait_ge(la, 1)
            for n in range(KT):
                if n >= 4:
                    pe.wait_ge(lw, n - 3)
                ins = mm(ps[:, n % 4, :], ring[0:HD, 2, n * P:n * P + P], TW, start=True, stop=True)
                ins.then_inc(lora if n < KT - 1 else used, 1)
            arrived(QL, 3)
            pe.wait_ge(la, 3)
            for n in range(KT):
                if n >= 4:
                    pe.wait_ge(la, 3 + n - 3)
                ins = mm(ps[:, 4 + n % 4, :], ring[0:HD, 3, n * P:n * P + P], TA_, start=True, stop=True)
                ins.then_inc(lora if n < KT - 1 else used, 1)
            pe.wait_ge(mix, 5 * KT)
            pe.wait_ge(lw, KT)
            for n in range(KT):
                rkv_tile(B_V, n, KT + n, MIX[0])
            pe.wait_ge(mix, 6 * KT)
            pe.wait_ge(cst2_in, 16)
            pe.wait_ge(la, 3 + KT)
            for n in range(KT):
                rkv_tile(B_R, n, 2 * KT + n, MIX[1])
                if n == 3:
                    for t in range(KT):
                        pe.wait_ge(kk["sq"], t + 1)
                        head_sums(4, t, Z[:, 24 + t % 4, :]).then_inc(kk["sum"], 1)
                if n in (5, 6):
                    pe.wait_ge(kk["root"], 2)
                    for t in range(4 * (n - 5), 4 * (n - 5) + 4):
                        if t >= 4:
                            pe.wait_ge(kk["done"], t - 3)
                        head_cast(4 + t % 4, t).then_inc(kk["cast"], 1)

            def chain(c, half, L):
                s, B, o = ch[L], LANES[L], 4 * L
                return s, B, o, c * 2 + half

            with pe.Fori(0, RC) as c:
                for half in range(2):
                    for L in range(2):
                        s, B, o, it = chain(c, half, L)
                        pe.wait_ge(s["hat"], it + 1)
                        for e in range(2):
                            for n in range(2):
                                ins = nc.tensor.transpose(ps[:, o, (2 * e + n) * P:(2 * e + n) * P + P], B["bk"][:, e, n, :], cst("ident"))
                        for n in range(2):
                            ins = nc.tensor.transpose(ps[:, o + 1, n * P:n * P + P], B["x"][:, n, :], cst("ident"))
                        ins.then_inc(s["tr"], 1)
                        for q in range(4):
                            r, n = (q % 2) * HD, q // 2
                            ins = mm(ps[:, o + 2 + q % 2, n * 2 * P:n * 2 * P + 2 * P], B["bk"][r:r + HD, 0, n, :],
                                     B["ar"][r:r + HD, n, :, :].rearrange("p a t -> p (a t)"), start=True, stop=True)
                        ins.then_inc(s["g1"], 1)
                    for L in range(2):
                        s, B, o, it = chain(c, half, L)
                        pe.wait_ge(s["tok"], it + 1)
                        for q in range(4):
                            r, n = (q % 2) * HD, q // 2
                            ins = mm(ps[:, o + q % 2, n * 2 * P:n * 2 * P + 2 * P], B["bk"][r:r + HD, 1, n, :],
                                     B["ar"][r:r + HD, n, :, :].rearrange("p a t -> p (a t)"), start=True, stop=True)
                        ins.then_inc(s["g2"], 1)
                    for L in range(2):
                        s, B, o, it = chain(c, half, L)
                        pe.wait_ge(s["x0t"], it + 1)
                        for q in range(4):
                            ins = nc.tensor.transpose(ps[:, o + 2, q * P:q * P + P], B["xt"][:, q, :], cst("ident"))
                        ins.then_inc(s["x0"], 1)
                    for v in range(LEVELS):
                        for L in range(2):
                            s, B, o, it = chain(c, half, L)
                            if v == 0:
                                pe.wait_ge(s["g2m"], it + 1)
                            pe.wait_ge(s["xc"], it * (2 * LEVELS + 1) + 2 * v + 1)
                            for q in range(4):
                                ins = mm(ps[:, o, q * P:q * P + P], B["g1"][:, q, 0, :], B["x"][:, q, :], start=True, stop=True)
                            ins.then_inc(s["z"], 1)
                        for L in range(2):
                            s, B, o, it = chain(c, half, L)
                            pe.wait_ge(s["zm"], it * LEVELS + v + 1)
                            for q in range(4):
                                ins = mm(ps[:, o + 1, q * P:q * P + P], B["xt"][:, q, :], B["z"][:, q, :], start=True, stop=True)
                            ins.then_inc(s["x"], 1)
                            for q in range(4):
                                ins = mm(ps[:, o + 2, q * P:q * P + P], B["z"][:, q, :], B["xt"][:, q, :], start=True, stop=True)
                            ins.then_inc(s["x"], 1)
                    for L in range(2):
                        s, B, o, it = chain(c, half, L)
                        pe.wait_ge(s["xc"], it * (2 * LEVELS + 1) + 2 * LEVELS + 1)
                        for q in range(4):
                            r, n = (q % 2) * HD, q // 2
                            mm(ps[:, o + q % 2, n * HD:n * HD + HD], B["ar"][r:r + HD, n, 0, :], B["sh"][r:r + HD, n, :], start=True, stop=False)
                            ins = mm(ps[:, o + q % 2, n * HD:n * HD + HD], B["g2"][:, q, 0, :], B["vtok"][:, n, r:r + HD], start=False, stop=True)
                        ins.then_inc(s["p"], 1)
                    for L in range(2):
                        s, B, o, it = chain(c, half, L)
                        pe.wait_ge(s["pc"], it + 1)
                        for q in range(4):
                            ins = mm(ps[:, o + 2, q * HD:q * HD + HD], B["xt"][:, q, :], B["pu"][:, 0, q, :], start=True, stop=True)
                        ins.then_inc(s["u"], 1)
                    for L in range(2):
                        s, B, o, it = chain(c, half, L)
                        pe.wait_ge(s["uc"], it + 1)
                        for n in range(2):
                            y = ps[:, o, n * P:n * P + P]
                            mm(y, B["bktok"][:, 0, n, :], B["pu"][:, 1, 2 * n:2 * n + 2, :].rearrange("p q i -> p (q i)"), start=True, stop=False)
                            mm(y, B["bktok"][:, 1, n, :], B["vtok"][:, n, :], start=False, stop=True)
                        for q in range(4):
                            r, n = (q % 2) * HD, q // 2
                            y = ps[r:r + HD, o + 3, n * P:n * P + P]
                            mm(y, B["sh"][r:r + HD, n, :], B["ar"][r:r + HD, n, 1, :], start=True, stop=False)
                            mm(y, B["pu"][:, 1, q, :], B["g1"][:, q, 1, :], start=False, stop=False)
                            ins = mm(y, B["vtok"][:, n, r:r + HD], B["g2"][:, q, 1, :], start=False, stop=True)
                        ins.then_inc(s["s"], 1)

            for L in range(2):
                pe.wait_ge(ch[L]["yc"], 2 * RC)
                pe.wait_ge(ch[L]["sc"], 2 * RC)
            for j in range(RING - 1):
                arrived((B_RWKV + C_RKV + C_LORA) // RING, j)
            pe.sem_inc(used, RING - 1)
            arrived((B_RWKV + C_RKV + C_LORA) // RING, RING - 1)
            for n in range(KT):
                if n >= 2:
                    pe.wait_ge(gn["yc"], n - 1)
                mm(ps[:, n % 2, :], cst2("center"), T[:, n, :], start=True, stop=True).then_inc(gn["center"], 1)
                pe.wait_ge(gn["rk"], n + 1)
                if n >= 2:
                    pe.wait_ge(gn["bout"], n - 1)
                mm(ps[:, 2 + n % 2, :], cst2("ones"), Z[:, 24 + n % 2, :], start=True, stop=True).then_inc(gn["bonus"], 1)
                if n >= 1:
                    pe.wait_ge(gn["sq"], n)
                    head_sums(4, n - 1, Z[:, 26 + (n - 1) % 2, :]).then_inc(gn["var"], 1)
            pe.wait_ge(gn["sq"], KT)
            head_sums(4, KT - 1, Z[:, 26 + (KT - 1) % 2, :]).then_inc(gn["var"], 1)
            pe.wait_ge(gn["yc"], KT)
            pe.wait_ge(gn["root"], 2)
            for n in range(KT):
                if n >= 2:
                    pe.wait_ge(gn["out"], n - 1)
                head_cast(5 + n % 2, n)
                mm(ps[:, [7, 0][n % 2], :], w(RING - 1, n), TG, start=True, stop=True).then_inc(gn["cast"], 1)
            pe.wait_ge(gn["out"], KT)
            pe.sem_inc(used, 1)
            gemm(B_RWKV + C_RKV + C_LORA + C_G2, C_RWO, AH, YL, t_ready, 32, SRC["rwo"])
            rms_out(8)
            tail(1)

        @block.scalar
        def _(act):
            av = nc.scalar.activation

            def round_chunk(quad, j):
                act.wait_ge(landed[j], quad * 16 + 16)
                av(RH[:, j, :], ring[:, j, :], ACT.Copy).then_inc(w_hi, 1)

            def ahead(quad, j, end=None):
                if end is None or quad * RING + j + 3 < end:
                    round_chunk(quad + (j + 3) // RING, (j + 3) % RING)

            def round_run(quad, before):
                act.wait_ge(used, before)
                for j in range(RING - 1):
                    round_chunk(quad, j)

            def layer_norm(l, i, bias):
                s, at = ln, l * 2 + i
                for n in range(KT):
                    act.wait_ge(s["xc"], at * KT + n + 1)
                    av(T1[:, n, :], X[:, n, :], ACT.Square).then_inc(s["sq"], 1)
                act.wait_ge(s["var"], at + 1)
                av(RS[:], ps[:, 5, :], ACT.Sqrt, bias=cst("eps")).then_inc(s["std"], 1)
                for n in range(KT):
                    act.wait_ge(s["y"], at * KT + n + 1)
                    av(XH[:, n, :], X[:, n, :], ACT.Identity, bias=par(bias, n, 1)).then_inc(s["hi"], 1)

            act.sem_inc(zc, 4)
            act.sem_inc(mg, 4)
            act.sem_inc(x1pre, 4)
            act.sem_inc(x2pre, 4)
            act.sem_inc(up_c, 4)
            act.sem_inc(up_h, 2)
            for free in (lru_in, t_ready, mq, mup, rkv):
                act.sem_inc(free, 4)
            for L in range(2):
                act.sem_inc(ch[L]["s"], 1)
            for j in range(RING - 1):
                round_chunk(0, j)
                if j < 2:
                    act.wait_ge(x_in[j], 16)
                    for n in range(j * KT // 2, (j + 1) * KT // 2):
                        av(XH[:, n, :], X[:, n, :], ACT.Copy).then_inc(x0_hi, 1)
            act.wait_ge(cst_in, 16)
            with act.Fori(0, DEPTH) as l:
                C, Q = l * CPL, l * (CPL // RING)
                act.wait_ge(x_ready, l * 16 + 16)
                act.dma_start(PAR[:], a["par"][bass.ds(l, 1)].rearrange("a p c -> (a p) c")).then_inc(par_in, 16)
                with act.Fori(0, C_Z // RING) as i:
                    for j in range(RING):
                        act.wait_ge(used, C + i * RING + (j + 1))
                        ahead(Q + i, j)
                        av(Z[:, bass.ds(i * RING + j, 1), :], ps[:, j:j + 1, :], ACT.Copy).then_inc(zc, 1)
                def passed(c):
                    act.wait_ge(used, C + c + 1)
                    if not B_PHI <= c + 3 < B_DV2:
                        round_chunk(Q + (c + 3) // RING, (c + 3) % RING)

                for c in range(B_VSG, B_DV):
                    passed(c)
                for t in range(ST):
                    av(VSG[:, t, :], ps[:, t, 0:VSG_N], ACT.Copy).then_inc(tokc, 1)
                act.wait_ge(rope, l * NR + Z_KC - Z_DQ + 1)
                for r in range(2):
                    act.dma_start(SWAP[(1 - r) * HD:(1 - r) * HD + HD, :, :], Z[r * HD:r * HD + HD, Z_KC:Z_VC + 1, :]).then_inc(kv_swap, 16)
                act.wait_ge(tokc, l * 8 + 4)
                av(GSIG[:].rearrange("p t b h -> p t (b h)"), VSG[:, :, 2 * P:VSG_N], ACT.Sigmoid).then_inc(gsig, 1)
                for c in range(B_DV, B_DV2):
                    passed(c)
                for kv in range(2):
                    av(HB[:, kv, :], ps[0:NB, 4 + kv, 0:P], ACT.Gelu).then_inc(cmp_step, 1)
                for c in range(B_DV2, B_MERGE):
                    passed(c)
                for t in range(ST):
                    av(DV[:, t, :], ps[:, t, :], ACT.Copy).then_inc(tokc, 1)
                act.wait_ge(lam_step, l * 2 + 1)
                av(LAM[:, 2 * HD + 2:2 * HD + 4], LAM[:, 2 * HD:2 * HD + 2], ACT.Exp).then_inc(lam_step, 1)
                def turned(u):
                    W = (UNITS[u][1] + 1) * P
                    for i in range(2):
                        t = HEADS_BEFORE[u] + i
                        act.wait_ge(at_tr, l * NHEADS + t + 1)
                        if t >= 4:
                            act.wait_ge(at_av, l * NHEADS + t - 3)
                        av(PT[:, t % 4, 0:W], ps[:, 4 + t % 2, 0:W], ACT.Copy).then_inc(at_pta, 1)

                def exps(u):
                    W = (UNITS[u][1] + 1) * P
                    act.wait_ge(at_max, l * NU + u + 1)
                    if u >= 2:
                        act.wait_ge(at_av, l * NHEADS + HEADS_BEFORE[u - 1])
                    for m in range(4):
                        ins = av(PROB[:, (u % 2) * 4 + m, 0:W], ps[:, m, 0:W], ACT.Exp, bias=AM[:, u % 2, 1, m:m + 1],
                                 scale=SCALE, accum_out=AM[:, u % 2, 2, m:m + 1])
                    ins.then_inc(at_exp, 1)

                def gate(g):
                    act.wait_ge(used, C + B_MERGE + g + 1)
                    ahead(Q + (B_MERGE + g) // RING, g % RING)
                    av(GATES[g], ps[:, 7, :], ACT.Sigmoid).then_inc(sg, 1)

                exps(0)
                act.wait_ge(cs_step, l * 4 + 2)
                av(CS[:], CS[:], ACT.Exp, scale=SCALE).then_inc(cs_step, 1)
                for u in range(NU):
                    if U_CS <= u < U_SEL:
                        qi = u - U_CS
                        act.wait_ge(cs_tr, l * ST + qi + 1)
                        if qi >= 2:
                            act.wait_ge(cs_av, l * ST + qi - 1)
                        av(SCR[0:NCMP, 2 * (qi % 2):2 * (qi % 2) + 2, :], ps[0:NCMP, 4:6, :], ACT.Copy).then_inc(cs_pt, 1)
                    if u + 1 < NU:
                        exps(u + 1)
                    turned(u)
                    gate(u)
                    if u == U_SEL + 3:
                        act.wait_ge(at_out, l * NU + U_SEL)
                        av(SCR[:, 0:4, :], YB.rearrange("p t h d -> p t (h d)"), ACT.Square).then_inc(yb_step, 1)
                        for c in range(4):
                            av(YH[c], Y[:, c, :], ACT.Copy).then_inc(y_hi, 1)
                    if u == U_SEL + 5:
                        act.wait_ge(yb_step, l * 4 + 2)
                        av(MS[:, 1, :], MS[:, 0, :], ACT.Sqrt, bias=cst("eps"), scale=1.0 / P).then_inc(yb_step, 1)
                for c in range(8):
                    act.wait_ge(ytr, l * 8 + c + 1)
                    kw = {"scale": LAM[:, 2 * HD + 6:2 * HD + 7]} if c < 4 else {}
                    av(YH[4 + c], ps[:, c, :], ACT.Copy, **kw).then_inc(y_hi, 1)
                for c in range(12):
                    act.wait_ge(used, C + B_BR + c + 1)
                    ahead(Q + (B_BR + c) // RING, c % RING)
                for n in range(KT):
                    act.wait_ge(mg, l * 24 + 4 + 16 + n + 1)
                    av(MR[n], M[n], ACT.Copy).then_inc(m_hi, 1)
                for c in range(C_WO):
                    act.wait_ge(used, C + B_WO + c + 1)
                    ahead(Q + (B_WO + c) // RING, c % RING)
                layer_norm(l, 0, "ln1_b")
                with act.Fori(0, C_UP // RING) as i:
                    for e in range(2):
                        act.wait_ge(up_h, l * FT + i * 2 + (e + 1))
                        for v in range(2):
                            j = 2 * e + v
                            act.wait_ge(used, C + B_UP + i * RING + (j + 1))
                            ahead(Q + B_UP // RING + i, j)
                            f = i * 2 + (e + v * FT)
                            av(T1[:, j, :], ps[:, j, :], ACT.Identity, bias=PAR[:, bass.ds(f + PCOL["up_b"][0], 1)],
                               scale=PAR[:, bass.ds(f + (PCOL["up_w"][0] + 2 * 2 * FT), 1)]).then_inc(up_a, 1)
                        act.wait_ge(up_c, l * C_UP + i * RING + (2 * e + 5))
                        av(T1[:, 4 + e, :], T1[:, 2 * e, :], ACT.Gelu).then_inc(up_g, 1)
                with act.Fori(0, C_DOWN // RING) as i:
                    for j in range(RING):
                        act.wait_ge(used, C + B_DOWN + i * RING + (j + 1))
                        ahead(Q + B_DOWN // RING + i, j)
                layer_norm(l, 1, "ln2_b")

            def rms(i, src, ready, base, cols=S):
                for n in range(KT):
                    if ready is not None:
                        act.wait_ge(ready, base + n + 1)
                    av(T[:, n, 0:cols], src[:, n, :], ACT.Square).then_inc(rms_sq, 1)
                act.wait_ge(rms_var, i + 1)
                if i == 1:
                    act.wait_ge(rms_y, NORMED[0])
                av(RS[:, 0:cols], ps[:, 5, 0:cols], ACT.Sqrt, bias=par2("rms_eps")).then_inc(rms_std, 1)

            def rms_out(i):
                act.wait_ge(rms_var, i + 1)
                av(RS[:], ps[:, 5, :], ACT.Sqrt, bias=par2("rms_eps")).then_inc(rms_std, 1)

            def copies(first, tiles, dst, at, done, func=ACT.Copy, cols=S, bias=None, bank=0, split=True, end=None):
                def quad(i):
                    for j in range(RING):
                        act.wait_ge(used, i * RING + (first + j + 1))
                        if split:
                            ahead(i + first // RING, j, end)
                        kw = {} if bias is None else {"bias": PAR2[:, bass.ds(i * RING + (bias + j), 1)]}
                        av(dst[:, bass.ds(i * RING + (at + j), 1), :], ps[:, bank + j:bank + j + 1, 0:cols], func, **kw).then_inc(done, 1)

                with act.Fori(0, tiles // RING - (end is not None)) as i:
                    quad(i)
                if end is not None:
                    quad(tiles // RING - 1)

            def rounded(hi, src, ready, base):
                for n in range(KT):
                    act.wait_ge(ready, base + n + 1)
                    av(hi[:, n, :], src[:, n, :], ACT.Copy).then_inc(src_hi, 1)

            def tail(l):
                B = B_TAIL0 if l == 0 else B_TAIL1
                act.wait_ge(rms_y, NORMED[1])
                av(MNH, MN, ACT.Copy).then_inc(mem_hi, 1)
                rms(3 + 6 * l, X, xr2, 3 * KT * l + KT)
                rounded(AH, N, rms_y, NORMED[3 + 6 * l] - KT)
                copies(B, C_MQ, Z, 0, mq)
                copies(B + C_MQ, C_MK, MK, 0, mq, cols=S2)
                for c in range(C_MV):
                    act.wait_ge(used, B + C_MQ + C_MK + c + 1)
                    ahead((B + C_MQ + C_MK + c) // RING, c % RING)
                    if c % RING == RING - 1:
                        half = c // RING
                        for t in range(2):
                            av(MV[:, t, half * 512:half * 512 + 512], ps[:, 4 + 2 * half + t, :], ACT.Copy).then_inc(mv, 1)

                def exps(qi):
                    act.wait_ge(m_max, l * ST + qi + 1)
                    if qi >= 2:
                        act.wait_ge(m_tr, l * 2 * ST + 2 * (qi - 1))
                    for h in range(MH):
                        ins = av(MP[:, qi % 2, h, :], ps[:, 2 * (qi % 2) + h // 2, (h % 2) * S2:(h % 2) * S2 + S2], ACT.Exp,
                                 bias=AM[:, qi % 2, 1, h:h + 1], scale=(MT * P) ** -0.5, accum_out=AM[:, qi % 2, 2, h:h + 1])
                    ins.then_inc(m_exp, 1)

                exps(0)
                for qi in range(ST):
                    if qi + 1 < ST:
                        exps(qi + 1)
                    for kb in range(2):
                        act.wait_ge(m_tr, l * 2 * ST + 2 * qi + kb + 1)
                        av(Z[:, 16 + kb:24:2, qi * P:qi * P + P],
                           ps[:, 4 + 2 * (qi % 2) + kb, :].rearrange("p (h q) -> p h q", h=MH), ACT.Copy).then_inc(m_pt, 1)
                for c in range(KT):
                    act.wait_ge(m_o, l * KT + c + 1)
                    av(AH[:, c, :], ps[:, c % 4, :], ACT.Copy).then_inc(src_hi, 1)
                copies(B + C_MQ + C_MK + C_MV, C_MO, N, 0, t_ready, bank=4)
                rms_out(4 + 6 * l)
                rms(5 + 6 * l, X, xr2, 3 * KT * l + 2 * KT)
                rounded(AH, N, rms_y, NORMED[5 + 6 * l] - KT)
                for h in range(2):
                    U = B + B_MFF + h * (C_HUP + C_HDN)
                    with act.Fori(0, C_HUP // RING) as i:
                        for j in range(RING):
                            act.wait_ge(used, i * RING + (U + j + 1))
                            ahead(i + U // RING, j)
                            act.wait_ge(mup, i * RING + (l * F2T + h * HALF + j + 1))
                            av(RELU[:, j, :], ps[:, 4 + j, :], ACT.Relu).then_inc(mup_r, 1)
                    for c in range(C_HDN):
                        act.wait_ge(used, U + C_HUP + c + 1)
                        ahead((U + C_HUP + c) // RING, c % RING, B + C_TAIL)
                        if h == 0 and c % 2:
                            n = c // 2
                            av(PART[:, n, :], ps[:, n % 4, :], ACT.Copy).then_inc(t_ready, 1)
                rms_out(6 + 6 * l)

            act.wait_ge(x_ready, 16 * (DEPTH + 1))
            act.dma_start(MN, a["mem"]).then_inc(mem_in, 16)
            act.wait_ge(par2_in, 16)
            rms(0, X, xr2, 0)
            rounded(AH, N, rms_y, NORMED[0] - KT)
            copies(B_LRU, KT, Z, 0, lru_in, ACT.Gelu_apprx_tanh, bias=P2COL["b_in"][0])
            copies(B_LRU + KT, KT, Z, 8, lru_in, ACT.Identity, bias=P2COL["b_in"][0] + KT, end=B_LRU + C_LRU_IN)
            act.wait_ge(mem_in, 16)
            rms(1, MN, None, 0, S2)
            act.wait_ge(lru_rate, 1)
            av(LRU[:, 1, :], LRU[:, 0, :], ACT.Exp, scale=-1.0).then_inc(lru_rate, 1)
            act.wait_ge(lru_rate, 3)
            av(LRU[:, 3, :], LRU[:, 2, :], ACT.Ln).then_inc(lru_rate, 1)
            def lru_gates(*chunks):
                for c in chunks:
                    act.wait_ge(used, B_LRU + C_LRU_IN + c + 1)
                    for b in range(4):
                        n = (c % 2) * 4 + b
                        av((Y if c < 2 else T)[:, n, :], ps[:, 4 * (c % 2) + b, :], ACT.Sigmoid,
                           bias=par2("gate_b", (c // 2) * KT + n, 1)).then_inc(lru_gate, 1)

            lru_gates(0, 1)
            act.wait_ge(lru_gate, KT)
            act.wait_ge(lru_rate, 5)
            for n in range(KT):
                av(Z[:, 8 + n, :], Y[:, n, :], ACT.Tanh, scale=LRU[:, 2, n:n + 1]).then_inc(lru_ea, 1)
            lru_gates(2)
            round_run((B_LRU + C_LRU_IN + C_LRU_GATE) // RING, B_LRU + C_LRU_IN + C_LRU_GATE)
            lru_gates(3)
            for n in range(KT):
                av(N[:, n, :], Y[:, n, :], ACT.Exp, scale=LRU[:, 1, n:n + 1]).then_inc(lru_ea, 1)
                av(Y[:, n, :], Y[:, n, :], ACT.Exp, scale=LRU[:, 3, n:n + 1]).then_inc(lru_ea, 1)
            for n in range(KT):
                act.wait_ge(lru_q, n + 1)
                av(Z[:, 8 + n, :], Z[:, 8 + n, :], ACT.Sqrt).then_inc(lru_m, 1)
            rounded(AH, Z[:, 16:24, :], lru_y, 0)
            copies(B_LRU + C_LRU_IN + C_LRU_GATE, C_LRU_OUT, N, 0, t_ready, ACT.Identity, bias=P2COL["b_out"][0])
            rms_out(2)
            tail(0)

            act.dma_start(CST2[:, 0:NCST2], a["cst2"]).then_inc(cst2_in, 16)
            rms(7, X, xr2, 3 * KT)
            copies(B_RWKV, KT, Z, 8, rkv, split=False)
            act.wait_ge(lora, 1)
            av(TW, ps[0:HD, 4, :], ACT.Tanh).then_inc(la, 1)
            act.wait_ge(used, B_LORA + 1)
            av(TA_, ps[0:HD, 5, :], ACT.Copy).then_inc(la, 1)
            act.wait_ge(used, B_LORA + 2)
            av(TG, ps[:, 6, :], ACT.Sigmoid).then_inc(la, 1)
            act.wait_ge(mix, 6 * KT)
            for i, (dst, bias, done) in enumerate(((N, "w0", lw), (Y, "a0", la))):
                for n in range(KT):
                    if n < KT - 1:
                        act.wait_ge(lora, 2 + i * (KT - 1) + n)
                    else:
                        act.wait_ge(used, B_LORA + 3 + i)
                    av(dst[:, n, :], ps[:, 4 * i + n % 4, :], ACT.Sigmoid, bias=par2(bias, n, 1)).then_inc(done, 1)
            copies(B_V, KT, Z, 16, rkv, split=False)
            for n in range(KT):
                av(T[:, n, :], Z[:, 8 + n, :], ACT.Copy, scale=par2("k_k", n, 1))
                if n >= 4:
                    act.wait_ge(kk["sum"], n - 3)
                av(Z[:, 24 + n % 4, :], Z[:, 8 + n, :], ACT.Square, scale=par2("k_k", n, 1)).then_inc(kk["sq"], 1)
            for n in range(KT):
                if n == 4:
                    act.wait_ge(kk["sum"], KT)
                    av(ROWS, ps[0:NHR, 4, :], ACT.Sqrt).then_inc(kk["root"], 1)
                act.wait_ge(used, B_R + n + 1)
                av(Z[:, n, :], ps[:, (B_R + n) % 4, :], ACT.Copy).then_inc(rkv, 1)
            act.wait_ge(cum, KT)
            av(MID[:, 1:3], MID[:, 1:3], ACT.Exp, scale=-K0).then_inc(mid_e, 1)
            act.wait_ge(kk["done"], KT)
            with act.Fori(0, RC) as c:
                for half in range(2):
                    def lane(L):
                        return ch[L], LANES[L], 4 * L, 2 * (2 * half + L), c * 2 + half

                    for L in range(2):
                        s, B, o, n0, it = lane(L)
                        act.wait_ge(s["s"], it + 1)
                        lws = N[:, n0:n0 + 2, bass.ds(c * P, P)]
                        av(B["e"][:, :, 0, 1:P + 1], lws, ACT.Exp, scale=-K0)
                        av(B["e"][:, :, 1, 0:P], lws, ACT.Exp, scale=K0)
                        av(B["e"][:, :, 0, 0:1], MID[:, 0, n0:n0 + 2, bass.ds(c, 1)], ACT.Exp, scale=K0)
                        av(B["x"][:, 0:2, :], Z[:, 16 + n0:18 + n0, bass.ds(c * P, P)], ACT.Copy).then_inc(s["exp"], 1)
                    for L in range(2):
                        s, B, o, n0, it = lane(L)
                        act.wait_ge(s["tr"], it + 1)
                        av(B["bktok"].rearrange("p a n c -> p (a n c)"), ps[:, o, :], ACT.Copy)
                        av(B["vtok"].rearrange("p n c -> p (n c)"), ps[:, o + 1, 0:2 * P], ACT.Copy).then_inc(s["tok"], 1)
                    for L in range(2):
                        s, B, o, n0, it = lane(L)
                        act.wait_ge(s["x0"], it + 1)
                        av(B["x"].rearrange("p q t -> p (q t)"), ps[:, o + 2, :], ACT.Copy).then_inc(s["xc"], 1)
                    for v in range(LEVELS):
                        for L in range(2):
                            s, B, o, n0, it = lane(L)
                            for e, t in enumerate(("x", "xt")):
                                act.wait_ge(s["x"], it * (2 * LEVELS) + 2 * v + e + 1)
                                av(B[t].rearrange("p q t -> p (q t)"), ps[:, o + 1 + e, :], ACT.Copy).then_inc(s["xc"], 1)
                    for L in range(2):
                        s, B, o, n0, it = lane(L)
                        act.wait_ge(s["p"], it + 1)
                        for r in range(2):
                            ins = av(B["pu"][:, 0, r:4:2, :], ps[:, o + r, 0:2 * HD].rearrange("p (n i) -> p n i", n=2), ACT.Copy)
                        ins.then_inc(s["pc"], 1)
                    for L in range(2):
                        s, B, o, n0, it = lane(L)
                        act.wait_ge(s["u"], it + 1)
                        av(B["pu"][:, 1].rearrange("p q i -> p (q i)"), ps[:, o + 2, 0:4 * HD], ACT.Copy).then_inc(s["uc"], 1)
                    for L in range(2):
                        s, B, o, n0, it = lane(L)
                        act.wait_ge(s["s"], it + 2)
                        av(T[:, n0:n0 + 2, bass.ds(c * P, P)], ps[:, o + 3, 0:2 * P].rearrange("p (n t) -> p n t", n=2),
                           ACT.Copy).then_inc(s["yc"], 1)
            round_run((B_RWKV + C_RKV + C_LORA + C_G2) // RING, B_RWKV + C_RKV + C_LORA + C_G2 - 1)
            for n in range(KT):
                act.wait_ge(gn["center"], n + 1)
                if n >= 2:
                    act.wait_ge(gn["var"], n - 1)
                av(Z[:, 26 + n % 2, :], ps[:, n % 2, :], ACT.Square).then_inc(gn["sq"], 1)
                av(T[:, n, :], ps[:, n % 2, :], ACT.Copy).then_inc(gn["yc"], 1)
            act.wait_ge(gn["var"], KT)
            av(ROWS, ps[0:NHR, 4, :], ACT.Sqrt, bias=par2("gn_eps")[0:NHR], scale=1.0 / HD).then_inc(gn["root"], 1)
            rounded(AH, Y, gn["out"], 0)
            copies(B_RWKV + C_RKV + C_LORA + C_G2, C_RWO, N, 0, t_ready)
            rms_out(8)
            tail(1)

        @block.vector
        def _(dve):
            v = nc.vector
            tt, ts, stt = v.tensor_tensor, v.tensor_scalar, v.scalar_tensor_tensor

            def remainder(lo, whole, hi, done, each=1):
                tt(lo, whole, hi, ALU.subtract).then_inc(done, each)

            def layer_norm(l, i, gain, bias, done, each):
                s, at = ln, l * 2 + i
                dve.wait_ge(s["mean"], at + 1)
                for n in range(KT):
                    tt(X[:, n, :], X[:, n, :], ps[:, 4, :], ALU.subtract).then_inc(s["xc"], 1)
                dve.wait_ge(s["std"], at + 1)
                v.reciprocal(RS[:], RS[:])
                dve.drain()
                for t in range(KT + 2):
                    if t < KT:
                        stt(X[:, t, :], X[:, t, :], par(gain, t, 1), RS[:], ALU.mult, ALU.mult).then_inc(s["y"], 1)
                    if t >= 2:
                        n = t - 2
                        dve.wait_ge(s["hi"], at * KT + n + 1)
                        stt(XL[:, n, :], X[:, n, :], par(bias, n, 1), XHF[:, n, :], ALU.add, ALU.subtract).then_inc(done, each)

            def whole_residual(x, xl, xh, out, done):
                stt(x, xl.bitcast(F32), ALPHA, out, ALU.mult, ALU.add)
                dve.drain()
                stt(x, xh, ALPHA, x, ALU.mult, ALU.add)
                dve.drain()
                tt(RS[:].unsqueeze(1), RS[:].unsqueeze(1), x, ALU.add).then_inc(done, 1)

            def maxima(l, u):
                W = (UNITS[u][1] + 1) * P
                dve.wait_ge(at_sc, l * NU + u + 1)
                v.tensor_reduce(AM[:, u % 2, 0, :], ps[:, 0:4, 0:W], AXX, ALU.max)
                dve.drain()
                ts(AM[:, u % 2, 1, :], AM[:, u % 2, 0, :], -SCALE, None, ALU.mult).then_inc(at_max, 1)

            def factors(l, u):
                kind, qi, which = UNITS[u]
                W = (qi + 1) * P
                dve.wait_ge(at_exp, l * NU + u + 1)
                v.reciprocal(AM[:, u % 2, 3, :], AM[:, u % 2, 2, :])
                dve.drain()
                if kind == "diff":
                    ts(AM[:, u % 2, 3, 1:4:2], AM[:, u % 2, 3, 1:4:2], LAM[:, 2 * HD + 5:2 * HD + 6], None, ALU.mult)
                    dve.drain()
                    for i in range(2):
                        b = (u % 2) * 4 + 2 * i
                        ts(PROB[:, b + 1, 0:W], PROB[:, b + 1, 0:W], AM[:, u % 2, 3, 2 * i + 1:2 * i + 2], None, ALU.mult)
                    dve.drain()
                    for i in range(2):
                        b = (u % 2) * 4 + 2 * i
                        ins = stt(PROB[:, b, 0:W], PROB[:, b, 0:W], AM[:, u % 2, 3, 2 * i:2 * i + 1], PROB[:, b + 1, 0:W], ALU.mult, ALU.add)
                    ins.then_inc(at_comb, 1)
                else:
                    tt(AM[:, u % 2, 3, :], AM[:, u % 2, 3, :], GSIG[:, qi, 1 + kind, which * HPG:which * HPG + HPG], ALU.mult)

            def turned(l, u):
                W = (UNITS[u][1] + 1) * P
                for i in range(2, HEADS_OF[u]):
                    t = HEADS_BEFORE[u] + i
                    dve.wait_ge(at_tr, l * NHEADS + t + 1)
                    if t >= 4:
                        dve.wait_ge(at_av, l * NHEADS + t - 3)
                    v.tensor_copy(PT[:, t % 4, 0:W], ps[:, 4 + t % 2, 0:W]).then_inc(at_ptd, 1)

            def outputs(l, u):
                kind, qi, which = UNITS[u]
                dve.wait_ge(at_av, l * NHEADS + HEADS_BEFORE[u + 1])
                if kind == "diff":
                    v.tensor_copy(YB[:, qi, 2 * which:2 * which + 2, :],
                                  ps[:, 6, 0:2 * P].rearrange("p (h d) -> p h d", h=2)).then_inc(at_out, 1)
                else:
                    o = YC_ADD.rearrange("p (h d) -> p h d", h=HPG)
                    tt(o, ps[:, 6, 0:HPG * HD].rearrange("p (h d) -> p h d", h=HPG),
                       AM[:, u % 2, 3, :].unsqueeze(2).to_broadcast([P, HPG, HD]), ALU.mult)
                    dve.drain()
                    y = YC[:, qi, which * HPG:which * HPG + HPG, :]
                    tt(y, y, o, ALU.add).then_inc(at_out, 1)

            for n in range(KT):
                dve.wait_ge(x0_hi, n + 1)
                remainder(XL[:, n, :], X[:, n, :], XHF[:, n, :], x_ready, 2)
            dve.wait_ge(cst_in, 16)
            v.tensor_copy(CONST_R[:, 0:P], cst("ident"))
            v.tensor_copy(CONST_R[:, P:2 * P], cst("maskneg")).then_inc(const_r, 1)
            with dve.Fori(0, DEPTH) as l:
                C = l * CPL
                dve.wait_ge(par_in, l * 16 + 16)
                lam4 = par("lam").rearrange("p (a b d) -> p a b d", a=2, b=2)
                tt(LAM[:, 0:2 * HD].rearrange("p (a d) -> p a d", a=2), lam4[:, :, 0, :], lam4[:, :, 1, :], ALU.mult)
                dve.drain()
                v.tensor_reduce(LAM[:, 2 * HD:2 * HD + 2], LAM[:, 0:2 * HD].rearrange("p (a d) -> p a d", a=2), AXX, ALU.add).then_inc(lam_step, 1)
                ts(LAM[:, 2 * HD + 6:2 * HD + 7], par("subln"), par("lam_keep"), None, ALU.mult)
                dve.wait_ge(zc, l * C_Z + 4 + Z_DQ)
                for c in range(4):
                    tt(SCR[:, 4 + c, :], Z[:, Z_AC + c, :], Z[:, Z_AV + c, :], ALU.mult)
                dve.drain()
                for c in range(4):
                    ts(Y[:, c, :], SCR[:, 4 + c, :], par("conv_a", 8 + c, 1), None, ALU.mult)
                for k in (1, 0):
                    dve.drain()
                    for c in range(4):
                        y = Y[:, c, 2 - k:S]
                        stt(y, SCR[:, 4 + c, 0:S - 2 + k], par("conv_a", 4 * k + c, 1), y, ALU.mult, ALU.add)
                dve.drain()
                for c in range(4):
                    tt(Y[:, c, :], Y[:, c, :], Z[:, Z_AB + c, :], ALU.mult).then_inc(conv_out, 1)
                dve.drain()
                for r, t in enumerate(ROPE_TILES):
                    dve.wait_ge(rot, l * NR + r + 1)
                    tt(SCR[:, 4 + r % 2, :], ps[:, 4 + r % 4, :], cst("sin"), ALU.mult)
                    tt(Z[:, t, :], Z[:, t, :], cst("cos"), ALU.mult)
                    dve.drain()
                    tt(Z[:, t, :], Z[:, t, :], SCR[:, 4 + r % 2, :], ALU.add).then_inc(rope, 1)
                dve.wait_ge(kv_swap, l * 32 + 32)
                for kv in range(2):
                    for half in range(2):
                        p0 = PCOL["pos"][0] + kv * CMP_BLOCK + half * CMP_STRIDE
                        for g in range(NG):
                            for odd in range(2):
                                r = slice(odd * HD, odd * HD + HD)
                                src = Z[r, Z_KC + kv, :] if g == odd else SWAP[r, kv, :]
                                src = src.rearrange("p (n e two) -> p n e two", e=8, two=2)[:, half:half + NCMP, :, odd]
                                pos = PAR[r, p0 + odd:p0 + CMP_STRIDE:2].unsqueeze(1).to_broadcast([HD, NCMP, 8])
                                ins = tt(BLK[r, kv, half, :, g * NCMP:g * NCMP + NCMP].rearrange("p e n -> p n e"), src, pos, ALU.add)
                ins.then_inc(cmpin, 1)
                dve.wait_ge(cmp_step, l * 6 + 3)
                v.tensor_copy(H[:], ps[:, 6, 0:2 * NB].rearrange("p (a g n) -> p a g n", a=2, g=NG)).then_inc(cmp_step, 1)
                dve.wait_ge(cmp_step, l * 6 + 5)
                for g in range(NG):
                    o = g * HD
                    v.tensor_copy(KCC[o:o + HD, 0:NCMP], ps[o:o + HD, 4, g * 32:g * 32 + NCMP])
                v.tensor_copy(VCC[0:NCMP, :, :], ps[0:NCMP, 5, 0:NG * HD].rearrange("p (g d) -> p g d", g=NG)).then_inc(cmp_step, 1)
                dve.wait_ge(lam_step, l * 2 + 2)
                tt(LAM[:, 2 * HD + 4:2 * HD + 5], LAM[:, 2 * HD + 3:2 * HD + 4], LAM[:, 2 * HD + 2:2 * HD + 3], ALU.subtract)
                dve.drain()
                tt(LAM[:, 2 * HD + 5:2 * HD + 6], LAM[:, 2 * HD + 4:2 * HD + 5], par("lam_init"), ALU.subtract)
                maxima(l, 0)
                dve.wait_ge(cs_step, l * 4 + 1)
                cm = cst("cmask").rearrange("p (t n) -> p t n", t=ST)
                cv = cst("cvalid").rearrange("p (t n) -> p t n", t=ST)
                for qi in range(ST):
                    for g in range(NG):
                        tt(CS[:, qi, g * HPG:g * HPG + HPG, :],
                           ps[:, 6 + g, qi * P:qi * P + P].rearrange("p (h n) -> p h n", h=HPG)[:, :, 0:NCMP],
                           cm[:, qi].unsqueeze(1).to_broadcast([P, HPG, NCMP]), ALU.add)
                dve.drain()
                csf = CS[:].rearrange("p t h n -> p (t h) n")
                v.tensor_reduce(CM[:, 0, :], csf, AXX, ALU.max)
                dve.drain()
                tt(csf, csf, CM[:, 0, :].unsqueeze(2).to_broadcast([P, ST * NH, NCMP]), ALU.subtract).then_inc(cs_step, 1)

                def compressed_sums():
                    dve.wait_ge(cs_step, l * 4 + 3)
                    v.tensor_reduce(CM[:, 1, :], csf, AXX, ALU.add)
                    dve.drain()
                    for qi in range(ST):
                        ins = tt(CS[:, qi], CS[:, qi], cv[:, qi].unsqueeze(1).to_broadcast([P, NH, NCMP]), ALU.mult)
                    ins.then_inc(cs_step, 1)
                    v.reciprocal(CM[:, 2, :], CM[:, 1, :])
                    dve.drain()
                    dve.wait_ge(gsig, l + 1)
                    c2, c3 = [CM[:, i, :].rearrange("p (t h) -> p t h", t=ST) for i in (2, 3)]
                    tt(c3, c2, GSIG[:, :, 0, :], ALU.mult)

                def compressed_output(qi):
                    dve.wait_ge(cs_av, l * ST + qi + 1)
                    tt(YC[:, qi], ps[:, 6, :].rearrange("p (h d) -> p h d", h=NH),
                       CM[:, 3, qi * NH:qi * NH + NH].unsqueeze(2).to_broadcast([P, NH, HD]), ALU.mult).then_inc(cs_out, 1)

                compressed_sums()
                for u in range(NU):
                    factors(l, u)
                    if u + 1 < NU:
                        maxima(l, u + 1)
                    if U_CS <= u < U_SEL:
                        compressed_output(u - U_CS)
                    turned(l, u)
                    outputs(l, u)
                    if u == U_SEL + 4:
                        dve.wait_ge(yb_step, l * 4 + 1)
                        v.tensor_reduce(MS[:, 0, :], SCR[:, 0:4, :].rearrange("p t (h d) -> p (t h) d", h=DH), AXX, ALU.add).then_inc(yb_step, 1)
                        for c in range(4):
                            dve.wait_ge(y_hi, l * 12 + c + 1)
                            remainder(YLs[c], Y[:, c, :], YH[c].bitcast(F32), y_lo)
                    if u == U_SEL + 6:
                        dve.wait_ge(yb_step, l * 4 + 3)
                        v.reciprocal(MS[:, 1, :], MS[:, 1, :])
                        dve.drain()
                        ybf = YB.rearrange("p t h d -> p (t h) d")
                        tt(ybf, ybf, MS[:, 1, :].unsqueeze(2).to_broadcast([P, ST * DH, P]), ALU.mult).then_inc(yb_step, 1)
                for c in range(8):
                    dve.wait_ge(y_hi, l * 12 + 4 + c + 1)
                    hi = YH[4 + c].bitcast(F32)
                    if c < 4:
                        stt(YLs[4 + c], ps[:, c, :], LAM[:, 2 * HD + 6:2 * HD + 7], hi, ALU.mult, ALU.subtract).then_inc(y_lo, 1)
                    else:
                        remainder(YLs[4 + c], ps[:, c, :], hi, y_lo)
                for b in range(3):
                    for n in range(KT):
                        g = GATES[b * KT + n]
                        dve.wait_ge(sg, l * NGATE + b * KT + n + 1)
                        dve.wait_ge(used, C + B_BR + b * 4 + n // 2 + 1)
                        ins = tt(g, g, ps[:, n % 4, :], ALU.mult)
                        if b > 0:
                            dve.drain()
                            ins = tt(M[n], M[n], g, ALU.add)
                        ins.then_inc(mg, 1)
                for n in range(KT):
                    dve.wait_ge(m_hi, l * KT + n + 1)
                    remainder(ML[n], M[n], MR[n].bitcast(F32), m_lo)
                v.memset(RS[:], 0.0)
                with dve.Fori(0, 2) as i:
                    for j in range(RING):
                        dve.wait_ge(used, C + B_WO + i * RING + (j + 1))
                        t = bass.ds(i * RING + j, 1)
                        whole_residual(X[:, t, :], XL[:, t, :], XHF[:, t, :], ps[:, j:j + 1, :], x1pre)
                dve.drain()
                layer_norm(l, 0, "ln1_g", "ln1_b", x1, 1)
                with dve.Fori(0, C_UP // RING) as i:
                    for e in range(2):
                        for b in range(2):
                            j = 2 * e + b
                            dve.wait_ge(up_a, l * C_UP + i * RING + (j + 1))
                            f = i * 2 + (e + b * FT)
                            for k in (1, 0):
                                y = T1[:, j, 2 - k:S]
                                ins = stt(y, ps[:, j, 0:S - 2 + k], PAR[:, bass.ds(f + (PCOL["up_w"][0] + k * 2 * FT), 1)], y, ALU.mult, ALU.add)
                                if k:
                                    dve.drain()
                            ins.then_inc(up_c, 1)
                        dve.drain()
                        dve.wait_ge(up_g, l * FT + i * 2 + (e + 1))
                        t = bass.ds(i * 2 + e, 1)
                        tt(FH[:, t, :], T1[:, 4 + e:5 + e, :], T1[:, 2 * e + 1:2 * e + 2, :], ALU.mult)
                        dve.drain()
                        v.tensor_copy(FHR[:, t, :], FH[:, t, :])
                        dve.drain()
                        remainder(FL[:, t, :], FH[:, t, :], FHRF[:, t, :], up_h)
                v.memset(RS[:], 0.0)
                with dve.Fori(0, 2) as i:
                    for n in range(4):
                        dve.wait_ge(used, C + B_DOWN + i * 12 + 3 * (n + 1))
                        t = bass.ds(i * 4 + n, 1)
                        whole_residual(X[:, t, :], XL[:, t, :], XHF[:, t, :], ps[:, n:n + 1, :], x2pre)
                dve.drain()
                layer_norm(l, 1, "ln2_g", "ln2_b", x_ready, 2)

            def inverse_root(i, cols=S):
                dve.wait_ge(rms_std, i + 1)
                v.reciprocal(RS[:, 0:cols], RS[:, 0:cols])
                dve.drain()

            def rms(i, src, dst, gain, cols=S):
                inverse_root(i, cols)
                for n in range(KT):
                    stt(dst[:, n, :], src[:, n, :], gain[:, n:n + 1], RS[:, 0:cols], ALU.mult, ALU.mult).then_inc(rms_y, 1)

            def square_sum(n):
                if n == 0:
                    tt(RS[:], N[:, n, :], N[:, n, :], ALU.mult)
                else:
                    dve.drain()
                    tt(TMP[1], N[:, n, :], N[:, n, :], ALU.mult)
                    dve.drain()
                    ins = tt(RS[:], RS[:], TMP[1], ALU.add)
                    if n == KT - 1:
                        ins.then_inc(rms_sq, KT)

            def squares(base):
                for n in range(KT):
                    dve.wait_ge(t_ready, base + n + 1)
                    square_sum(n)

            def residual(i, gain):
                inverse_root(i)
                for n0 in range(0, KT, 2):
                    for n in (n0, n0 + 1):
                        stt(T[:, n, :], N[:, n, :], gain[:, n:n + 1], RS[:], ALU.mult, ALU.mult)
                    dve.drain()
                    for n in (n0, n0 + 1):
                        tt(X[:, n, :], X[:, n, :], T[:, n, :], ALU.add).then_inc(xr2, 1)
                dve.drain()

            def rms_split(i, gain, base):
                inverse_root(i)
                for t in range(KT + 2):
                    if t < KT:
                        stt(N[:, t, :], X[:, t, :], gain[:, t:t + 1], RS[:], ALU.mult, ALU.mult).then_inc(rms_y, 1)
                    if t >= 2:
                        remainders(NL, N, base, t - 2, t - 1)

            def remainders(lo, whole, base, first=0, end=KT):
                for n in range(first, end):
                    dve.wait_ge(src_hi, base + n + 1)
                    remainder(lo[:, n, :], whole[:, n, :], XHF[:, n, :], src_lo)

            def gain(l, i):
                return par2("ln", (l * 6 + i) * KT, KT)

            def tail(l):
                dve.wait_ge(mem_hi, l + 1)
                remainder(MNL, MN, MNHF, mem_lo)
                rms_split(3 + 6 * l, gain(l, 2), SRC[f"q{l}"])

                def maxima2(qi):
                    dve.wait_ge(m_sc, l * ST + qi + 1)
                    v.tensor_reduce(AM[:, qi % 2, 0, :], ps[:, 2 * (qi % 2):2 * (qi % 2) + 2, :].rearrange("p b (h s) -> p (b h) s", h=2),
                                    AXX, ALU.max)
                    dve.drain()
                    ts(AM[:, qi % 2, 1, :], AM[:, qi % 2, 0, :], -((MT * P) ** -0.5), None, ALU.mult).then_inc(m_max, 1)

                maxima2(0)
                for qi in range(ST):
                    if qi + 1 < ST:
                        maxima2(qi + 1)
                    dve.wait_ge(m_exp, l * ST + qi + 1)
                    v.reciprocal(AM[:, qi % 2, 3, :], AM[:, qi % 2, 2, :])
                    dve.drain()
                    p = MP[:, qi % 2]
                    tt(p, p, AM[:, qi % 2, 3, :].unsqueeze(2).to_broadcast([P, MH, S2]), ALU.mult).then_inc(m_p, 1)
                for c in range(KT):
                    dve.wait_ge(src_hi, SRC[f"o{l}"] + c + 1)
                    remainder(YL[:, c, :], ps[:, c % 4, :], XHF[:, c, :], src_lo)
                squares(4 + l * 32 + 8)
                residual(4 + 6 * l, gain(l, 3))
                rms_split(5 + 6 * l, gain(l, 4), SRC[f"up{l}"])
                for h in range(2):
                    with dve.Fori(0, C_HUP // RING) as i:
                        for j in range(RING):
                            dve.wait_ge(mup_r, i * RING + (l * F2T + h * HALF + j + 1))
                            r, t = RELU[:, j:j + 1, :], bass.ds(i * RING + j, 1)
                            tt(HW[:, t, :], r, r, ALU.mult)
                            dve.drain()
                            v.tensor_copy(HR[:, t, :], HW[:, t, :])
                            dve.drain()
                            remainder(HL[:, t, :], HW[:, t, :], HRF[:, t, :], mup)
                U = B_TAIL0 if l == 0 else B_TAIL1
                for n in range(KT):
                    dve.wait_ge(used, U + C_TAIL - C_HDN + 2 * n + 2)
                    tt(N[:, n, :], PART[:, n, :], ps[:, n % 4, :], ALU.add).then_inc(t_ready, 1)
                    dve.drain()
                    square_sum(n)
                residual(6 + 6 * l, gain(l, 5))

            for n in range(KT):
                dve.wait_ge(x_ready, 16 * DEPTH + 2 * n + 2)
                tt(X[:, n, :], XL[:, n, :].bitcast(F32), XHF[:, n, :], ALU.add).then_inc(xr2, 1)
            dve.drain()
            dve.wait_ge(par2_in, 16)
            rms_split(0, gain(0, 0), SRC["lru_in"])
            for n0 in (0, 4):
                dve.wait_ge(lru_in, 4 + KT + n0 + 4)
                for n in range(n0, n0 + 4):
                    ts(Z[:, 16 + n, :], Z[:, 8 + n, :], par2("conv_w", 3 * KT + n, 1), par2("conv_b", n, 1), ALU.mult, ALU.add)
                for k in (2, 1, 0):
                    dve.drain()
                    for n in range(n0, n0 + 4):
                        y = Z[:, 16 + n, 3 - k:S]
                        ins = stt(y, Z[:, 8 + n, 0:S - 3 + k], par2("conv_w", k * KT + n, 1), y, ALU.mult, ALU.add)
                        if k == 0:
                            ins.then_inc(lru_conv, 1)
            dve.drain()
            lam = par2("lam")
            ts(LRU[:, 2, :], lam, -1.0, None, ALU.mult)
            dve.drain()
            tt(LRU[:, 0, :], lam, LRU[:, 2, :], ALU.max).then_inc(lru_rate, 1)
            dve.wait_ge(lru_rate, 2)
            e, u, d, low = LRU[:, 1, :], LRU[:, 2, :], LRU[:, 0, :], LAM[:, 0:KT]
            ts(u, e, 1.0, None, ALU.add).then_inc(lru_rate, 1)
            dve.drain()
            ts(d, u, -1.0, 1e-30, ALU.add, ALU.max)
            ts(low, e, -0.5, 1.0, ALU.mult, ALU.add)
            dve.drain()
            v.reciprocal(d, d)
            tt(low, low, e, ALU.mult)
            dve.drain()
            tt(d, d, e, ALU.mult)
            dve.wait_ge(lru_rate, 4)
            dve.drain()
            tt(d, d, LRU[:, 3, :], ALU.mult)
            ts(u, lam, -1.0, 0.0, ALU.mult, ALU.max)
            dve.drain()
            tt(d, d, low, ALU.max)
            dve.drain()
            tt(d, d, u, ALU.add)
            dve.drain()
            ts(LRU[:, 2, :], d, LRU_C, None, ALU.mult)
            ts(LRU[:, 1, :], d, -2 * LRU_C, None, ALU.mult)
            ts(LRU[:, 3, :], d, -LRU_C, None, ALU.mult).then_inc(lru_rate, 1)
            dve.drain()
            rms(1, MN, MN, par2("mem_norm"), S2)
            for n in range(KT):
                dve.wait_ge(lru_gate, KT + n + 1)
                tt(T[:, n, :], T[:, n, :], Z[:, 16 + n, :], ALU.mult)
            for n in range(KT):
                dve.wait_ge(lru_ea, KT + 2 * n + 1)
                stt(Z[:, 8 + n, :], N[:, n, :], 1.0, Z[:, 8 + n, :], ALU.add, ALU.mult).then_inc(lru_q, 1)
            for n0 in range(0, KT, 2):
                pair = (n0, n0 + 1)
                dve.drain()
                for n in pair:
                    dve.wait_ge(lru_m, n + 1)
                    tt(T[:, n, :], T[:, n, :], Z[:, 8 + n, :], ALU.mult)
                dve.drain()
                for n in pair:
                    dve.wait_ge(lru_ea, KT + 2 * n + 2)
                    v.tensor_tensor_scan(Z[:, 16 + n, :], Y[:, n, :], T[:, n, :], 0.0, ALU.mult, ALU.add)
                dve.drain()
                for n in pair:
                    tt(Z[:, 16 + n, :], Z[:, 16 + n, :], Z[:, n, :], ALU.mult).then_inc(lru_y, 1)
                if n0:
                    remainders(ZL2[:, 16:24, :], Z[:, 16:24, :], SRC["lru_out"], n0 - 2, n0)
            remainders(ZL2[:, 16:24, :], Z[:, 16:24, :], SRC["lru_out"], KT - 2)
            squares(4)
            residual(2, gain(0, 1))
            tail(0)

            def mixed(m, mu, n):
                stt(MIX[m % 2][n], Y[:, n, :], par2("mu", mu * KT + n, 1), N[:, n, :], ALU.mult, ALU.add).then_inc(mix, 1)

            v.memset(STATE, 0.0)
            inverse_root(7)
            for n0 in range(0, KT, 2):
                for n in (n0, n0 + 1):
                    stt(N[:, n, :], X[:, n, :], gain(1, 0)[:, n:n + 1], RS[:], ALU.mult, ALU.mult).then_inc(rms_y, 1)
                dve.drain()
                for n in (n0, n0 + 1):
                    tt(Y[:, n, 1:S], N[:, n, 0:S - 1], N[:, n, 1:S], ALU.subtract)
                    ts(Y[:, n, 0:1], N[:, n, 0:1], -1.0, None, ALU.mult)
                dve.drain()
                for n in (n0, n0 + 1):
                    mixed(0, 2, n)
            def heads_channels():
                own = cst("ident")[0:NHR, 0:NHR].unsqueeze(2).to_broadcast([NHR, NHR, HD])
                v.tensor_copy(CAST.rearrange("p (h c) -> p h c", h=NHR), own)

            for m, mu in enumerate((1, 4, 5, 3, 0), 1):
                if m == 3:
                    dve.wait_ge(lora, 1)
                elif m >= 2:
                    dve.wait_ge(used, {2: B_LORA, 4: B_LORA + 1, 5: B_LORA + 2}[m])
                for n in range(KT):
                    mixed(m, mu, n)
            dve.wait_ge(cst2_in, 16)
            for n in range(KT):
                dve.wait_ge(lw, n + 1)
                t = TMP[n % 2]
                v.tensor_tensor_scan(t, cst2("reset"), N[:, n, :], 0.0, ALU.mult, ALU.add)
                dve.drain()
                t4 = t.rearrange("p (c t) -> p c t", c=RC)
                v.tensor_copy(MID[:, 0:2, n, :], t4[:, :, P // 2 - 1].unsqueeze(1).to_broadcast([P, 2, RC]))
                tt(MID[:, 2, n, :], t4[:, :, P - 1], t4[:, :, P // 2 - 1], ALU.subtract)
                tt(N[:, n, :].rearrange("p (c t) -> p c t", c=RC), t4, t4[:, :, P // 2 - 1:P // 2].to_broadcast([P, RC, P]),
                   ALU.subtract).then_inc(cum, 1)
            dve.drain()
            for n in range(KT):
                dve.wait_ge(kk["sq"], n + 1)
                dve.wait_ge(la, 3 + n + 1)
                ts(TMP[n % 2], Y[:, n, :], 1.0, par2("k_a", n, 1), ALU.subtract, ALU.mult)
                dve.drain()
                stt(Z[:, 8 + n, :], TMP[n % 2], 1.0, Z[:, 8 + n, :], ALU.add, ALU.mult)
            heads_channels()
            dve.wait_ge(kk["root"], 1)
            ts(ROWS, ROWS, 1e-12, None, ALU.max)
            dve.drain()
            v.reciprocal(ROWS, ROWS).then_inc(kk["root"], 1)
            for n in range(KT):
                dve.wait_ge(kk["cast"], n + 1)
                tt(T[:, n, :], T[:, n, :], ps[:, 4 + n % 4, :], ALU.mult)
                dve.drain()
                tt(Y[:, n, :], Y[:, n, :], T[:, n, :], ALU.mult).then_inc(kk["done"], 1)
            dve.wait_ge(mid_e, 1)
            dve.drain()
            pair = cst2("pair").rearrange("p (a t) -> p a t", a=2).unsqueeze(1).to_broadcast([P, 2, 2, P])
            ident4 = cst("ident").unsqueeze(1).to_broadcast([P, 4, P])

            def level(i):
                return cst2("levels", i * P, P).unsqueeze(1).to_broadcast([P, 4, P])

            with dve.Fori(0, RC) as c:
                for half in range(2):
                    def lane(L):
                        return ch[L], LANES[L], 4 * L, 2 * (2 * half + L), c * 2 + half

                    for L in range(2):
                        s, B, o, n0, it = lane(L)
                        dve.wait_ge(s["exp"], it + 1)
                        e, tsl = B["e"], bass.ds(c * P, P)
                        stt(B["ar"][:, :, 0, :], T[:, n0:n0 + 2, tsl], -1.0, e[:, :, 0, 0:P], ALU.mult, ALU.mult)
                        tt(B["ar"][:, :, 1, :], Z[:, n0:n0 + 2, tsl], e[:, :, 0, 1:P + 1], ALU.mult)
                        tt(B["bk"][:, 0], Y[:, n0:n0 + 2, tsl], e[:, :, 1, 0:P], ALU.mult)
                        tt(B["sh"], STATE[:, n0:n0 + 2, :], MID[:, 1, n0:n0 + 2, bass.ds(c, 1)].to_broadcast([P, 2, HD]), ALU.mult)
                        tt(B["bk"][:, 1], Z[:, 8 + n0:10 + n0, tsl], e[:, :, 1, 0:P], ALU.mult).then_inc(s["hat"], 1)
                    for L in range(2):
                        s, B, o, n0, it = lane(L)
                        dve.wait_ge(s["g1"], it + 1)
                        for r in range(2):
                            tt(B["g1"][:, r:4:2], ps[:, o + 2 + r, :].rearrange("p (n a t) -> p n a t", n=2, a=2), pair, ALU.mult)
                        dve.drain()
                        tt(B["g1"][:, :, 0, :], B["g1"][:, :, 0, :], ident4, ALU.add)
                        dve.drain()
                        tt(B["xt"], B["g1"][:, :, 0, :], level(0), ALU.mult).then_inc(s["x0t"], 1)
                    for L in range(2):
                        s, B, o, n0, it = lane(L)
                        dve.wait_ge(s["g2"], it + 1)
                        for r in range(2):
                            ins = tt(B["g2"][:, r:4:2], ps[:, o + r, :].rearrange("p (n a t) -> p n a t", n=2, a=2), pair, ALU.mult)
                        ins.then_inc(s["g2m"], 1)
                    for k in range(LEVELS):
                        for L in range(2):
                            s, B, o, n0, it = lane(L)
                            dve.wait_ge(s["z"], it * LEVELS + k + 1)
                            tt(B["z"], ps[:, o, :].rearrange("p (q t) -> p q t", q=4), level(k + 1), ALU.mult).then_inc(s["zm"], 1)
                    for L in range(2):
                        s, B, o, n0, it = lane(L)
                        dve.wait_ge(s["s"], it + 2)
                        for r in (0, HD):
                            tt(STATE[r:r + HD, n0:n0 + 2, :], ps[r:r + HD, o, 0:2 * P].rearrange("p (n i) -> p n i", n=2)[:, :, r:r + HD],
                               B["sh"][r:r + HD], ALU.add)
                        dve.drain()
                        st = STATE[:, n0:n0 + 2, :]
                        tt(st, st, MID[:, 2, n0:n0 + 2, bass.ds(c, 1)].to_broadcast([P, 2, HD]), ALU.mult).then_inc(s["sc"], 1)
                    dve.drain()
            def bonus_in(n):
                if n >= 2:
                    dve.wait_ge(gn["bonus"], n - 1)
                stt(Z[:, 24 + n % 2, :], Z[:, n, :], par2("r_k", n, 1), Z[:, 8 + n, :], ALU.mult, ALU.mult).then_inc(gn["rk"], 1)

            bonus_in(0)
            for n in range(KT):
                if n + 1 < KT:
                    bonus_in(n + 1)
                dve.wait_ge(gn["bonus"], n + 1)
                tt(Z[:, 16 + n, :], Z[:, 16 + n, :], ps[:, 2 + n % 2, :], ALU.mult).then_inc(gn["bout"], 1)
            heads_channels()
            dve.wait_ge(gn["root"], 1)
            v.reciprocal(ROWS, ROWS).then_inc(gn["root"], 1)
            for n in range(KT):
                dve.wait_ge(gn["yc"], n + 1)
                dve.wait_ge(gn["cast"], n + 1)
                stt(T[:, n, :], T[:, n, :], par2("gn_g", n, 1), ps[:, 5 + n % 2, :], ALU.mult, ALU.mult)
                dve.drain()
                stt(T[:, n, :], T[:, n, :], par2("gn_b", n, 1), Z[:, 16 + n, :], ALU.add, ALU.add)
                dve.drain()
                tt(Y[:, n, :], T[:, n, :], ps[:, [7, 0][n % 2], :], ALU.mult).then_inc(gn["out"], 1)
            remainders(YL, Y, SRC["rwo"])
            squares(4 + 32)
            residual(8, gain(1, 1))
            tail(1)

        @block.gpsimd
        def _(pool):
            def remainder(split, j):
                pool.wait_ge(w_hi, split + 1)
                nc.gpsimd.tensor_tensor(RL[:, j, :], ring[:, j, :], RH[:, j, :].bitcast(F32), ALU.subtract).then_inc(w_lo, 1)

            def remainders(split, quads):
                with pool.Fori(0, quads) as i:
                    for j in range(RING):
                        remainder(split + i * RING + j, j)

            with pool.Fori(0, DEPTH) as l:
                W0 = l * SPL
                remainders(W0, B_DV // RING)
                for c in (B_DV, B_DV + 1, B_DV2, B_DV2 + 1):
                    remainder(W0 + n_split(c), c % RING)
                remainders(W0 + n_split(B_MERGE), (CPL - B_MERGE) // RING)
            for first, n in SPLIT_RUNS:
                remainders(n_split(first), n // RING)


def _tiles(w):
    k, n = w.shape
    return w.reshape(k // P, P, n // P, P).transpose(2, 1, 0, 3)


def _blocks(w, nk):
    t = _tiles(w)
    t = np.concatenate([t, np.zeros((t.shape[0], P, nk - t.shape[2], P), w.dtype)], axis=2) if nk > t.shape[2] else t
    return t.reshape(t.shape[0], P, nk * P)


def _rows(w):
    k, n = w.shape
    full = np.zeros((k, 512), w.dtype)
    full[:, :n] = w
    return full.reshape(k // 256, 2, P, 512).transpose(0, 2, 1, 3).reshape(k // 256, P, CHUNK)


def _chunks(t):
    return t.reshape(-1, P, CHUNK) if t.shape[2] == CHUNK else \
        t.reshape(t.shape[0], P, t.shape[2] // CHUNK, CHUNK).transpose(0, 2, 1, 3).reshape(-1, P, CHUNK)


def _cols(v):
    return v.reshape(-1, P).T


def first_weights(i, l):
    w = i["w_in"][l]
    col = lambda s, n: w[:, s:s + n]
    q = col(3072, 512).reshape(D, NG, HPG, HD).transpose(0, 2, 1, 3).reshape(D, 512)
    kv = col(3584, 768).reshape(D, 6, P)
    g = col(4352, 24).reshape(D, NH, 3).transpose(0, 2, 1).reshape(D, 24)
    zw = np.concatenate([col(0, 1536), col(1536, 1024), q, kv[:, 0], kv[:, 1], kv[:, 2], kv[:, 4]], axis=1)
    dv, phi = _rows(col(2560, 512)), i["nsa_phi_w1"][l].reshape(2, 2, 8, P, P).transpose(0, 1, 3, 2, 4).reshape(4, P, CHUNK)
    out = [_chunks(_blocks(zw, KT)), _rows(np.concatenate([kv[:, 3], kv[:, 5], g], axis=1)), dv[:2], phi, dv[2:]]
    br = [_tiles(i["w_branch"][l][b]).reshape(4, 2, P, 4 * P).transpose(0, 2, 1, 3).reshape(4, P, CHUNK) for b in range(3)]
    out += [_blocks(col(4376, 3 * D), KT), *br]
    out.append(_blocks(i["w_o"][l], KT))
    up = _blocks(i["ffn_w_up"][l], KT)
    out.append(up.reshape(2, FT, P, CHUNK).transpose(1, 0, 2, 3).reshape(2 * FT, P, CHUNK))
    out.append(_chunks(_blocks(i["ffn_w_down"][l], 24)))
    return np.concatenate(out)


def first_params(i, l):
    lam_init = 0.8 - 0.6 * math.exp(-0.3 * l)
    f = np.float32
    part = {
        "conv_a": _cols(i["conv_a_w"][l]), "subln": _cols(i["diff_subln"][l]),
        "ln1_g": _cols(i["ln1_g"][l]), "ln1_b": _cols(i["ln1_b"][l]),
        "ln2_g": _cols(i["ln2_g"][l]), "ln2_b": _cols(i["ln2_b"][l]),
        "up_w": _cols(i["ffn_conv_w"][l]), "up_b": _cols(i["ffn_conv_b"][l]),
        "pos": np.tile(i["nsa_cmp_pos"][l].transpose(2, 0, 1).reshape(HD, 2 * CMP_BLOCK), (2, 1)),
        "phi_w2k": np.tile(i["nsa_phi_w2"][l][0], (1, 2)), "phi_w2v": i["nsa_phi_w2"][l][1],
        "lam": np.tile(i["diff_lambda"][l].reshape(1, 4 * HD), (P, 1)),
        "lam_init": np.full((P, 1), lam_init, f), "lam_keep": np.full((P, 1), 1.0 - lam_init, f),
    }
    return np.concatenate([part[n] for n in PCOL], axis=1)


def second_weights(i):
    lin = lambda w: _chunks(_blocks(w, KT))
    zeros = lambda n: np.zeros((n, P, CHUNK), np.float32)

    def rows(w):
        return [_rows(w[:, h * 512:h * 512 + 512]) for h in range(2)]

    def tail(l):
        kv = i["c_w_kv_2"][l]
        up = lin(i["m_w_up_2"][l])
        down = _blocks(i["m_w_down_2"][l], F2T).reshape(KT, P, 2, 2, CHUNK).transpose(2, 0, 3, 1, 4).reshape(2, C_HDN, P, CHUNK)
        return [lin(i["c_w_q_2"][l]), lin(kv[:, :D]), *rows(kv[:, D:]), lin(i["c_w_o_2"][l]),
                up[:HALF], down[0], up[HALF:], down[1]]

    gate = i["a_gate_w_2"][0].reshape(2, 2, 2, 2, P, 2, P).transpose(0, 1, 4, 2, 5, 3, 6).reshape(4, P, CHUNK)
    out = [lin(i["a_w_in_2"][0]), gate, lin(i["a_w_out_2"][0]), *tail(0)]
    out.append(lin(i["b_w_rkv_2"][0][1]))
    thin = lambda w: w.reshape(KT, P, HD).transpose(1, 0, 2).reshape(P, KT * HD)
    tall = lambda w: np.concatenate([w, np.zeros((P - HD, D), w.dtype)])
    out.append(np.concatenate([thin(i["b_w1_2"][0]), thin(i["b_a1_2"][0])], axis=1)[None])
    out += [lin(i["b_g1_2"][0]), tall(i["b_w2_2"][0])[None], tall(i["b_a2_2"][0])[None], lin(i["b_w_rkv_2"][0][2]), lin(i["b_w_rkv_2"][0][0]), zeros(3), i["b_g2_2"][0][None]]
    return np.concatenate(out + [lin(i["b_w_o_2"][0]), *tail(1)])


def second_params(i):
    f = np.float32
    part = {
        "ln": _cols(i["ln_gains_2"]), "mem_norm": _cols(i["mem_norm_2"]), "conv_w": _cols(i["a_conv_w_2"]),
        "conv_b": _cols(i["a_conv_b_2"]), "b_in": _cols(i["a_b_in_2"]), "gate_b": _cols(i["a_gate_b_2"]),
        "lam": _cols(i["a_lambda_2"]), "b_out": _cols(i["a_b_out_2"]), "mu": _cols(i["b_mu_2"]),
        "w0": _cols(i["b_w0_2"]), "a0": _cols(i["b_a0_2"]), "k_k": _cols(i["b_k_k_2"]), "k_a": _cols(i["b_k_a_2"]),
        "r_k": _cols(i["b_r_k_2"]), "gn_g": _cols(i["b_gn_g_2"]), "gn_b": _cols(i["b_gn_b_2"]),
        "rms_eps": np.full((P, 1), RMS_EPS, f), "gn_eps": np.full((P, 1), GN_EPS, f),
    }
    return np.concatenate([part[n] for n in P2COL], axis=1)


def second_constants():
    f = np.float32
    k = np.arange(P)
    r, c = k[:, None], k[None, :]
    pair = np.concatenate([(r < c), (r <= c)], axis=1)
    eye = r == c
    levels = [(r // 2 == c // 2) & (r < c) | eye]
    for v in range(1, LEVELS + 1):
        b = 1 << v
        levels.append((r // (2 * b) == c // (2 * b)) & (r // b > c // b) | eye)
    part = {
        "pair": pair, "levels": np.concatenate(levels, axis=1), "reset": np.tile((np.arange(S) % P != 0)[None], (P, 1)),
        "ones": r // HD == c // HD, "center": eye - (r // HD == c // HD) / HD,
        "sel": np.arange(2 * NHR - 2)[None] - (NHR - 2) == r // HD,
    }
    return np.concatenate([part[n].astype(f) for n in C2COL], axis=1)


def constants():
    f = np.float32
    pos = np.arange(S, dtype=f)
    inv = (np.float32(500000.0) ** (-np.arange(0, 16, 2, dtype=f) / f(16))).astype(f)
    ang = (pos[:, None] * inv[None, :]).astype(f)
    cos, sin = np.ones((P, S), f), np.zeros((P, S), f)
    rot = np.zeros((P, P), f)
    for h in range(2):
        for d in range(8):
            a0, a1 = h * HD + d, h * HD + 8 + d
            cos[a0], cos[a1] = np.cos(ang[:, d]), np.cos(ang[:, d])
            sin[a0], sin[a1] = np.sin(ang[:, d]), np.sin(ang[:, d])
            rot[a1, a0], rot[a0, a1] = -1.0, 1.0
    t = np.arange(S).reshape(ST, P).T[:, :, None]
    valid = (np.arange(NCMP) * CMP_STRIDE + CMP_BLOCK - 1)[None, None, :] <= t
    k = np.arange(P)
    part = {
        "ident": np.eye(P, dtype=f), "rot": rot, "maskneg": np.where(k[None, :] > k[:, None], f(NEG), f(0)),
        "mean": np.full((P, P), 1.0 / D, f), "cmask": np.where(valid, f(0), f(NEG)).reshape(P, -1),
        "cvalid": valid.astype(f).reshape(P, -1), "cos": cos, "sin": sin, "eps": np.full((P, 1), LN_EPS, f),
    }
    return np.concatenate([part[n] for n in CCOL], axis=1).astype(f)


def kernel(**inputs):
    import concourse.bacc as bacc
    from concourse.bass_utils import run_bass_kernel_spmd

    i = {k: np.asarray(v) for k, v in inputs.items()}
    nc = bacc.Bacc("TRN2", target_bir_lowering=False, num_devices=1)
    arrays = {
        "x": i["x"][0].T.reshape(KT, P, S).transpose(1, 0, 2),
        "weights": np.concatenate([first_weights(i, l) for l in range(DEPTH)] + [second_weights(i)]),
        "par": np.stack([first_params(i, l) for l in range(DEPTH)]),
        "cst": constants(), "par2": second_params(i), "cst2": second_constants(),
        "mem": i["mem_2"][0].T.reshape(KT, P, S2).transpose(1, 0, 2),
    }
    arrays = {k: np.ascontiguousarray(v) for k, v in arrays.items()}
    aps = {k: nc.dram_tensor(f"in_{k}", v.shape, F32, kind="ExternalInput").ap() for k, v in arrays.items()}
    out = nc.dram_tensor("out_x", (P, KT, S), F32, kind="ExternalOutput").ap()
    build(nc, aps, out)
    r = run_bass_kernel_spmd(nc, [{f"in_{k}": v for k, v in arrays.items()}], core_ids=[0])
    return np.ascontiguousarray(r.results[0]["out_x"].transpose(1, 0, 2).reshape(D, S).T)[None]
```
